# Optimizing a Trainium2 kernel written in Bass

```python
import math
import jax, jax.numpy as jnp
from jax import lax
import numpy as np

D_MODEL = 1024
BATCH = 1
SEQ = 512
DEPTH = 4

N_MIXERS = 3
N_A = (DEPTH + 2) // 3
N_B = (DEPTH + 1) // 3
N_C = DEPTH // 3

NORM_EPS = 1e-5

RWKV_HEAD = 64
RWKV_HEADS = D_MODEL // RWKV_HEAD
LORA_W = 64
LORA_A = 64
LORA_V = 32
LORA_G = 128
GN_EPS = 64e-5

CONV_WIDTH = 31
CONV_CH = D_MODEL

MLA_HEADS = 16
QK_NOPE = 64
QK_ROPE = 32
V_DIM = 64
Q_LORA = 384
KV_LORA = 256
ROPE_THETA = 10000.0
Q_BLOCK = 128

D_FF = 4 * D_MODEL

kernel_name = "hybrid_rwkv7_conformer_mla_trunk"

def rmsnorm(x, g):
    xf = x.astype(jnp.float32)
    y = xf * lax.rsqrt(jnp.mean(xf * xf, axis=-1, keepdims=True) + NORM_EPS) * g.astype(jnp.float32)
    return y.astype(x.dtype)

def layernorm(x, g, b):
    xf = x.astype(jnp.float32)
    mu = jnp.mean(xf, axis=-1, keepdims=True)
    var = jnp.mean(jnp.square(xf - mu), axis=-1, keepdims=True)
    y = (xf - mu) * lax.rsqrt(var + NORM_EPS) * g.astype(jnp.float32) + b.astype(jnp.float32)
    return y.astype(x.dtype)

def wkv7_scan(r, decay, k, v, a, b):
    B, S, H, N = r.shape

    def step(state, inp):
        r_t, w_t, k_t, v_t, a_t, b_t = inp
        sa = jnp.einsum('bhvk,bhk->bhv', state, a_t)
        state = (state * w_t[:, :, None, :]
                 + sa[..., None] * b_t[:, :, None, :]
                 + v_t[..., None] * k_t[:, :, None, :])
        return state, jnp.einsum('bhvk,bhk->bhv', state, r_t)

    xs = tuple(jnp.moveaxis(t, 1, 0) for t in (r, decay, k, v, a, b))
    s0 = jnp.zeros((B, H, N, N), jnp.float32)
    _, ys = lax.scan(step, s0, xs)
    return jnp.moveaxis(ys, 0, 1)

def rwkv7_time_mix(u, mu, wr, wk, wv, wo, w0, w1, w2, a0, a1, a2, g1, g2,
                   k_k, k_a, r_k, lnx_w, lnx_b, vres):
    B, S, D = u.shape
    H, N = RWKV_HEADS, RWKV_HEAD
    xx = jnp.pad(u, ((0, 0), (1, 0), (0, 0)))[:, :-1] - u
    xr, xw, xk, xv, xa, xg = [u + xx * mu[j] for j in range(6)]
    r = xr @ wr
    k = xk @ wk
    v = xv @ wv
    w = -jax.nn.softplus(-(w0 + jnp.tanh(xw @ w1) @ w2)) - 0.5
    if vres is not None:
        v0, v1, v2, v_first = vres
        v = v + (v_first - v) * jax.nn.sigmoid(v0 + (xv @ v1) @ v2)
    a = jax.nn.sigmoid(a0 + (xa @ a1) @ a2)
    g = jax.nn.sigmoid(xg @ g1) @ g2

    hs = lambda t: t.astype(jnp.float32).reshape(B, S, H, N)
    kk = hs(k * k_k)
    kk = kk * lax.rsqrt(jnp.maximum(jnp.sum(kk * kk, axis=-1, keepdims=True), 1e-24))
    k_eff = k * (1 + (a - 1) * k_a)
    decay = jnp.exp(-jnp.exp(hs(w)))
    rf, kf, vf, af = hs(r), hs(k_eff), hs(v), hs(a)
    y = wkv7_scan(rf, decay, kf, vf, -kk, kk * af)

    mean = jnp.mean(y, axis=-1, keepdims=True)
    var = jnp.mean(jnp.square(y - mean), axis=-1, keepdims=True)
    y = ((y - mean) * lax.rsqrt(var + GN_EPS)).reshape(B, S, D)
    y = y * lnx_w.astype(jnp.float32) + lnx_b.astype(jnp.float32)
    bonus = jnp.sum(rf * kf * r_k.astype(jnp.float32), axis=-1, keepdims=True) * vf
    y = (y + bonus.reshape(B, S, D)) * g.astype(jnp.float32)
    return y.astype(u.dtype) @ wo, v

def conformer_conv(u, w1, b1, dw, bdw, ln_w, ln_b, w2, b2):
    z = u @ w1 + b1
    za, zb = jnp.split(z, 2, axis=-1)
    z = za * jax.nn.sigmoid(zb)
    z = lax.conv_general_dilated(
        z, dw[:, None, :].astype(z.dtype), window_strides=(1,),
        padding=[(CONV_WIDTH - 1, 0)],
        dimension_numbers=('NWC', 'WIO', 'NWC'),
        feature_group_count=CONV_CH) + bdw
    z = jax.nn.silu(layernorm(z, ln_w, ln_b))
    return z @ w2 + b2

def rope_tables(positions):
    inv_freq = ROPE_THETA ** (-jnp.arange(0, QK_ROPE, 2, dtype=jnp.float32) / QK_ROPE)
    ang = positions.astype(jnp.float32)[..., None] * inv_freq
    return jnp.cos(ang), jnp.sin(ang)

def apply_rope(x, cos, sin):
    x1, x2 = jnp.split(x.astype(jnp.float32), 2, axis=-1)
    return jnp.concatenate([x1 * cos - x2 * sin, x1 * sin + x2 * cos], axis=-1).astype(x.dtype)

def mla_attention(u, positions, wd, gq, wuq, gkv, wukv, wo):
    B, S, _ = u.shape
    H = MLA_HEADS
    c = u @ wd
    cq, ckv, kr = jnp.split(c, [Q_LORA, Q_LORA + KV_LORA], axis=-1)
    q = (rmsnorm(cq, gq) @ wuq).reshape(B, S, H, QK_NOPE + QK_ROPE)
    q_nope, q_rope = q[..., :QK_NOPE], q[..., QK_NOPE:]
    kv = (rmsnorm(ckv, gkv) @ wukv).reshape(B, S, H, QK_NOPE + V_DIM)
    k_nope, v = kv[..., :QK_NOPE], kv[..., QK_NOPE:]
    cos, sin = rope_tables(positions)
    q_rope = apply_rope(q_rope, cos[:, :, None, :], sin[:, :, None, :])
    k_rope = apply_rope(kr, cos, sin)
    scale = 1.0 / math.sqrt(QK_NOPE + QK_ROPE)
    key_idx = jnp.arange(S)

    def block(i):
        qs = i * Q_BLOCK
        qn = lax.dynamic_slice_in_dim(q_nope, qs, Q_BLOCK, axis=1)
        qr = lax.dynamic_slice_in_dim(q_rope, qs, Q_BLOCK, axis=1)
        s = (jnp.einsum('bqhd,bkhd->bhqk', qn, k_nope)
             + jnp.einsum('bqhd,bkd->bhqk', qr, k_rope)).astype(jnp.float32) * scale
        q_idx = qs + jnp.arange(Q_BLOCK)
        s = jnp.where(key_idx[None, :] <= q_idx[:, None], s, -1e30)
        p = jax.nn.softmax(s, axis=-1).astype(v.dtype)
        return jnp.einsum('bhqk,bkhd->bqhd', p, v)

    o = lax.map(block, jnp.arange(S // Q_BLOCK))
    o = jnp.moveaxis(o, 0, 1).reshape(B, S, H * V_DIM)
    return o @ wo

def squared_relu_mlp(u, w1, w2):
    return jnp.square(jax.nn.relu(u @ w1)) @ w2

def setup_inputs(seed: int = 0) -> dict:
    key = jax.random.key(seed)
    ks = iter(jax.random.split(key, 64))
    D = D_MODEL

    def nrm(shape, scale):
        return jax.random.normal(next(ks), shape, jnp.float32) * scale

    def gain(shape):
        return 1.0 + nrm(shape, 0.05)

    x = jax.random.normal(next(ks), (BATCH, SEQ, D), jnp.float32)
    start = jax.random.randint(next(ks), (BATCH, 1), 0, 4096, dtype=jnp.int32)
    positions = start + jnp.arange(SEQ, dtype=jnp.int32)[None, :]
    HD = RWKV_HEADS * RWKV_HEAD
    return {
        "x": x,
        "positions": positions,
        "norm_mix": gain((DEPTH, D)),
        "norm_ffn": gain((DEPTH, D)),
        "norm_final": gain((D,)),
        "rw_mu": jax.random.uniform(next(ks), (N_A, 6, D), jnp.float32),
        "rw_wr": nrm((N_A, D, HD), D ** -0.5),
        "rw_wk": nrm((N_A, D, HD), D ** -0.5),
        "rw_wv": nrm((N_A, D, HD), D ** -0.5),
        "rw_wo": nrm((N_A, HD, D), HD ** -0.5),
        "rw_w0": jax.random.uniform(next(ks), (N_A, D), jnp.float32, -6.0, 1.0),
        "rw_w1": nrm((N_A, D, LORA_W), D ** -0.5),
        "rw_w2": nrm((N_A, LORA_W, D), 0.5 * LORA_W ** -0.5),
        "rw_a0": nrm((N_A, D), 0.1),
        "rw_a1": nrm((N_A, D, LORA_A), D ** -0.5),
        "rw_a2": nrm((N_A, LORA_A, D), 0.5 * LORA_A ** -0.5),
        "rw_g1": nrm((N_A, D, LORA_G), D ** -0.5),
        "rw_g2": nrm((N_A, LORA_G, D), LORA_G ** -0.5),
        "rw_kk": 0.85 + nrm((N_A, D), 0.05),
        "rw_ka": 1.0 + nrm((N_A, D), 0.05),
        "rw_rk": nrm((N_A, RWKV_HEADS, RWKV_HEAD), 0.1),
        "rw_lnx_w": gain((N_A, D)),
        "rw_lnx_b": nrm((N_A, D), 0.01),
        "rw_v0": nrm((N_A - 1, D), 0.1),
        "rw_v1": nrm((N_A - 1, D, LORA_V), D ** -0.5),
        "rw_v2": nrm((N_A - 1, LORA_V, D), 0.5 * LORA_V ** -0.5),
        "cv_w1": nrm((N_B, D, 2 * CONV_CH), D ** -0.5),
        "cv_b1": nrm((N_B, 2 * CONV_CH), 0.02),
        "cv_dw": nrm((N_B, CONV_WIDTH, CONV_CH), CONV_WIDTH ** -0.5),
        "cv_bdw": nrm((N_B, CONV_CH), 0.02),
        "cv_ln_w": gain((N_B, CONV_CH)),
        "cv_ln_b": nrm((N_B, CONV_CH), 0.02),
        "cv_w2": nrm((N_B, CONV_CH, D), CONV_CH ** -0.5),
        "cv_b2": nrm((N_B, D), 0.02),
        "ml_wd": nrm((N_C, D, Q_LORA + KV_LORA + QK_ROPE), D ** -0.5),
        "ml_gq": gain((N_C, Q_LORA)),
        "ml_wuq": nrm((N_C, Q_LORA, MLA_HEADS * (QK_NOPE + QK_ROPE)), Q_LORA ** -0.5),
        "ml_gkv": gain((N_C, KV_LORA)),
        "ml_wukv": nrm((N_C, KV_LORA, MLA_HEADS * (QK_NOPE + V_DIM)), KV_LORA ** -0.5),
        "ml_wo": nrm((N_C, MLA_HEADS * V_DIM, D), (MLA_HEADS * V_DIM) ** -0.5),
        "ff_w1": nrm((DEPTH, D, D_FF), D ** -0.5),
        "ff_w2": nrm((DEPTH, D_FF, D), D_FF ** -0.5),
    }

def reference(x, positions, norm_mix, norm_ffn, norm_final,
              rw_mu, rw_wr, rw_wk, rw_wv, rw_wo, rw_w0, rw_w1, rw_w2,
              rw_a0, rw_a1, rw_a2, rw_g1, rw_g2, rw_kk, rw_ka, rw_rk,
              rw_lnx_w, rw_lnx_b, rw_v0, rw_v1, rw_v2,
              cv_w1, cv_b1, cv_dw, cv_bdw, cv_ln_w, cv_ln_b, cv_w2, cv_b2,
              ml_wd, ml_gq, ml_wuq, ml_gkv, ml_wukv, ml_wo,
              ff_w1, ff_w2):
    h = x
    v_first = None
    ia = ib = ic = 0
    for i in range(DEPTH):
        u = rmsnorm(h, norm_mix[i])
        kind = i % N_MIXERS
        if kind == 0:
            vres = None if ia == 0 else (rw_v0[ia - 1], rw_v1[ia - 1], rw_v2[ia - 1], v_first)
            y, v = rwkv7_time_mix(u, rw_mu[ia], rw_wr[ia], rw_wk[ia], rw_wv[ia], rw_wo[ia],
                                  rw_w0[ia], rw_w1[ia], rw_w2[ia], rw_a0[ia], rw_a1[ia], rw_a2[ia],
                                  rw_g1[ia], rw_g2[ia], rw_kk[ia], rw_ka[ia], rw_rk[ia],
                                  rw_lnx_w[ia], rw_lnx_b[ia], vres)
            if ia == 0:
                v_first = v
            ia += 1
        elif kind == 1:
            y = conformer_conv(u, cv_w1[ib], cv_b1[ib], cv_dw[ib], cv_bdw[ib],
                               cv_ln_w[ib], cv_ln_b[ib], cv_w2[ib], cv_b2[ib])
            ib += 1
        else:
            y = mla_attention(u, positions, ml_wd[ic], ml_gq[ic], ml_wuq[ic],
                              ml_gkv[ic], ml_wukv[ic], ml_wo[ic])
            ic += 1
        h = h + y
        h = h + squared_relu_mlp(rmsnorm(h, norm_ffn[i]), ff_w1[i], ff_w2[i])
    return rmsnorm(h, norm_final)


_drawn_inputs = setup_inputs


def setup_inputs(seed=0):
    import zlib

    import numpy as np

    out = dict(_drawn_inputs(seed))
    spreads = {}
    factors = {'rw_w1': 2.946,
     'rw_w2': 3.076,
     'rw_lnx_b': 8.0,
     'rw_v0': 38.189,
     'cv_b1': 6.311,
     'cv_bdw': 3.416,
     'cv_ln_b': 7.072,
     'cv_b2': 4.106,
     'ml_gq': 8.0,
     'ml_gkv': 5.565,
     'rw_v1': 3.654,
     'rw_v2': 3.308}
    for name, (base, spread) in spreads.items():
        noise = np.random.default_rng([zlib.crc32(name.encode()), seed]).standard_normal(out[name].shape)
        drawn = base * np.exp(spread * noise) if base else spread * noise
        out[name] = __import__('jax').numpy.asarray(drawn.astype(out[name].dtype))
    for name, factor in factors.items():
        out[name] = (out[name] * factor).astype(out[name].dtype)
    return out
```

```python
from contextlib import ExitStack

import numpy as np

import concourse.bass as bass
from concourse import mybir

F32 = mybir.dt.float32
I32 = mybir.dt.int32
ALU = mybir.AluOpType
ACT = mybir.ActivationFunctionType
AX_X = mybir.AxisListType.X

P = 128
SEQ, DM, DEPTH = 512, 1024, 4
NT = DM // P
HEAD = 64
CH = 64
NCH = SEQ // CH
LORA_W, LORA_A, LORA_V, LORA_G = 64, 64, 32, 128
TAPS = 31
PAD = TAPS - 1
D_FF = 4 * DM
FT = D_FF // P
HEADS, NOPE, ROPE, VDIM = 16, 64, 32, 64
QK = NOPE + ROPE
Q_LORA, KV_LORA = 384, 256
NORM_EPS, GN_EPS = 1e-5, 64e-5
DECAY = float(np.exp(-0.5))
TWO_PI = 2.0 * np.pi
PI_BELOW = float(np.nextafter(np.float32(np.pi), np.float32(0)))
PE_TAPS, ACT_TAPS = 13, 6

SLOTS = 4
SLOT = 2048

VECTORS = [
    [("rw_mu", 96), ("norm_mix", 32)],
    [("norm_ffn", 32), ("norm_final", 8), ("rw_w0", 16), ("rw_a0", 16), ("rw_kk", 16), ("rw_ka", 16),
     ("rw_rk", 16), ("rw_v0", 8)],
    [("rw_lnx_w", 16), ("rw_lnx_b", 16), ("cv_b1", 16), ("cv_bdw", 8), ("cv_ln_w", 8), ("cv_ln_b", 8),
     ("cv_b2", 8), ("ml_gq", 3), ("ml_gkv", 2)],
]
VEC_ROW = {}
for _g, _names in enumerate(VECTORS):
    _r = 0
    for _n, _k in _names:
        VEC_ROW[_n] = (_g, _r, _k)
        _r += _k

CONSTS = {}
_at = 0
for _n, _w in [("ident", P), ("ones", P), ("pair", P), ("mask_g", P), ("mask_d", CH), ("mask_dt", CH),
               ("mask_et", CH), ("eye2", CH), ("cols", 8)]:
    CONSTS[_n] = (_at, _w)
    _at += _w
CONST_W = _at


def constants():
    c = np.zeros((P, CONST_W), np.float32)

    def put(name, a):
        at, w = CONSTS[name]
        c[: a.shape[0], at:at + w] = a

    p, f = np.arange(P)[:, None], np.arange(P)[None, :]
    put("ident", np.eye(P))
    put("ones", np.ones((P, P)))
    put("pair", (p // HEAD == f // HEAD) * 1.0)
    j, i = p % CH, f % CH
    put("mask_g", np.where(f < CH, (p >= CH) & (j < i), j <= i) * 1.0)
    i2, j2 = np.arange(P)[:, None] % CH, np.arange(CH)[None, :]
    put("mask_d", ((j2 < i2) & (j2 // 16 == i2 // 16)) * 1.0)
    put("mask_dt", ((i2 < j2) & (j2 // 16 == i2 // 16)) * 1.0)
    put("mask_et", (i2 // 16 < j2 // 16) * 1.0)
    put("eye2", (i2 == j2) * 1.0)
    t = np.zeros((P, ROPE))
    for k in range(ROPE // 2):
        t[NOPE + ROPE // 2 + k, k] = -1.0
        t[NOPE + k, ROPE // 2 + k] = 1.0
    cols = np.zeros((P, 8))
    cols[:, 0] = NORM_EPS
    cols[:, 1] = GN_EPS
    freq = np.float32(10000.0) ** (-np.arange(0, ROPE, 2, dtype=np.float32) / np.float32(ROPE))
    cols[NOPE:NOPE + ROPE, 2] = np.tile(freq, 2)
    cols[:, 3] = np.pi / 2
    put("cols", cols)
    reset = np.ones((P, SEQ), np.float32)
    reset[:, ::CH] = 0.0
    return c, np.concatenate([np.where(f <= p, 0.0, -1e30), t, reset], axis=1).astype(np.float32)


class Steps:

    def __init__(self, sem, known):
        self.sem, self.known, self.new = sem, known, {}
        self.count, self.loop_base, self.reg, self.per, self.stage = 0, None, None, 0, ""

    def mark(self, name):
        self.count += 1
        key = (self.stage, name)
        assert key not in self.new, key
        self.new[key] = (self.count, self.loop_base)
        return self.sem, 1

    def start_loop(self, reg):
        self.loop_base, self.reg = self.count, reg

    def end_loop(self, n):
        per = self.count - self.loop_base
        self.new[("per", self.loop_base)] = (per, None)
        self.count += per * (n - 1)
        self.loop_base = self.reg = None

    def at(self, name, i=None, stage=None):
        value, base = self.known.get((stage or self.stage, name), (None, None))
        if value is None:
            assert not self.known, (stage or self.stage, name)
            return 1
        if base is None or i is None:
            return value
        return i * self.known[("per", base)][0] + value

    def __call__(self, name, i=None, stage=None):
        return self.sem, self.at(name, i, stage)


class Ring:

    def __init__(self, buf, landed):
        self.buf, self.landed = buf, landed
        self.loads = self.uses = 0

    def slot(self, s):
        return self.buf[:, s % SLOTS, :]

    def load(self, sp, view, src, last_use):
        if last_use:
            sp.wait_ge(*last_use)
        sp.dma_start(view, src).then_inc(self.landed[self.loads % SLOTS], 16)
        self.loads += 1


def build(nc, a, known):
    ctx = ExitStack()
    new = {}
    with ctx:
        def sb(name, shape, dt=F32):
            return ctx.enter_context(nc.sbuf_tensor(name, shape, dt))

        def sem(name):
            return ctx.enter_context(nc.semaphore(name))

        arena = sb("arena", [P, 10, NT * SEQ])
        ring_buf = sb("ring", [P, SLOTS, SLOT])
        lora = sb("lora", [P, 5120])
        small = sb("small", [P, 1536])
        vec = sb("vec", [P, 3 * P])
        cst = sb("cst", [P, CONST_W])
        psum = ctx.enter_context(nc.psum_tensor("psum", [P, 8, 512], F32))

        def region(k):
            return arena[:, k, :].rearrange("p (t s) -> p t s", s=SEQ)

        def const(name, rows=P):
            at, w = CONSTS[name]
            return cst[0:rows, at:at + w]

        def col(name, j):
            g, r, _ = VEC_ROW[name]
            return vec[:, g * P + r + j:g * P + r + j + 1]

        eps = cst[:, CONSTS["cols"][0]:CONSTS["cols"][0] + 1]
        gn_eps = cst[:, CONSTS["cols"][0] + 1:CONSTS["cols"][0] + 2]
        rstd = small[:, 0:512]
        low = [small[:, 512:1024], small[:, 1024:1536]]

        pe_s = Steps(sem("pe_steps"), known.get("pe", {}))
        act_s = Steps(sem("act_steps"), known.get("act", {}))
        dve_s = Steps(sem("dve_steps"), known.get("dve", {}))
        pool_s = Steps(sem("pool_steps"), known.get("pool", {}))
        everyone = {"pe": pe_s, "act": act_s, "dve": dve_s, "pool": pool_s}

        landed = [sem(f"weights_landed{s}") for s in range(SLOTS)]
        ring = Ring(ring_buf, landed)
        in_landed = sem("inputs_landed")
        out_landed = sem("outputs_landed")
        ins = {"n": 0}

        h, u = region(0), region(1)

        def stage(name):
            for s in everyone.values():
                s.stage = name

        passed_pe, passed_pool = sem("passed_pe"), sem("passed_pool")

        class Banks:

            def __init__(self, jobs):
                self.names = [n for n, _ in jobs]
                self.who = dict(jobs)

            def bank(self, name):
                return psum[:, self.names.index(name) % 8, :]

            def free(self, name):
                k = self.names.index(name) - 8
                if k < 0:
                    return None
                before = self.names[k]
                return (act_s if self.who[before] == "act" else dve_s)("ev " + before)

        def bring(eng, dst, src):
            eng.dma_start(dst, src).then_inc(in_landed, 16)
            ins["n"] += 16

        def norm_act(act, tag, src, sq, scale=1.0 / DM, tiles=NT):
            for t in range(tiles):
                act.activation(sq[:, t, :], src[:, t, :], ACT.Square).then_inc(*act_s.mark(f"{tag} sq{t}"))
            act.wait_ge(*pe_s(f"{tag} sum"))
            act.activation(rstd, psum[:, 7, :], ACT.Sqrt, bias=eps, scale=scale).then_inc(*act_s.mark(f"{tag} root"))

        def norm_pe(pe, tag, sq, tiles=NT):
            for t in range(tiles):
                pe.wait_ge(*act_s(f"{tag} sq{t}"))
                mm = pe.matmul(psum[:, 7, :], const("ones"), sq[:, t, :], start=(t == 0), stop=(t == tiles - 1))
            mm.then_inc(*pe_s.mark(f"{tag} sum"))

        def norm_dve(dve, tag, src, dst, gain, tiles=NT):
            dve.wait_ge(*act_s(f"{tag} root"))
            dve.reciprocal(rstd, rstd).then_inc(*dve_s.mark(f"{tag} rstd"))
            dve.wait_ge(*dve_s(f"{tag} rstd"))
            for t in range(tiles):
                dve.scalar_tensor_tensor(dst[:, t, :], src[:, t, :], gain(t), rstd, ALU.mult,
                                         ALU.mult).then_inc(*dve_s.mark(f"{tag} out{t}"))

        def cols_slot(s):
            return ring.slot(s).rearrange("p (k n) -> p k n", n=256)

        def rows_slot(s):
            return ring.slot(s).rearrange("p (k n) -> p k n", n=DM)

        def load_proj(sp, w, last_use):
            wv = w.rearrange("(k p) n -> p k n", p=P)
            for s in range(SLOTS):
                ring.load(sp, cols_slot(s), wv[:, :, s * 256:(s + 1) * 256], last_use(s))

        def ffn_head(sp, layer, last_use):
            load_proj(sp, a["ff_w1"][layer][:, 0:SLOTS * 256], last_use)

        def ffn_body(sp, layer):
            w1 = a["ff_w1"][layer].rearrange("(k p) n -> p k n", p=P)
            w2 = a["ff_w2"][layer].rearrange("(c k p) n -> p c k n", p=P, k=2)
            turns = D_FF // 256 // SLOTS
            with sp.Fori(0, turns - 1) as i:
                for s in range(SLOTS):
                    ring.load(sp, cols_slot(s), w1[:, :, bass.ds((i * SLOTS + (SLOTS + s)) * 256, 256)],
                              pe_s(f"up{2 * s + 1}", i))
            for t in range(2):
                for s in range(SLOTS):
                    ring.load(sp, rows_slot(s), w2[:, t * SLOTS + s, :, :],
                              pe_s(f"down{s} first") if t else pe_s(f"up{2 * s + 1}", turns - 1))
            with sp.Fori(0, turns - 2) as i:
                for s in range(SLOTS):
                    ring.load(sp, rows_slot(s), w2[:, i * SLOTS + (2 * SLOTS + s), :, :], pe_s(f"down{s}", i))
            ring.loads += SLOTS * (2 * turns - 1) - 4 * SLOTS

        def ffn_last_use(layer):
            return lambda s: pe_s(f"down{s}", D_FF // 256 // SLOTS - 2, f"ffn{layer}")

        def slot_landed(pe, s, i=0):
            pe.wait_ge(landed[(ring.uses + s) % SLOTS], 16 * (i + (ring.uses + s) // SLOTS + 1))

        def proj_pe(pe, tag, banks, x, ready):
            for s in range(SLOTS):
                slot_landed(pe, s)
                for n in range(2):
                    job = f"{tag}{2 * s + n}"
                    if banks.free(job):
                        pe.wait_ge(*banks.free(job))
                    for k in range(NT):
                        if s == 0 and n == 0:
                            pe.wait_ge(*ready(k))
                        mm = pe.matmul(banks.bank(job), cols_slot(s)[:, k, n * P:(n + 1) * P], x[:, k, :],
                                       start=(k == 0), stop=(k == NT - 1))
                    mm.then_inc(*pe_s.mark(job))
            ring.uses += SLOTS


        def begin():
            stage("begin")
            x_in = arena[:, 2, :].rearrange("p (t d) -> p t d", d=DM)
            rows = arena[:, 3, 0:3 * P].rearrange("p (g c) -> p g c", c=P)
            with nc.Block() as block:
                @block.sync
                def _(sp):
                    bring(sp, cst[:], a["consts"])
                    bring(sp, x_in, a["x"][0].rearrange("(t p) d -> p t d", p=P))
                    for name, (g, r, k) in VEC_ROW.items():
                        src = a[name]
                        pat = {1: "(r c) -> r c", 2: "l (r c) -> (l r) c", 3: "l m (r c) -> (l m r) c"}[len(src.shape)]
                        if name == "rw_rk":
                            src, pat = src.rearrange("l h n -> l (h n)"), "l (r c) -> (l r) c"
                        bring(sp, rows[r:r + k, g, :], src.rearrange(pat, c=P))
                    first_loads(sp)

                @block.gpsimd
                def _(pool):
                    pool.memset(lora[:], 0.0).then_inc(*pool_s.mark("clear"))

                @block.tensor
                def _(pe):
                    pe.wait_ge(in_landed, ins["n"])
                    for g, names in enumerate(VECTORS):
                        r = sum(k for _, k in names)
                        mm = pe.transpose(psum[:, 7, g * P:g * P + r], rows[0:r, g, :], cst[0:r, 0:r])
                    mm.then_inc(*pe_s.mark("vectors"))
                    for t in range(NT):
                        if t == 7:
                            pe.wait_ge(*act_s("vectors"))
                        for q in range(SEQ // P):
                            mm = pe.transpose(psum[:, t, q * P:(q + 1) * P], x_in[:, q, t * P:(t + 1) * P], const("ident"))
                        mm.then_inc(*pe_s.mark(f"x{t}"))

                @block.scalar
                def _(act):
                    act.wait_ge(*pe_s("vectors"))
                    for g, names in enumerate(VECTORS):
                        r = sum(k for _, k in names)
                        op = act.activation(vec[:, g * P:g * P + r], psum[:, 7, g * P:g * P + r], ACT.Copy)
                    op.then_inc(*act_s.mark("vectors"))
                    for t in range(0, NT, 2):
                        act.wait_ge(*pe_s(f"x{t}"))
                        act.activation(h[:, t, :], psum[:, t, :], ACT.Copy).then_inc(*act_s.mark(f"ev x{t}"))

                @block.vector
                def _(dve):
                    for t in range(1, NT, 2):
                        dve.wait_ge(*pe_s(f"x{t}"))
                        dve.tensor_copy(h[:, t, :], psum[:, t, :]).then_inc(*dve_s.mark(f"ev x{t}"))

        def ffn(layer, next_loads):
            stage(f"ffn{layer}")
            hid = arena[:, 2:6, :].rearrange("p a (t s) -> p (a t) s", s=SEQ)
            sq = region(6)
            turns = FT // 8
            use0 = ring.uses
            with nc.Block() as block:
                @block.sync
                def _(sp):
                    ffn_body(sp, layer)
                    next_loads(sp)

                @block.tensor
                def _(pe):
                    norm_pe(pe, "n", sq)
                    pe.wait_ge(*dve_s(f"n out{NT - 1}"))
                    with pe.Fori(0, turns) as i:
                        pe_s.start_loop(i)
                        for s in range(SLOTS):
                            slot_landed(pe, s, i)
                            for n in range(2):
                                b = 2 * s + n
                                pe.wait_ge(*act_s(f"relu{b}", i - 1))
                                for k in range(NT):
                                    mm = pe.matmul(psum[:, b, :], cols_slot(s)[:, k, n * P:(n + 1) * P], u[:, k, :],
                                                   start=(k == 0), stop=(k == NT - 1))
                                mm.then_inc(*pe_s.mark(f"up{b}"))
                        pe_s.end_loop(turns)
                    ring.uses += turns * SLOTS
                    pe.wait_ge(*dve_s("square7", turns - 1))

                    def down(turn, i, first):
                        for s in range(SLOTS):
                            slot_landed(pe, s, turn)
                            for k in range(2):
                                for n in range(NT):
                                    mm = pe.matmul(psum[:, n, :], rows_slot(s)[:, k, n * P:(n + 1) * P],
                                                   hid[:, turn * 8 + (2 * s + k), :], start=(first and s == 0 and k == 0),
                                                   stop=False, skip_group_check=True)
                            mm.then_inc(*pe_s.mark(f"down{s}" + first * " first"))

                    down(0, None, True)
                    with pe.Fori(0, turns - 1) as i:
                        pe_s.start_loop(i)
                        down(i + 1, i, False)
                        pe_s.end_loop(turns - 1)
                    ring.uses += turns * SLOTS

                @block.scalar
                def _(act):
                    norm_act(act, "n", h, sq)
                    with act.Fori(0, turns) as i:
                        act_s.start_loop(i)
                        for b in range(8):
                            act.wait_ge(*pe_s(f"up{b}", i))
                            act.activation(hid[:, i * 8 + b, :], psum[:, b, :], ACT.Relu).then_inc(*act_s.mark(f"relu{b}"))
                        act_s.end_loop(turns)

                @block.vector
                def _(dve):
                    norm_dve(dve, "n", h, u, lambda t: col("norm_ffn", layer * NT + t))
                    with dve.Fori(0, turns) as i:
                        dve_s.start_loop(i)
                        for b in range(8):
                            dve.wait_ge(*act_s(f"relu{b}", i))
                            dve.tensor_tensor(hid[:, i * 8 + b, :], hid[:, i * 8 + b, :], hid[:, i * 8 + b, :],
                                              ALU.mult).then_inc(*dve_s.mark(f"square{b}"))
                        dve_s.end_loop(turns)
                    dve.wait_ge(*pe_s(f"down{SLOTS - 1}", turns - 2))
                    for n in range(NT):
                        dve.tensor_tensor(h[:, n, :], h[:, n, :], psum[:, n, :], ALU.add).then_inc(*dve_s.mark(f"add{n}"))

        def end():
            stage("end")
            sq = region(6)
            out_sb = arena[:, 2, :].rearrange("p (t d) -> p t d", d=DM)
            with nc.Block() as block:
                @block.tensor
                def _(pe):
                    norm_pe(pe, "n", sq)
                    for q in range(SEQ // P):
                        for half in range(2):
                            j = 2 * q + half
                            if j == 7:
                                pe.wait_ge(*act_s("n root"))
                            for t in range(4):
                                pe.wait_ge(*dve_s(f"n out{4 * half + t}"))
                                mm = pe.transpose(psum[:, j, t * P:(t + 1) * P],
                                                  u[:, 4 * half + t, q * P:(q + 1) * P], const("ident"))
                            mm.then_inc(*pe_s.mark(f"y{j}"))

                @block.scalar
                def _(act):
                    norm_act(act, "n", h, sq)
                    for j in range(0, 8, 2):
                        act.wait_ge(*pe_s(f"y{j}"))
                        act.activation(out_sb[:, j // 2, 0:512], psum[:, j, :], ACT.Copy).then_inc(*act_s.mark(f"y{j}"))

                @block.vector
                def _(dve):
                    norm_dve(dve, "n", h, u, lambda t: col("norm_final", t))
                    for j in range(1, 8, 2):
                        dve.wait_ge(*pe_s(f"y{j}"))
                        dve.tensor_copy(out_sb[:, j // 2, 512:1024], psum[:, j, :]).then_inc(*dve_s.mark(f"y{j}"))

                @block.sync
                def _(sp):
                    for q in range(SEQ // P):
                        sp.wait_ge(*act_s(f"y{2 * q}"))
                        sp.wait_ge(*dve_s(f"y{2 * q + 1}"))
                        sp.dma_start(a["out"][0, q * P:(q + 1) * P, :], out_sb[:, q, :]).then_inc(out_landed, 16)
                    sp.wait_ge(out_landed, 16 * (SEQ // P))

        def rwkv_jobs(second):
            eight = lambda tag, who="act": [(f"{tag}{n}", who) for n in range(NT)]
            jobs = eight("r") + eight("k") + eight("v")
            if second:
                jobs += [("v low", "act")] + eight("vmix")
            jobs += [("w low", "act")] + eight("w") + [("a low", "act")] + eight("a") + [("g low", "act")]
            jobs += eight("g") + eight("kk", "dve")
            return jobs

        MIX = {"r": 0, "w": 1, "k": 2, "v": 3, "a": 4, "g": 5}

        def rwkv_project(layer, m):
            stage(f"project{m}")
            second = m > 0
            xx = gate = region(2)
            mixed = [region(3), region(4)]
            order = ["r", "k", "v", "w", "a", "g"]
            r, k, v, lw, av = (region(j) for j in range(5, 10))
            low_v = arena[:, 8, 0:1024].rearrange("p (t s) -> p t s", s=512)
            v1 = arena[:, 8, 1024:1024 + NT * LORA_V].rearrange("p (k n) -> p k n", n=LORA_V)
            v2 = arena[0:LORA_V, 8, 2048:2048 + DM]
            w1 = lora[:, 0:512].rearrange("p (k n) -> p k n", n=LORA_W)
            a1 = lora[:, 512:1024].rearrange("p (k n) -> p k n", n=LORA_A)
            g1 = lora[:, 1024:2048].rearrange("p (k n) -> p k n", n=LORA_G)
            w2, a2 = lora[0:LORA_W, 2048:3072], lora[0:LORA_A, 3072:4096]
            g2 = lora[:, 4096:5120]
            banks = Banks(rwkv_jobs(second))
            kkn = region(1)
            resets = arena[:, 4, 0:512]
            loads0 = ins["n"]

            def mixed_of(p):
                return mixed[order.index(p) % 2]

            with nc.Block() as block:
                @block.sync
                def _(sp):
                    km = lambda w: w.rearrange("(k p) n -> p k n", p=P)
                    bring(sp, w1, km(a["rw_w1"][m]))
                    bring(sp, a1, km(a["rw_a1"][m]))
                    bring(sp, g1, km(a["rw_g1"][m]))
                    bring(sp, w2, a["rw_w2"][m])
                    bring(sp, a2, a["rw_a2"][m])
                    bring(sp, g2, a["rw_g2"][m])
                    if second:
                        bring(sp, v1, km(a["rw_v1"][0]))
                        bring(sp, v2, a["rw_v2"][0])
                        bring(sp, av, a["v_first"].rearrange("p (t s) -> p t s", s=SEQ))
                    load_proj(sp, a["rw_wk"][m], lambda s: pe_s(f"r{2 * s + 1}"))
                    load_proj(sp, a["rw_wv"][m], lambda s: pe_s(f"k{2 * s + 1}"))
                    load_proj(sp, a["rw_wo"][m], lambda s: pe_s(f"v{2 * s + 1}"))
                    sp.wait_ge(*pe_s("g low"))
                    bring(sp, resets, a["extras"][:, P + ROPE:P + ROPE + 512])
                    if not second:
                        sp.wait_ge(*act_s(f"ev v{NT - 1}"))
                        sp.dma_start(a["v_first"].rearrange("p (t s) -> p t s", s=SEQ), v).then_inc(v_stored, 16)
                        sp.wait_ge(v_stored, 16)
                loads_all = ins["n"]

                @block.tensor
                def _(pe):
                    norm_pe(pe, "n", mixed[1])

                    def low_rank(p, job, w, x, rows):
                        pe.wait_ge(*banks.free(job))
                        for kt in range(NT):
                            pe.wait_ge(*dve_s(f"mix {p}{kt}"))
                            mm = pe.matmul(banks.bank(job)[0:rows], w[:, kt, :], x[:, kt, :],
                                           start=(kt == 0), stop=(kt == NT - 1))
                        mm.then_inc(*pe_s.mark(job))

                    def widen(tag, low_job, w, x):
                        pe.wait_ge(*act_s(f"ev {low_job}"))
                        for n in range(NT):
                            job = f"{tag}{n}"
                            pe.wait_ge(*banks.free(job))
                            pe.matmul(banks.bank(job), w[:, n * P:(n + 1) * P], x,
                                      start=True, stop=True).then_inc(*pe_s.mark(job))

                    for p in "rkv":
                        proj_pe(pe, p, banks, mixed_of(p), lambda kt: dve_s(f"mix {p}{kt}"))
                    pe.wait_ge(in_landed, loads_all - 16)
                    if second:
                        low_rank("v", "v low", v1, mixed_of("v"), LORA_V)
                        widen("vmix", "v low", v2, low[0][0:LORA_V, :])
                    low_rank("w", "w low", w1, mixed_of("w"), LORA_W)
                    widen("w", "w low", w2, low[1][0:LORA_W, :])
                    low_rank("a", "a low", a1, mixed_of("a"), LORA_A)
                    widen("a", "a low", a2, low[0][0:LORA_A, :])
                    low_rank("g", "g low", g1, mixed_of("g"), LORA_G)
                    widen("g", "g low", g2, low[1])
                    for t in range(NT):
                        pe.wait_ge(*banks.free(f"kk{t}"))
                        pe.wait_ge(*act_s(f"kk sq{t}"))
                        pe.matmul(banks.bank(f"kk{t}"), const("pair"), mixed[0][:, t, :],
                                  start=True, stop=True).then_inc(*pe_s.mark(f"kk{t}"))

                @block.scalar
                def _(act):
                    norm_act(act, "n", h, mixed[1])

                    def out(job, dst, func=ACT.Copy, **kw):
                        act.wait_ge(*pe_s(job))
                        act.activation(dst, banks.bank(job)[0:dst.shape[0]], func, **kw).then_inc(*act_s.mark(f"ev {job}"))

                    for n in range(NT):
                        out(f"r{n}", r[:, n, :])
                    for n in range(NT):
                        out(f"k{n}", k[:, n, :])
                    for n in range(NT):
                        out(f"v{n}", v[:, n, :])
                    if second:
                        out("v low", low[0][0:LORA_V, :])
                        for n in range(NT):
                            if n >= 2:
                                act.wait_ge(*dve_s(f"vmix{n - 2}"))
                            out(f"vmix{n}", low_v[:, n % 2, :], ACT.Sigmoid, bias=col("rw_v0", n))
                        act.wait_ge(*dve_s(f"vmix{NT - 1}"))
                    out("w low", low[1][0:LORA_W, :], ACT.Tanh)
                    for n in range(NT):
                        out(f"w{n}", lw[:, n, :], ACT.Sigmoid, bias=col("rw_w0", m * NT + n))
                    if second:
                        act.wait_ge(*pe_s(f"vmix{NT - 1}"))
                    out("a low", low[0][0:LORA_A, :])
                    for n in range(NT):
                        out(f"a{n}", av[:, n, :], ACT.Sigmoid, bias=col("rw_a0", m * NT + n))
                    act.wait_ge(*pe_s(f"w{NT - 1}"))
                    out("g low", low[1], ACT.Sigmoid)
                    act.wait_ge(*dve_s(f"mix g{NT - 1}"))
                    for t in range(NT):
                        act.activation(kkn[:, t, :], k[:, t, :], ACT.Copy,
                                       scale=col("rw_kk", m * NT + t)).then_inc(*act_s.mark(f"kk{t}"))
                    for t in range(NT):
                        act.wait_ge(*act_s(f"kk{t}"))
                        act.activation(mixed[0][:, t, :], kkn[:, t, :], ACT.Square).then_inc(*act_s.mark(f"kk sq{t}"))
                    for n in range(NT):
                        out(f"g{n}", gate[:, n, :])
                    for t in range(NT):
                        act.wait_ge(*dve_s(f"kk max{t}"))
                        act.activation(mixed[0][:, t, :], mixed[0][:, t, :],
                                       ACT.Sqrt).then_inc(*act_s.mark(f"kk root{t}"))

                @block.vector
                def _(dve):
                    norm_dve(dve, "n", h, u, lambda t: col("norm_mix", layer * NT + t))
                    for t in range(NT):
                        dve.wait_ge(*dve_s(f"n out{t}"))
                        dve.tensor_tensor(xx[:, t, 1:SEQ], u[:, t, 0:SEQ - 1], u[:, t, 1:SEQ],
                                          ALU.subtract).then_inc(*dve_s.mark(f"shift{t}"))
                        dve.tensor_scalar(xx[:, t, 0:1], u[:, t, 0:1], -1.0, None,
                                          ALU.mult).then_inc(*dve_s.mark(f"shift first{t}"))

                    def mix(p):
                        if p in "rk":
                            dve.wait_ge(*dve_s(f"shift first{NT - 1}"))
                        else:
                            dve.wait_ge(*pe_s({"v": "r7", "w": "k7", "a": "v low" if second else "v7", "g": "w low"}[p]))
                        for t in range(NT):
                            dve.scalar_tensor_tensor(mixed_of(p)[:, t, :], xx[:, t, :],
                                                     col("rw_mu", (m * 6 + MIX[p]) * NT + t), u[:, t, :],
                                                     ALU.mult, ALU.add).then_inc(*dve_s.mark(f"mix {p}{t}"))

                    mix("r")
                    mix("k")
                    mix("v")
                    mix("w")
                    if second:
                        dve.wait_ge(in_landed, loads_all - 16)
                        for t in range(NT):
                            dve.wait_ge(*act_s(f"ev v{t}"))
                            dve.tensor_tensor(av[:, t, :], av[:, t, :], v[:, t, :],
                                              ALU.subtract).then_inc(*dve_s.mark(f"v gap{t}"))
                        for t in range(NT):
                            dve.wait_ge(*dve_s(f"v gap{t}"))
                            dve.wait_ge(*act_s(f"ev vmix{t}"))
                            dve.tensor_tensor(av[:, t, :], av[:, t, :], low_v[:, t % 2, :],
                                              ALU.mult).then_inc(*dve_s.mark(f"vmix{t}"))
                        for t in range(NT):
                            dve.wait_ge(*dve_s(f"vmix{t}"))
                            dve.tensor_tensor(v[:, t, :], v[:, t, :], av[:, t, :],
                                              ALU.add).then_inc(*dve_s.mark(f"v mixed{t}"))
                    mix("a")
                    mix("g")
                    for t in range(NT):
                        dve.wait_ge(*pe_s(f"kk{t}"))
                        dve.tensor_scalar(mixed[0][:, t, :], banks.bank(f"kk{t}"), 1e-24, None,
                                          ALU.max).then_inc(*dve_s.mark(f"kk max{t}"))
                    for t in range(NT):
                        dve.wait_ge(*act_s(f"ev a{t}"))
                        dve.tensor_scalar(mixed[1][:, t % 2 + 2, :], av[:, t, :], 1.0, col("rw_ka", m * NT + t),
                                          ALU.subtract, ALU.mult).then_inc(*dve_s.mark(f"ka{t}"))
                        dve.wait_ge(*dve_s(f"ka{t}"))
                        dve.wait_ge(*act_s(f"kk{t}"))
                        dve.scalar_tensor_tensor(k[:, t, :], mixed[1][:, t % 2 + 2, :], 1.0, k[:, t, :],
                                                 ALU.add, ALU.mult).then_inc(*dve_s.mark(f"k eff{t}"))
                    dve.wait_ge(in_landed, loads_all)
                    for t in range(NT):
                        dve.wait_ge(*act_s(f"ev w{t}"))
                        dve.tensor_tensor_scan(lw[:, t, :], resets, lw[:, t, :], 0.0, ALU.mult,
                                               ALU.add).then_inc(*dve_s.mark(f"decay{t}"))
                    for t in range(NT):
                        dve.wait_ge(*act_s(f"kk root{t}"))
                        dve.reciprocal(mixed[0][:, t, :], mixed[0][:, t, :]).then_inc(*dve_s.mark(f"kk inv{t}"))
                        dve.wait_ge(*dve_s(f"kk inv{t}"))
                        dve.scalar_tensor_tensor(kkn[:, t, :], kkn[:, t, :], -1.0, mixed[0][:, t, :],
                                                 ALU.mult, ALU.mult).then_inc(*dve_s.mark(f"kkn{t}"))
                        dve.wait_ge(*dve_s(f"kkn{t}"))
                        dve.scalar_tensor_tensor(av[:, t, :], av[:, t, :], -1.0, kkn[:, t, :],
                                                 ALU.mult, ALU.mult).then_inc(*dve_s.mark(f"b{t}"))

        def rwkv_scan(m):
            stage(f"scan{m}")
            r, k, v, lw, b, kkn = region(5), region(6), region(7), region(8), region(9), region(1)
            flat = arena[:, 3:5, :].rearrange("p a n -> p (a n)")
            at = {"n": 0}

            def take(n, of=None):
                at["n"] += n
                return flat[:, at["n"] - n:at["n"]]

            def tile3(x, w):
                return x.rearrange("p (t n) -> p t n", n=w)

            ar = take(1024).rearrange("p (t two n) -> p t two n", two=2, n=CH)
            bk = take(1024).rearrange("p (t two n) -> p t two n", two=2, n=CH)
            gm = take(2048).rearrange("p (h n) -> p h n", n=P)
            bkt = tile3(take(1024), P)
            uv = tile3(take(1024), P)
            state = tile3(take(1024), P)
            vst = tile3(take(1024), P)
            grow = tile3(lora[:, 0:512], CH)
            prod = tile3(lora[:, 512:1024], CH)
            xs = tile3(lora[:, 1024:1536], CH)
            decay = lora[:, 1536:1536 + NT * (CH + 1)].rearrange("p (t n) -> p t n", n=CH + 1)
            tb = [tile3(lora[:, 2112 + 512 * j:2624 + 512 * j], CH) for j in range(5)]
            tb += [tile3(small[:, 512 * j:512 * (j + 1)], CH) for j in range(3)]
            bank = lambda j: psum[:, j, :]
            b64 = lambda j: psum[:, j, :].rearrange("p (t n) -> p t n", n=CH)
            b128 = lambda j: psum[:, j, :].rearrange("p (t n) -> p t n", n=P)

            def wide(name):
                return const(name).unsqueeze(1).broadcast_to([P, NT, CH])

            mask_g = const("mask_g").unsqueeze(1).broadcast_to([P, 4, P])
            halves = [slice(0, CH), slice(CH, P)]
            D, Dt, Et, IpD = tb[0], tb[1], tb[2], tb[3]
            D2, D2t, ID2t = tb[4], tb[5], tb[6]
            D4, D4t, ID4t, X2 = tb[0], tb[1], tb[6], tb[7]
            ID8t, X4 = tb[4], tb[5]
            X8, X8t = tb[3], tb[0]
            F, Ft, IpF = tb[1], tb[6], tb[7]
            IF2, Z, Tt = tb[4], tb[5], tb[3]

            with nc.Block() as block:
                @block.gpsimd
                def _(pool):
                    pool.memset(state[:], 0.0).then_inc(*pool_s.mark("zero state"))
                    pool.memset(uv[:], 0.0).then_inc(*pool_s.mark("zero uv"))
                    pool.memset(vst[:], 0.0).then_inc(*pool_s.mark("zero v"))
                    pool.memset(decay[:, :, 0:1], 1.0).then_inc(*pool_s.mark("ones"))
                    pool.wait_ge(*pool_s("ones"))
                    with pool.Fori(0, NCH) as i:
                        pool_s.start_loop(i)
                        now = bass.ts(i, CH)
                        pool.wait_ge(*pe_s("V", i - 1))
                        pool.tensor_copy(vst[:, :, CH:P], v[:, :, now]).then_inc(*pool_s.mark("stage v"))
                        pool.wait_ge(*pe_s("bonus", i - 1))
                        pool.sem_inc(passed_pool, 1)
                        pool.tensor_tensor(prod, r[:, :, now], k[:, :, now], ALU.mult).then_inc(*pool_s.mark("rk"))
                        pool.wait_ge(*pool_s("rk", i))
                        rk0 = VEC_ROW["rw_rk"][0] * P + VEC_ROW["rw_rk"][1] + m * NT
                        pool.tensor_tensor(prod, prod, vec[:, rk0:rk0 + NT].unsqueeze(2).broadcast_to([P, NT, CH]),
                                           ALU.mult).then_inc(*pool_s.mark("rk r_k"))
                        pool.wait_ge(*act_s("decay", i))
                        pool.wait_ge(*pe_s("Y", i - 1))
                        pool.sem_inc(passed_pool, 1)
                        pool.tensor_tensor(ar[:, :, 1, :], r[:, :, now], decay[:, :, 1:CH + 1],
                                           ALU.mult).then_inc(*pool_s.mark("R"))
                        pool_s.end_loop(NCH)

                @block.scalar
                def _(act):
                    act.wait_ge(*pool_s("ones"))
                    with act.Fori(0, NCH) as i:
                        act_s.start_loop(i)
                        now = bass.ts(i, CH)
                        act.wait_ge(*dve_s("state1", i - 1))
                        act.activation(decay[:, :, 1:CH + 1], lw[:, :, now], ACT.Exp,
                                       scale=-DECAY).then_inc(*act_s.mark("decay"))
                        act.activation(grow, lw[:, :, now], ACT.Exp, scale=DECAY).then_inc(*act_s.mark("grow"))

                        def out(name, dst, src):
                            act.wait_ge(*pe_s(name, i))
                            act.activation(dst, src, ACT.Copy).then_inc(*act_s.mark(f"ev {name}"))

                        out("BK0", bkt[:, 0:4, :], b128(2))
                        out("BK1", bkt[:, 4:8, :], b128(3))
                        out("V0", uv[halves[1], 0:4, :], b128(4)[halves[1]])
                        out("V", uv[halves[1], 4:8, :], b128(5)[halves[1]])
                        out("D2", D2, b64(0))
                        out("D2t", D2t, b64(1))
                        act.wait_ge(*dve_s("I+D2t", i))
                        out("D4", D4, b64(2))
                        out("D4t", D4t, b64(3))
                        out("X2", X2, b64(4))
                        out("X4", X4, b64(6))
                        out("X8", X8, b64(0))
                        out("F", F, b64(2))
                        out("Ft", Ft, b64(3))
                        out("Z", Z, b64(5))
                        out("U0", uv[halves[0], :, halves[0]], b64(1)[halves[0]])
                        out("U1", uv[halves[0], :, halves[1]], b64(2)[halves[0]])
                        act.wait_ge(*pool_s("R", i))
                        out("Y", r[:, :, now], b64(3))
                        act_s.end_loop(NCH)

                @block.vector
                def _(dve):
                    with dve.Fori(0, NCH) as i:
                        dve_s.start_loop(i)
                        now = bass.ts(i, CH)
                        dve.wait_ge(*act_s("decay", i))
                        dve.tensor_tensor(ar[:, :, 0, :], kkn[:, :, now], decay[:, :, 0:CH],
                                          ALU.mult).then_inc(*dve_s.mark("A"))
                        dve.wait_ge(*act_s("grow", i))
                        dve.tensor_tensor(bk[:, :, 0, :], b[:, :, now], grow, ALU.mult).then_inc(*dve_s.mark("B"))
                        dve.tensor_tensor(bk[:, :, 1, :], k[:, :, now], grow, ALU.mult).then_inc(*dve_s.mark("K"))

                        def masked(mark, job, dst, src, mask, **kw):
                            dve.wait_ge(*pe_s(job, i))
                            dve.tensor_tensor(dst, src, mask, kw.get("op", ALU.mult)).then_inc(*dve_s.mark(mark))

                        masked("D", "M", D, b64(0), wide("mask_d"))
                        masked("Dt", "Mt", Dt, b64(1), wide("mask_dt"))
                        masked("Et", "Mt", Et, b64(1), wide("mask_et"))
                        dve.wait_ge(*dve_s("D", i))
                        dve.tensor_tensor(IpD, D, wide("eye2"), ALU.add).then_inc(*dve_s.mark("I+D"))
                        dve.wait_ge(*pe_s("bonus", i))
                        dve.wait_ge(*pool_s("rk r_k", i))
                        dve.tensor_tensor(k[:, :, now], v[:, :, now], b64(6), ALU.mult).then_inc(*dve_s.mark("ev bonus"))
                        dve.wait_ge(*act_s("ev D2t", i))
                        dve.tensor_tensor(ID2t, D2t, wide("eye2"), ALU.add).then_inc(*dve_s.mark("I+D2t"))
                        masked("G0", "G0", gm[:, 0:8:2, :], b128(7), mask_g)
                        masked("G1", "G1", gm[:, 1:8:2, :], b128(5), mask_g)
                        dve.wait_ge(*act_s("ev D4t", i))
                        dve.wait_ge(*pe_s("X2", i))
                        dve.tensor_tensor(ID4t, D4t, wide("eye2"), ALU.add).then_inc(*dve_s.mark("I+D4t"))
                        masked("G2", "G2", gm[:, 8:16:2, :], b128(6), mask_g)
                        masked("I+D8t", "D8t", ID8t, b64(5), wide("eye2"), op=ALU.add)
                        masked("G3", "G3", gm[:, 9:16:2, :], b128(7), mask_g)
                        dve.wait_ge(*pe_s("X8t", i))
                        dve.tensor_copy(X8t, b64(1)).then_inc(*dve_s.mark("X8t"))
                        dve.wait_ge(*act_s("ev F", i))
                        dve.tensor_tensor(IpF, F, wide("eye2"), ALU.add).then_inc(*dve_s.mark("I+F"))
                        masked("I+F2", "F2", IF2, b64(4), wide("eye2"), op=ALU.add)
                        dve.wait_ge(*pe_s("Tt", i))
                        dve.tensor_copy(Tt, b64(0)).then_inc(*dve_s.mark("Tt"))
                        dve.wait_ge(*pe_s("X", i))
                        dve.tensor_copy(xs, b64(7)).then_inc(*dve_s.mark("X"))
                        dve.wait_ge(*pe_s("S", i))
                        for q, part in enumerate(halves):
                            dve.tensor_tensor(state[part, :, part], state[part, :, part], b64(4)[part],
                                              ALU.add).then_inc(*dve_s.mark(f"sum{q}"))
                        for q, part in enumerate(halves):
                            dve.wait_ge(*dve_s(f"sum{q}", i))
                            dve.tensor_tensor(state[part, :, part], state[part, :, part],
                                              decay[part, :, CH:CH + 1].broadcast_to([CH, NT, CH]),
                                              ALU.mult).then_inc(*dve_s.mark(f"state{q}"))
                        dve_s.end_loop(NCH)

                @block.tensor
                def _(pe):
                    pe.wait_ge(*pool_s("ones"))
                    with pe.Fori(0, NCH) as i:
                        pe_s.start_loop(i)

                        def heads(job, j, lhsT, rhs):
                            for t in range(NT):
                                for part in halves:
                                    mm = pe.matmul(b64(j)[part, t, :], lhsT(part, t), rhs(part, t), start=True, stop=True)
                            mm.then_inc(*pe_s.mark(job))

                        A = lambda part, t: ar[part, t, 0, :]
                        B = lambda part, t: bk[part, t, 0, :]
                        of = lambda x: (lambda part, t: x[part, t, :])
                        pe.wait_ge(*dve_s("B", i))
                        pe.wait_ge(*act_s("ev Y", i - 1))
                        pe.sem_inc(passed_pe, 1)
                        heads("M", 0, A, B)
                        heads("Mt", 1, B, A)
                        pe.wait_ge(*dve_s("K", i))
                        pe.sem_inc(passed_pe, 1)
                        for half in range(2):
                            for t in range(4):
                                mm = pe.transpose(b128(2 + half)[:, t, :], bk[:, 4 * half + t, :, :].rearrange("p a n -> p (a n)"),
                                                  const("ident"))
                            mm.then_inc(*pe_s.mark(f"BK{half}"))
                        pe.wait_ge(*pool_s("stage v", i))
                        pe.sem_inc(passed_pe, 1)
                        for half in range(2):
                            for t in range(4):
                                mm = pe.transpose(b128(4 + half)[:, t, :], vst[:, 4 * half + t, :], const("ident"))
                            mm.then_inc(*pe_s.mark("V" if half else "V0"))
                        pe.wait_ge(*pool_s("rk r_k", i))
                        pe.sem_inc(passed_pe, 1)
                        pe.matmul(bank(6), const("pair"), prod.rearrange("p t n -> p (t n)"),
                                  start=True, stop=True).then_inc(*pe_s.mark("bonus"))
                        pe.wait_ge(*dve_s("Dt", i))
                        pe.sem_inc(passed_pe, 1)
                        heads("D2", 0, of(Dt), of(D))
                        pe.wait_ge(*dve_s("Et", i))
                        pe.sem_inc(passed_pe, 1)
                        heads("D2t", 1, of(D), of(Dt))

                        def products(job, j, t0, part):
                            for t in range(4):
                                mm = pe.matmul(b128(j)[:, t, :], bk[part, t0 + t, :, :], ar[part, t0 + t, :, :],
                                               start=True, stop=True)
                            mm.then_inc(*pe_s.mark(job))

                        pe.wait_ge(*pool_s("R", i))
                        pe.sem_inc(passed_pe, 1)
                        products("G0", 7, 0, halves[0])
                        pe.wait_ge(*act_s("ev V", i))
                        pe.sem_inc(passed_pe, 1)
                        products("G1", 5, 0, halves[1])
                        pe.wait_ge(*act_s("ev D2t", i))
                        pe.sem_inc(passed_pe, 1)
                        heads("D4", 2, of(D2t), of(D2))
                        heads("D4t", 3, of(D2), of(D2t))
                        pe.wait_ge(*dve_s("I+D2t", i))
                        pe.sem_inc(passed_pe, 1)
                        heads("X2", 4, of(ID2t), of(IpD))
                        products("G2", 6, 4, halves[0])
                        pe.wait_ge(*dve_s("G1", i))
                        pe.wait_ge(*act_s("ev D4t", i))
                        pe.sem_inc(passed_pe, 1)
                        heads("D8t", 5, of(D4), of(D4t))
                        products("G3", 7, 4, halves[1])
                        pe.wait_ge(*act_s("ev X2", i))
                        pe.wait_ge(*dve_s("G2", i))
                        pe.sem_inc(passed_pe, 1)
                        heads("X4", 6, of(ID4t), of(X2))
                        pe.wait_ge(*act_s("ev X4", i))
                        pe.wait_ge(*dve_s("I+D8t", i))
                        pe.sem_inc(passed_pe, 1)
                        heads("X8", 0, of(ID8t), of(X4))
                        heads("X8t", 1, of(X4), of(ID8t))
                        pe.wait_ge(*act_s("ev X8", i))
                        pe.sem_inc(passed_pe, 1)
                        heads("F", 2, of(Et), of(X8))
                        heads("Ft", 3, of(X8), of(Et))
                        pe.wait_ge(*act_s("ev Ft", i))
                        pe.sem_inc(passed_pe, 1)
                        heads("F2", 4, of(Ft), of(F))
                        pe.wait_ge(*dve_s("I+F", i))
                        pe.sem_inc(passed_pe, 1)
                        heads("Z", 5, of(IpF), of(X8t))
                        pe.wait_ge(*act_s("ev Z", i))
                        pe.wait_ge(*dve_s("I+F2", i))
                        pe.sem_inc(passed_pe, 1)
                        heads("Tt", 0, of(IF2), of(Z))
                        pe.wait_ge(*dve_s("state1", i - 1))
                        pe.sem_inc(passed_pe, 1)
                        for t in range(NT):
                            for q, part in enumerate(halves):
                                pe.matmul(b64(7)[part, t, :], ar[:, t, 0, :], state[:, t, part], start=True, stop=False)
                                mm = pe.matmul(b64(7)[part, t, :], gm[:, 2 * t + q, 0:CH], uv[:, t, part],
                                               start=False, stop=True)
                        mm.then_inc(*pe_s.mark("X"))
                        pe.wait_ge(*dve_s("X", i))
                        pe.sem_inc(passed_pe, 1)
                        for q, part in enumerate(halves):
                            for t in range(NT):
                                mm = pe.matmul(b64(1 + q)[halves[0], t, :], Tt[part, t, :], xs[part, t, :],
                                               start=True, stop=True)
                            mm.then_inc(*pe_s.mark(f"U{q}"))
                        pe.wait_ge(*act_s("ev U1", i))
                        pe.sem_inc(passed_pe, 1)
                        for t in range(NT):
                            pe.matmul(b64(3)[:, t, :], state[:, t, :], ar[:, t, 1, :], start=True, stop=False,
                                      skip_group_check=True)
                            for q, part in enumerate(halves):
                                mm = pe.matmul(b64(3)[part, t, :], uv[:, t, part], gm[:, 2 * t + q, CH:P],
                                               start=False, stop=True, skip_group_check=True)
                        mm.then_inc(*pe_s.mark("Y"))
                        for t in range(NT):
                            for part in halves:
                                mm = pe.matmul(b64(4)[part, t, :], bkt[:, t, part], uv[:, t, part], start=True, stop=True)
                        mm.then_inc(*pe_s.mark("S"))
                        pe_s.end_loop(NCH)

        def rwkv_finish(layer, m):
            stage(f"finish{m}")
            y, bonus, gate, yc, sq, sd = region(5), region(6), region(2), region(7), region(3), region(4)
            banks = Banks([(f"mean{t}", "dve") for t in range(NT)] + [(f"var{t}", "act") for t in range(NT)]
                          + [(f"o{t}", "dve") for t in range(NT)])
            with nc.Block() as block:
                @block.sync
                def _(sp):
                    ffn_head(sp, layer, lambda s: pe_s(f"o{2 * s + 1}"))

                @block.tensor
                def _(pe):
                    for t in range(NT):
                        pe.matmul(banks.bank(f"mean{t}"), const("pair"), y[:, t, :],
                                  start=True, stop=True).then_inc(*pe_s.mark(f"mean{t}"))
                    for t in range(NT):
                        pe.wait_ge(*banks.free(f"var{t}"))
                        pe.wait_ge(*act_s(f"sq{t}"))
                        pe.matmul(banks.bank(f"var{t}"), const("pair"), sq[:, t, :],
                                  start=True, stop=True).then_inc(*pe_s.mark(f"var{t}"))
                    proj_pe(pe, "o", banks, y, lambda k: pool_s(f"gated{k}"))

                @block.scalar
                def _(act):
                    for t in range(NT):
                        act.wait_ge(*dve_s(f"ev mean{t}"))
                        act.activation(sq[:, t, :], yc[:, t, :], ACT.Square).then_inc(*act_s.mark(f"sq{t}"))
                    for t in range(NT):
                        act.wait_ge(*pe_s(f"var{t}"))
                        act.activation(sd[:, t, :], banks.bank(f"var{t}"), ACT.Sqrt, bias=gn_eps,
                                       scale=1.0 / HEAD).then_inc(*act_s.mark(f"ev var{t}"))

                @block.vector
                def _(dve):
                    for t in range(NT):
                        dve.wait_ge(*pe_s(f"mean{t}"))
                        dve.scalar_tensor_tensor(yc[:, t, :], banks.bank(f"mean{t}"), -1.0 / HEAD, y[:, t, :],
                                                 ALU.mult, ALU.add).then_inc(*dve_s.mark(f"ev mean{t}"))
                    for t in range(NT):
                        dve.wait_ge(*act_s(f"ev var{t}"))
                        dve.reciprocal(sd[:, t, :], sd[:, t, :]).then_inc(*dve_s.mark(f"inv{t}"))
                        dve.wait_ge(*dve_s(f"inv{t}"))
                        dve.scalar_tensor_tensor(yc[:, t, :], yc[:, t, :], col("rw_lnx_w", m * NT + t), sd[:, t, :],
                                                 ALU.mult, ALU.mult).then_inc(*dve_s.mark(f"scaled{t}"))
                        dve.wait_ge(*dve_s(f"scaled{t}"))
                        dve.scalar_tensor_tensor(yc[:, t, :], yc[:, t, :], col("rw_lnx_b", m * NT + t), bonus[:, t, :],
                                                 ALU.add, ALU.add).then_inc(*dve_s.mark(f"with bonus{t}"))
                    for t in range(NT):
                        dve.wait_ge(*pe_s(f"o{t}"))
                        dve.tensor_tensor(h[:, t, :], h[:, t, :], banks.bank(f"o{t}"),
                                          ALU.add).then_inc(*dve_s.mark(f"ev o{t}"))

                @block.gpsimd
                def _(pool):
                    for t in range(NT):
                        pool.wait_ge(*dve_s(f"with bonus{t}"))
                        pool.tensor_tensor(y[:, t, :], yc[:, t, :], gate[:, t, :],
                                           ALU.mult).then_inc(*pool_s.mark(f"gated{t}"))

        def conv_glu(layer):
            stage("glu")
            sq = region(6)
            banks = Banks([(f"{x}{4 * turn + 2 * p + n}", "dve" if x == "a" else "act")
                           for turn in range(2) for p in range(2) for x in "ab" for n in range(2)])
            with nc.Block() as block:
                @block.sync
                def _(sp):
                    bring(sp, taps_rows, a["cv_dw"][0])
                    w1 = a["cv_w1"][0].rearrange("(k p) n -> p k n", p=P)
                    for s in range(SLOTS):
                        c = (2 + s // 2) * 256 + (s % 2) * DM
                        last = [f"a{1 + 2 * (s // 2)}", f"b{1 + 2 * (s // 2)}"][s % 2]
                        ring.load(sp, cols_slot(s), w1[:, :, c:c + 256], pe_s(last))
                    load_proj(sp, a["cv_w2"][0], lambda s: pe_s([f"a{5 + 2 * (s // 2)}", f"b{5 + 2 * (s // 2)}"][s % 2]))
                taps_in = ins["n"]

                @block.gpsimd
                def _(pool):
                    pool.memset(glu[:, :, 0:PAD], 0.0).then_inc(*pool_s.mark("pad"))

                @block.tensor
                def _(pe):
                    pe.wait_ge(in_landed, taps_in)
                    for t in range(NT):
                        mm = pe.transpose(psum[:, 6, t * TAPS:(t + 1) * TAPS], taps_rows[:, t * P:(t + 1) * P],
                                          cst[0:TAPS, 0:TAPS])
                    mm.then_inc(*pe_s.mark("taps"))
                    norm_pe(pe, "n", sq)
                    for turn in range(2):
                        for s in range(SLOTS):
                            slot_landed(pe, s)
                            for n in range(2):
                                job = f"{'ab'[s % 2]}{4 * turn + 2 * (s // 2) + n}"
                                if banks.free(job):
                                    pe.wait_ge(*banks.free(job))
                                if turn == 0 and banks.names.index(job) == 6:
                                    pe.wait_ge(*act_s("taps"))
                                if turn == 0 and banks.names.index(job) == 7:
                                    pe.wait_ge(*act_s("n root"))
                                for k in range(NT):
                                    if job == "a0":
                                        pe.wait_ge(*dve_s(f"n out{k}"))
                                    mm = pe.matmul(banks.bank(job), cols_slot(s)[:, k, n * P:(n + 1) * P], u[:, k, :],
                                                   start=(k == 0), stop=(k == NT - 1))
                                mm.then_inc(*pe_s.mark(job))
                        ring.uses += SLOTS

                @block.scalar
                def _(act):
                    norm_act(act, "n", h, sq)
                    act.wait_ge(*pe_s("taps"))
                    act.activation(taps.rearrange("p t j -> p (t j)"), psum[:, 6, 0:NT * TAPS],
                                   ACT.Copy).then_inc(*act_s.mark("taps"))
                    for n in range(NT):
                        act.wait_ge(*pe_s(f"b{n}"))
                        act.activation(sig[:, n, :], banks.bank(f"b{n}"), ACT.Sigmoid,
                                       bias=col("cv_b1", NT + n)).then_inc(*act_s.mark(f"ev b{n}"))

                @block.vector
                def _(dve):
                    norm_dve(dve, "n", h, u, lambda t: col("norm_mix", layer * NT + t))
                    for n in range(NT):
                        dve.wait_ge(*pe_s(f"a{n}"))
                        dve.wait_ge(*act_s(f"ev b{n}"))
                        dve.scalar_tensor_tensor(glu[:, n, PAD:PAD + SEQ], banks.bank(f"a{n}"), col("cv_b1", n),
                                                 sig[:, n, :], ALU.add, ALU.mult).then_inc(*dve_s.mark(f"ev a{n}"))

        def conv_taps():
            stage("taps")
            z, acc, acc2 = region(4), region(5), region(6)
            diag = arena[:, 7, :].rearrange("p (b j c) -> p b j c", b=2, c=P)
            term = arena[:, 8, :].rearrange("p (b s) -> p b s", s=SEQ)
            eye = const("ident").unsqueeze(1).broadcast_to([P, PE_TAPS, P])
            with nc.Block() as block:
                @block.vector
                def _(dve):
                    for t in range(NT):
                        b = t % 2
                        if t >= 2:
                            dve.wait_ge(*pe_s(f"conv{t - 2}"))
                        dve.tensor_tensor(diag[:, b, 0:PE_TAPS, :], eye,
                                          taps[:, t, 0:PE_TAPS].unsqueeze(2).broadcast_to([P, PE_TAPS, P]),
                                          ALU.mult).then_inc(*dve_s.mark(f"diag{t}"))
                        for j in range(PE_TAPS + ACT_TAPS, TAPS):
                            first = j == PE_TAPS + ACT_TAPS
                            if first:
                                op = dve.tensor_scalar(acc[:, t, :], glu[:, t, j:j + SEQ], taps[:, t, j:j + 1], None, ALU.mult)
                            else:
                                dve.wait_ge(*dve_s(f"tap{t} {j - 1}"))
                                op = dve.scalar_tensor_tensor(acc[:, t, :], glu[:, t, j:j + SEQ], taps[:, t, j:j + 1],
                                                              acc[:, t, :], ALU.mult, ALU.add)
                            op.then_inc(*dve_s.mark(f"tap{t} {j}"))
                        dve.wait_ge(*pe_s(f"conv{t}"))
                        dve.wait_ge(*dve_s(f"tap{t} {TAPS - 1}"))
                        dve.scalar_tensor_tensor(acc[:, t, :], psum[:, t, :], col("cv_bdw", t), acc[:, t, :],
                                                 ALU.add, ALU.add).then_inc(*dve_s.mark(f"taps{t}"))
                        dve.wait_ge(*dve_s(f"taps{t}"))
                        dve.wait_ge(*pool_s(f"term{t} {ACT_TAPS - 1}"))
                        dve.tensor_tensor(z[:, t, :], acc[:, t, :], acc2[:, t, :],
                                          ALU.add).then_inc(*dve_s.mark(f"z{t}"))

                @block.scalar
                def _(act):
                    for t in range(NT):
                        for j in range(ACT_TAPS):
                            n = t * ACT_TAPS + j
                            if n >= 8:
                                before = n - 8
                                act.wait_ge(*pool_s(f"term{before // ACT_TAPS} {before % ACT_TAPS}"))
                            tap = PE_TAPS + j
                            act.activation(term[:, n % 8, :], glu[:, t, tap:tap + SEQ], ACT.Copy,
                                           scale=taps[:, t, tap:tap + 1]).then_inc(*act_s.mark(f"term{t} {j}"))

                @block.gpsimd
                def _(pool):
                    for t in range(NT):
                        for j in range(ACT_TAPS):
                            n = t * ACT_TAPS + j
                            pool.wait_ge(*act_s(f"term{t} {j}"))
                            if j == 0:
                                op = pool.tensor_copy(acc2[:, t, :], term[:, n % 8, :])
                            else:
                                pool.wait_ge(*pool_s(f"term{t} {j - 1}"))
                                op = pool.tensor_tensor(acc2[:, t, :], acc2[:, t, :], term[:, n % 8, :], ALU.add)
                            op.then_inc(*pool_s.mark(f"term{t} {j}"))

                @block.tensor
                def _(pe):
                    for t in range(NT):
                        pe.wait_ge(*dve_s(f"diag{t}"))
                        for j in range(PE_TAPS):
                            mm = pe.matmul(psum[:, t, :], diag[:, t % 2, j, :], glu[:, t, j:j + SEQ],
                                           start=(j == 0), stop=(j == PE_TAPS - 1))
                        mm.then_inc(*pe_s.mark(f"conv{t}"))

        def conv_finish(layer):
            stage("convout")
            z, zc, sq = region(4), region(5), region(6)
            banks = Banks([(f"o{t}", "dve") for t in range(NT)])
            with nc.Block() as block:
                @block.sync
                def _(sp):
                    ffn_head(sp, layer, lambda s: pe_s(f"o{2 * s + 1}"))

                @block.tensor
                def _(pe):
                    for t in range(NT):
                        mm = pe.matmul(psum[:, 6, :], const("ones"), z[:, t, :], start=(t == 0), stop=(t == NT - 1))
                    mm.then_inc(*pe_s.mark("mean"))
                    norm_pe(pe, "n", sq)
                    proj_pe(pe, "o", banks, z, lambda k: act_s(f"silu{k}"))

                @block.scalar
                def _(act):
                    for t in range(NT):
                        act.wait_ge(*dve_s(f"centred{t}"))
                        act.activation(sq[:, t, :], zc[:, t, :], ACT.Square).then_inc(*act_s.mark(f"n sq{t}"))
                    act.wait_ge(*pe_s("n sum"))
                    act.activation(rstd, psum[:, 7, :], ACT.Sqrt, bias=eps, scale=1.0 / DM).then_inc(*act_s.mark("n root"))
                    for t in range(NT):
                        act.wait_ge(*dve_s(f"n out{t}"))
                        act.activation(z[:, t, :], zc[:, t, :], ACT.Silu,
                                       bias=col("cv_ln_b", t)).then_inc(*act_s.mark(f"silu{t}"))

                @block.vector
                def _(dve):
                    dve.wait_ge(*pe_s("mean"))
                    for t in range(NT):
                        dve.scalar_tensor_tensor(zc[:, t, :], psum[:, 6, :], -1.0 / DM, z[:, t, :],
                                                 ALU.mult, ALU.add).then_inc(*dve_s.mark(f"centred{t}"))
                    norm_dve(dve, "n", zc, zc, lambda t: col("cv_ln_w", t))
                    for t in range(NT):
                        dve.wait_ge(*pe_s(f"o{t}"))
                        dve.scalar_tensor_tensor(h[:, t, :], banks.bank(f"o{t}"), col("cv_b2", t), h[:, t, :],
                                                 ALU.add, ALU.add).then_inc(*dve_s.mark(f"ev o{t}"))

        glu = arena[:, 2:4, :].rearrange("p a n -> p (a n)")[:, 0:NT * (PAD + SEQ)].rearrange(
            "p (t s) -> p t s", s=PAD + SEQ)
        sig = region(4)
        taps_rows = arena[0:TAPS, 9, 0:DM]
        taps = arena[:, 9, DM:DM + NT * TAPS].rearrange("p (t j) -> p t j", j=TAPS)

        cbuf = region(2)
        kr, sin_t, cos_t = (cbuf[NOPE:QK, t, :] for t in (5, 6, 7))
        q_t = arena[:, 3:5, :].rearrange("p a (t s) -> p (a t) s", s=SEQ)
        k_t = arena[:, 5:7, :].rearrange("p a (t s) -> p (a t) s", s=SEQ)
        v_tok = arena[:, 7, :].rearrange("p (t d) -> p t d", d=HEADS * VDIM)
        probs = region(8)
        o_t = region(9)
        causal, turn_m = lora[:, 0:P], lora[NOPE:QK, P:P + ROPE]
        CQ, CKV = Q_LORA // P, KV_LORA // P
        Q_HEADS = [6, 6, 4]
        wd_slot = lambda s, w: ring.slot(s)[:, 0:NT * w].rearrange("p (k n) -> p k n", n=w)
        uq_slot = lambda s, w: ring.slot(s)[:, 0:CQ * w].rearrange("p (k n) -> p k n", n=w)

        def mla_down(layer):
            stage("down")
            sq = region(3)
            banks = Banks([(f"c{t}", "act") for t in range(6)])
            pos_i = small[NOPE:QK, 1024:1536].bitcast(I32)
            pos = lora[NOPE:QK, 512:1024]
            turns_f, turns_i, gap = lora[NOPE:QK, 1024:1536], lora[NOPE:QK, 1536:2048].bitcast(I32), lora[NOPE:QK, 2048:2560]
            angle = lora[NOPE:QK, 2560:3072]
            freq = cst[NOPE:QK, CONSTS["cols"][0] + 2:CONSTS["cols"][0] + 3]
            rstd_kv = low[0]
            with nc.Block() as block:
                @block.sync
                def _(sp):
                    bring(sp, pos_i, a["positions"][0].partition_broadcast(ROPE))
                    bring(sp, lora[:, 0:P + ROPE], a["extras"][:, 0:P + ROPE])
                    wuq = a["ml_wuq"][0].rearrange("(k p) n -> p k n", p=P)
                    wukv = a["ml_wukv"][0].rearrange("(k p) n -> p k n", p=P)
                    c = 0
                    for j, nh in enumerate(Q_HEADS):
                        ring.load(sp, uq_slot(3 + j, nh * QK), wuq[:, :, c:c + nh * QK],
                                  pe_s(["", "c1", "c3"][j]) if j else ffn_last_use(layer - 1)(3))
                        c += nh * QK
                    ring.load(sp, rows_slot(2), wukv[:, :, 0:DM], pe_s("c5"))
                loads_all = ins["n"]

                @block.tensor
                def _(pe):
                    norm_pe(pe, "n", sq)
                    for s, tiles in enumerate(([0, 1], [2, 3], [4, 5])):
                        slot_landed(pe, s)
                        w = wd_slot(s, 256 if s < 2 else P + ROPE)
                        for n, t in enumerate(tiles):
                            rows = slice(NOPE, QK) if t == 5 else slice(0, P)
                            for k in range(NT):
                                if t == 0:
                                    pe.wait_ge(*dve_s(f"n out{k}"))
                                mm = pe.matmul(banks.bank(f"c{t}")[rows], w[:, k, n * P:n * P + (rows.stop - rows.start)],
                                               u[:, k, :], start=(k == 0), stop=(k == NT - 1))
                            mm.then_inc(*pe_s.mark(f"c{t}"))
                    ring.uses += 3
                    for t in range(CQ + CKV):
                        pe.wait_ge(*act_s(f"csq{t}"))
                        mm = pe.matmul(psum[:, 6 if t < CQ else 7, :], const("ones"), sq[:, t, :],
                                       start=t in (0, CQ), stop=t in (CQ - 1, CQ + CKV - 1))
                        if t == CQ - 1:
                            mm.then_inc(*pe_s.mark("cq sum"))
                    mm.then_inc(*pe_s.mark("ckv sum"))

                @block.scalar
                def _(act):
                    norm_act(act, "n", h, sq)
                    for t in range(6):
                        rows = slice(NOPE, QK) if t == 5 else slice(0, P)
                        act.wait_ge(*pe_s(f"c{t}"))
                        act.activation(cbuf[rows, t, :], banks.bank(f"c{t}")[rows], ACT.Copy).then_inc(*act_s.mark(f"ev c{t}"))
                    for t in range(CQ + CKV):
                        act.wait_ge(*act_s(f"ev c{t}"))
                        act.activation(sq[:, t, :], cbuf[:, t, :], ACT.Square).then_inc(*act_s.mark(f"csq{t}"))
                    act.wait_ge(*pe_s("cq sum"))
                    act.wait_ge(*dve_s(f"n out{NT - 1}"))
                    act.activation(rstd, psum[:, 6, :], ACT.Sqrt, bias=eps, scale=1.0 / Q_LORA).then_inc(*act_s.mark("cq root"))
                    act.wait_ge(*pe_s("ckv sum"))
                    act.activation(rstd_kv, psum[:, 7, :], ACT.Sqrt, bias=eps,
                                   scale=1.0 / KV_LORA).then_inc(*act_s.mark("ckv root"))
                    act.wait_ge(*dve_s("sin angle"))
                    act.activation(sin_t, angle, ACT.Sin).then_inc(*act_s.mark("sin"))
                    act.wait_ge(*dve_s("cos angle"))
                    act.activation(cos_t, gap, ACT.Sin).then_inc(*act_s.mark("cos"))

                @block.vector
                def _(dve):
                    norm_dve(dve, "n", h, u, lambda t: col("norm_mix", layer * NT + t))
                    steps = [0]

                    def then(op):
                        steps[0] += 1
                        name = f"angle {steps[0]}"
                        op.then_inc(*dve_s.mark(name))
                        dve.wait_ge(*dve_s(name))

                    def wrap(x):
                        then(dve.tensor_scalar(turns_f, x, float(np.pi), -TWO_PI, ALU.is_gt, ALU.mult))
                        then(dve.tensor_tensor(x, x, turns_f, ALU.add))
                        then(dve.tensor_scalar(turns_f, x, -float(np.pi), TWO_PI, ALU.is_lt, ALU.mult))
                        then(dve.tensor_tensor(x, x, turns_f, ALU.add))

                    dve.wait_ge(in_landed, loads_all)
                    then(dve.tensor_copy(pos, pos_i))
                    then(dve.tensor_scalar(angle, pos, freq, None, ALU.mult))
                    then(dve.tensor_scalar(turns_i, angle, 1.0 / TWO_PI, None, ALU.mult))
                    then(dve.tensor_copy(turns_f, turns_i))
                    then(dve.scalar_tensor_tensor(angle, turns_f, -6.28125, angle, ALU.mult, ALU.add))
                    then(dve.scalar_tensor_tensor(angle, turns_f, -(TWO_PI - 6.28125), angle, ALU.mult, ALU.add))
                    wrap(angle)
                    then(dve.tensor_scalar(gap, angle, float(np.pi / 2), None, ALU.add))
                    dve.tensor_scalar(angle, angle, PI_BELOW, -PI_BELOW, ALU.min,
                                      ALU.max).then_inc(*dve_s.mark("sin angle"))
                    wrap(gap)
                    dve.tensor_scalar(gap, gap, PI_BELOW, -PI_BELOW, ALU.min, ALU.max).then_inc(*dve_s.mark("cos angle"))
                    for name, buf, ts, gain in (("cq", rstd, range(CQ), "ml_gq"), ("ckv", rstd_kv, range(CQ, CQ + CKV), "ml_gkv")):
                        dve.wait_ge(*act_s(f"{name} root"))
                        dve.reciprocal(buf, buf).then_inc(*dve_s.mark(f"{name} rstd"))
                        dve.wait_ge(*dve_s(f"{name} rstd"))
                        for t in ts:
                            dve.scalar_tensor_tensor(cbuf[:, t, :], cbuf[:, t, :], col(gain, t - ts[0]), buf,
                                                     ALU.mult, ALU.mult).then_inc(*dve_s.mark(f"latent{t}"))

        def mla_up(layer):
            stage("up")
            jobs = ["rot k"]
            for hd in range(HEADS):
                jobs += [f"q{hd}"] + ([f"rot q{hd - 1}"] if hd else [])
            jobs += [f"rot q{HEADS - 1}"] + [f"k{hd}" for hd in range(HEADS)] + [f"v{j}" for j in range(8)]
            banks = Banks([(j, "dve" if j.startswith("rot") or j[0] == "v" else "act") for j in jobs])
            rot_sin = [lora[NOPE:QK, 512:1024], lora[NOPE:QK, 1024:1536]]
            raw_cos = [lora[NOPE:QK, 1536:2048], lora[NOPE:QK, 2048:2560]]
            with nc.Block() as block:
                @block.sync
                def _(sp):
                    wukv = a["ml_wukv"][0].rearrange("(k p) n -> p k n", p=P)
                    ring.load(sp, rows_slot(3), wukv[:, :, DM:2 * DM], pe_s(f"q{Q_HEADS[0] - 1}"))
                    wv = a["ml_wo"][0].rearrange("(k p) n -> p k n", p=P)
                    last = [f"q{Q_HEADS[0] + Q_HEADS[1] - 1}", f"q{HEADS - 1}", "v6", "v7"]
                    for s in range(SLOTS):
                        ring.load(sp, cols_slot(s), wv[:, :, s * 256:(s + 1) * 256], pe_s(last[s]))

                def rotated(pe, name, rows):
                    if banks.free(f"rot {name}"):
                        pe.wait_ge(*banks.free(f"rot {name}"))
                    pe.matmul(banks.bank(f"rot {name}")[NOPE:QK], turn_m, rows,
                              start=True, stop=True).then_inc(*pe_s.mark(f"rot {name}"))

                @block.tensor
                def _(pe):
                    rotated(pe, "k", kr)
                    hd = 0
                    for j, nh in enumerate(Q_HEADS):
                        slot_landed(pe, j)
                        w = uq_slot(3 + j, nh * QK)
                        for n in range(nh):
                            if banks.free(f"q{hd}"):
                                pe.wait_ge(*banks.free(f"q{hd}"))
                            for k in range(CQ):
                                mm = pe.matmul(banks.bank(f"q{hd}")[0:QK], w[:, k, n * QK:(n + 1) * QK], cbuf[:, k, :],
                                               start=(k == 0), stop=(k == CQ - 1))
                            mm.then_inc(*pe_s.mark(f"q{hd}"))
                            if hd:
                                pe.wait_ge(*act_s(f"ev q{hd - 1}"))
                                rotated(pe, f"q{hd - 1}", q_t[NOPE:QK, hd - 1, :])
                            hd += 1
                    pe.wait_ge(*act_s(f"ev q{HEADS - 1}"))
                    rotated(pe, f"q{HEADS - 1}", q_t[NOPE:QK, HEADS - 1, :])
                    for hd in range(HEADS):
                        if hd % 8 == 0:
                            slot_landed(pe, 3 + hd // 8)
                        w = rows_slot(2 + hd // 8)
                        pe.wait_ge(*banks.free(f"k{hd}"))
                        for k in range(CKV):
                            c = (hd % 8) * (NOPE + VDIM)
                            mm = pe.matmul(banks.bank(f"k{hd}")[0:NOPE], w[:, k, c:c + NOPE], cbuf[:, CQ + k, :],
                                           start=(k == 0), stop=(k == CKV - 1))
                        mm.then_inc(*pe_s.mark(f"k{hd}"))
                    for j in range(8):
                        tok, half = j // 2, j % 2
                        pe.wait_ge(*banks.free(f"v{j}"))
                        for k in range(CKV):
                            w = rows_slot(2 + half)[:, k, :].rearrange("p (h d) -> p h d", d=NOPE + VDIM)[:, :, NOPE:]
                            mm = pe.matmul(banks.bank(f"v{j}"), cbuf[:, CQ + k, tok * P:(tok + 1) * P], w,
                                           start=(k == 0), stop=(k == CKV - 1))
                        mm.then_inc(*pe_s.mark(f"v{j}"))
                ring.uses += 5

                @block.scalar
                def _(act):
                    for hd in range(HEADS):
                        act.wait_ge(*pe_s(f"q{hd}"))
                        act.activation(q_t[0:QK, hd, :], banks.bank(f"q{hd}")[0:QK], ACT.Copy).then_inc(*act_s.mark(f"ev q{hd}"))
                    for hd in range(HEADS):
                        act.wait_ge(*pe_s(f"k{hd}"))
                        act.activation(k_t[0:NOPE, hd, :], banks.bank(f"k{hd}")[0:NOPE],
                                       ACT.Copy).then_inc(*act_s.mark(f"ev k{hd}"))

                @block.gpsimd
                def _(pool):
                    pool.tensor_tensor(raw_cos[1], kr, cos_t, ALU.mult).then_inc(*pool_s.mark("cos k"))
                    for hd in range(HEADS):
                        if hd:
                            pool.wait_ge(*dve_s("roped k" if hd == 1 else f"roped q{hd - 2}"))
                        pool.wait_ge(*act_s(f"ev q{hd}"))
                        pool.tensor_tensor(raw_cos[hd % 2], q_t[NOPE:QK, hd, :], cos_t,
                                           ALU.mult).then_inc(*pool_s.mark(f"cos q{hd}"))
                    pool.wait_ge(*dve_s("roped k"))
                    pool.tensor_copy(k_t[NOPE:QK, :, :], kr.unsqueeze(1).broadcast_to([ROPE, HEADS, SEQ])
                                     ).then_inc(*pool_s.mark("rotary key"))

                @block.vector
                def _(dve):
                    def rope(name, dst, b):
                        dve.wait_ge(*pe_s(f"rot {name}"))
                        dve.tensor_tensor(rot_sin[b], banks.bank(f"rot {name}")[NOPE:QK], sin_t,
                                          ALU.mult).then_inc(*dve_s.mark(f"ev rot {name}"))
                        dve.wait_ge(*dve_s(f"ev rot {name}"))
                        dve.wait_ge(*pool_s(f"cos {name}"))
                        dve.tensor_tensor(dst, raw_cos[b], rot_sin[b], ALU.add).then_inc(*dve_s.mark(f"roped {name}"))

                    rope("k", kr, 1)
                    for hd in range(HEADS):
                        rope(f"q{hd}", q_t[NOPE:QK, hd, :], hd % 2)
                    for j in range(8):
                        dve.wait_ge(*pe_s(f"v{j}"))
                        dve.tensor_copy(v_tok[:, j // 2, (j % 2) * 512:(j % 2 + 1) * 512],
                                        banks.bank(f"v{j}")).then_inc(*dve_s.mark(f"ev v{j}"))

        def mla_attend(layer):
            stage("attend")
            scale = 1.0 / float(np.sqrt(QK))
            NQ = SEQ // P
            blocks = [(kt, qi) for kt in (0, 1, 3, 2) for qi in range(kt, NQ)]
            turned = [lora[:, 256 + 1280 * j:1536 + 1280 * j].rearrange("p (b q) -> p b q", q=P) for j in range(2)]
            q_now = [lora[0:QK, 2816 + 512 * j:3328 + 512 * j] for j in range(2)]
            v_now = [lora[:, 3840 + 256 * j:4096 + 256 * j].rearrange("p (t d) -> p t d", d=VDIM) for j in range(2)]
            top, ntop, total, inv = (small[:, 8 * j:8 * j + 8] for j in range(4))
            with nc.Block() as block:
                @block.gpsimd
                def _(pool):
                    with pool.Fori(0, HEADS // 2) as i:
                        pool_s.start_loop(i)
                        for b in range(2):
                            pool.wait_ge(*pe_s(f"S{b}{NQ - 1}", i - 1))
                            pool.sem_inc(passed_pool, 1)
                            pool.tensor_copy(q_now[b], q_t[0:QK, i * 2 + b, :]).then_inc(*pool_s.mark(f"q{b}"))
                            pool.wait_ge(*pe_s(f"O{b}", i - 1))
                            pool.sem_inc(passed_pool, 1)
                            pool.tensor_copy(v_now[b], v_tok[:, :, bass.ds((i * 2 + b) * VDIM, VDIM)]
                                             ).then_inc(*pool_s.mark(f"v{b}"))
                        pool_s.end_loop(HEADS // 2)

                @block.tensor
                def _(pe):
                    with pe.Fori(0, HEADS // 2) as i:
                        pe_s.start_loop(i)
                        for b in range(2):
                            pe.wait_ge(*pool_s(f"q{b}", i))
                            for qi in range(NQ):
                                pe.wait_ge(*(act_s(f"exp0{qi}", i) if b else act_s(f"exp1{qi}", i - 1)))
                                n = (qi + 1) * P
                                pe.matmul(psum[:, qi, 0:n], q_now[b][:, qi * P:n], k_t[0:QK, i * 2 + b, 0:n],
                                          start=True, stop=True).then_inc(*pe_s.mark(f"S{b}{qi}"))
                        for b in range(2):
                            pe.wait_ge(*dve_s(f"p{b}{NQ - 1}", i))
                            if b:
                                pe.wait_ge(*act_s("turned02", i))
                            else:
                                pe.wait_ge(*act_s("turned12", i - 1))
                            pe.wait_ge(*dve_s("turned01", i) if b else dve_s("turned11", i - 1))
                            for j, (kt, qi) in enumerate(blocks):
                                mm = pe.transpose(psum[:, 4 + j // 4, (j % 4) * P:(j % 4 + 1) * P],
                                                  probs[:, 4 * b + qi, kt * P:(kt + 1) * P], const("ident"))
                                if j in (3, 7, 9):
                                    mm.then_inc(*pe_s.mark(f"T{b}{j // 4}"))
                            if b == 0:
                                pe.wait_ge(*act_s("O", i - 1))
                            pe.wait_ge(*pool_s(f"v{b}", i))
                            pe.wait_ge(*act_s(f"turned{b}2", i))
                            pe.wait_ge(*dve_s(f"turned{b}1", i))
                            for kt in range(NQ):
                                at = blocks.index((kt, kt))
                                mm = pe.matmul(psum[b * VDIM:(b + 1) * VDIM, 7, kt * P:SEQ], v_now[b][:, kt, :],
                                               turned[b][:, at:at + NQ - kt, :], start=(kt == 0), stop=(kt == NQ - 1))
                            mm.then_inc(*pe_s.mark(f"O{b}"))
                        pe_s.end_loop(HEADS // 2)

                @block.vector
                def _(dve):
                    with dve.Fori(0, HEADS // 2) as i:
                        dve_s.start_loop(i)
                        for b in range(2):
                            for qi in range(NQ):
                                j = 4 * b + qi
                                dve.wait_ge(*pe_s(f"S{b}{qi}", i))
                                dve.tensor_tensor(psum[:, qi, qi * P:(qi + 1) * P], psum[:, qi, qi * P:(qi + 1) * P],
                                                  causal, ALU.add).then_inc(*dve_s.mark(f"mask{j}"))
                                dve.wait_ge(*dve_s(f"mask{j}", i))
                                dve.reduce_max(top[:, j:j + 1], psum[:, qi, 0:(qi + 1) * P], AX_X
                                               ).then_inc(*dve_s.mark(f"max{j}"))
                                dve.wait_ge(*dve_s(f"max{j}", i))
                                dve.tensor_scalar(ntop[:, j:j + 1], top[:, j:j + 1], -scale, None,
                                                  ALU.mult).then_inc(*dve_s.mark(f"top{b}{qi}"))
                        for b in range(2):
                            for qi in range(NQ):
                                j = 4 * b + qi
                                dve.wait_ge(*act_s(f"exp{b}{qi}", i))
                                dve.reciprocal(inv[:, j:j + 1], total[:, j:j + 1]).then_inc(*dve_s.mark(f"inv{j}"))
                                dve.wait_ge(*dve_s(f"inv{j}", i))
                                dve.tensor_scalar(probs[:, j, 0:(qi + 1) * P], probs[:, j, 0:(qi + 1) * P],
                                                  inv[:, j:j + 1], None, ALU.mult).then_inc(*dve_s.mark(f"p{b}{qi}"))
                        for b in range(2):
                            dve.wait_ge(*pe_s(f"T{b}1", i))
                            dve.wait_ge(*pe_s(f"O{b}", i - 1))
                            dve.tensor_copy(turned[b][:, 4:8, :], psum[:, 5, :].rearrange("p (b q) -> p b q", q=P)
                                            ).then_inc(*dve_s.mark(f"turned{b}1"))
                        dve_s.end_loop(HEADS // 2)

                @block.scalar
                def _(act):
                    with act.Fori(0, HEADS // 2) as i:
                        act_s.start_loop(i)
                        for b in range(2):
                            for qi in range(NQ):
                                j = 4 * b + qi
                                act.wait_ge(*dve_s(f"top{b}{qi}", i))
                                act.wait_ge(*pe_s(f"T{b}2", i - 1))
                                act.activation(probs[:, j, 0:(qi + 1) * P], psum[:, qi, 0:(qi + 1) * P], ACT.Exp,
                                               bias=ntop[:, j:j + 1], scale=scale,
                                               accum_out=total[:, j:j + 1]).then_inc(*act_s.mark(f"exp{b}{qi}"))
                        for b in range(2):
                            for part, lo, hi in ((0, 0, 4), (2, 8, 10)):
                                act.wait_ge(*pe_s(f"T{b}{part}", i))
                                act.activation(turned[b][:, lo:hi, :],
                                               psum[:, 4 + part, 0:(hi - lo) * P].rearrange("p (b q) -> p b q", q=P),
                                               ACT.Copy).then_inc(*act_s.mark(f"turned{b}{part}"))
                        act.wait_ge(*pe_s("O1", i))
                        act.activation(o_t[:, i, :], psum[:, 7, :], ACT.Copy).then_inc(*act_s.mark("O"))
                        act_s.end_loop(HEADS // 2)

        def mla_finish(layer):
            stage("mlaout")
            banks = Banks([(f"o{t}", "dve") for t in range(NT)])
            with nc.Block() as block:
                @block.sync
                def _(sp):
                    ffn_head(sp, layer, lambda s: pe_s(f"o{2 * s + 1}"))

                @block.tensor
                def _(pe):
                    proj_pe(pe, "o", banks, o_t, lambda k: act_s("O", HEADS // 2 - 1, "attend"))

                @block.vector
                def _(dve):
                    for t in range(NT):
                        dve.wait_ge(*pe_s(f"o{t}"))
                        dve.tensor_tensor(h[:, t, :], h[:, t, :], banks.bank(f"o{t}"),
                                          ALU.add).then_inc(*dve_s.mark(f"ev o{t}"))

        v_stored = sem("v_first_stored")

        def first_loads(sp):
            load_proj(sp, a["rw_wr"][0], lambda s: None)

        def conv_head(sp, last_use):
            w1 = a["cv_w1"][0].rearrange("(k p) n -> p k n", p=P)
            for s in range(SLOTS):
                c = (s // 2) * 256 + (s % 2) * DM
                ring.load(sp, cols_slot(s), w1[:, :, c:c + 256], last_use(s))

        def mla_head(sp, last_use):
            wd = a["ml_wd"][0].rearrange("(k p) n -> p k n", p=P)
            for s, w in enumerate((256, 256, P + ROPE)):
                ring.load(sp, wd_slot(s, w), wd[:, :, s * 256:s * 256 + w], last_use(s))

        last = lambda layer: ffn_last_use(layer)
        begin()
        rwkv_project(0, 0)
        rwkv_scan(0)
        rwkv_finish(0, 0)
        ffn(0, lambda sp: conv_head(sp, last(0)))
        conv_glu(1)
        conv_taps()
        conv_finish(1)
        ffn(1, lambda sp: mla_head(sp, last(1)))
        mla_down(2)
        mla_up(2)
        mla_attend(2)
        mla_finish(2)
        ffn(2, lambda sp: load_proj(sp, a["rw_wr"][1], last(2)))
        rwkv_project(3, 1)
        rwkv_scan(1)
        rwkv_finish(3, 1)
        ffn(3, lambda sp: None)
        end()
        for n, s in everyone.items():
            new[n] = s.new
    return new


IN_NAMES = ["x", "consts", "extras"] + [n for g in VECTORS for n, _ in g] + [
    "positions", "cv_dw", "cv_w1", "cv_w2", "ml_wd", "ml_wuq", "ml_wukv", "ml_wo",
    "rw_wr", "rw_wk", "rw_wv", "rw_wo", "rw_w1", "rw_w2", "rw_a1", "rw_a2", "rw_g1", "rw_g2", "rw_v1", "rw_v2", "ff_w1", "ff_w2"]

def kernel(**inputs):
    import numpy as _np
    import concourse.bacc as _bacc
    from concourse.bass_utils import run_bass_kernel_spmd as _run

    known = {}
    for _pass in range(2):
        nc = _bacc.Bacc("TRN2", target_bir_lowering=False, num_devices=1, dynamic_dma_scratch_size=1024)
        arrays, args = {}, {}
        consts, extras = constants()
        given = dict(inputs, consts=consts, extras=extras)
        for name in IN_NAMES:
            arr = _np.ascontiguousarray(given[name])
            arrays[f"in_{name}"] = arr
            args[name] = nc.dram_tensor(f"in_{name}", arr.shape, mybir.dt.from_np(arr.dtype), kind="ExternalInput").ap()
        args["out"] = nc.dram_tensor("out_0", (1, SEQ, DM), F32, kind="ExternalOutput").ap()
        args["v_first"] = nc.dram_tensor("v_first", (P, NT * SEQ), F32, kind="Internal").ap()
        known = build(nc, args, known)
    r = _run(nc, [arrays], core_ids=[0])
    return r.results[0]["out_0"]
```

```python
from contextlib import ExitStack

import numpy as np

import concourse.bass as bass
from concourse import mybir

F32 = mybir.dt.float32
F32R = mybir.dt.float32r
I32 = mybir.dt.int32
ALU = mybir.AluOpType
ACT = mybir.ActivationFunctionType
AX_X = mybir.AxisListType.X

P = 128
SEQ, DM, DEPTH = 512, 1024, 4
NT = DM // P
HEAD = 64
CH = 64
NCH = SEQ // CH
LORA_W, LORA_A, LORA_V, LORA_G = 64, 64, 32, 128
TAPS = 31
PAD = TAPS - 1
D_FF = 4 * DM
FT = D_FF // P
HEADS, NOPE, ROPE, VDIM = 16, 64, 32, 64
QK = NOPE + ROPE
Q_LORA, KV_LORA = 384, 256
NORM_EPS, GN_EPS = 1e-5, 64e-5
DECAY = float(np.exp(-0.5))
TWO_PI = 2.0 * np.pi
PI_BELOW = float(np.nextafter(np.float32(np.pi), np.float32(0)))
TURNS = D_FF // DM
PE_TAPS, ACT_TAPS = 11, 9

SLOTS = 4
SLOT = 2048

VECTORS = [
    [("rw_mu", 96), ("norm_mix", 32)],
    [("norm_ffn", 32), ("norm_final", 8), ("rw_w0", 16), ("rw_a0", 16), ("rw_kk", 16), ("rw_ka", 16),
     ("rw_rk", 16), ("rw_v0", 8)],
    [("rw_lnx_w", 16), ("rw_lnx_b", 16), ("cv_b1", 16), ("cv_bdw", 8), ("cv_ln_w", 8), ("cv_ln_b", 8),
     ("cv_b2", 8), ("ml_gq", 3), ("ml_gkv", 2)],
]
VEC_ROW = {}
for _g, _names in enumerate(VECTORS):
    _r = 0
    for _n, _k in _names:
        VEC_ROW[_n] = (_g, _r, _k)
        _r += _k

CONSTS = {}
_at = 0
for _n, _w in [("ident", P), ("ones", P), ("pair", P), ("mask_g", P), ("mask_d", CH), ("mask_dt", CH),
               ("mask_et", CH), ("eye2", CH), ("cols", 8), ("pick", 30)]:
    CONSTS[_n] = (_at, _w)
    _at += _w
CONST_W = _at


def constants():
    c = np.zeros((P, CONST_W), np.float32)

    def put(name, a):
        at, w = CONSTS[name]
        c[: a.shape[0], at:at + w] = a

    p, f = np.arange(P)[:, None], np.arange(P)[None, :]
    put("ident", np.eye(P))
    put("ones", np.ones((P, P)))
    put("pair", (p // HEAD == f // HEAD) * 1.0)
    j, i = p % CH, f % CH
    put("mask_g", np.where(f < CH, (p >= CH) & (j < i), j <= i) * 1.0)
    i2, j2 = np.arange(P)[:, None] % CH, np.arange(CH)[None, :]
    put("mask_d", ((j2 < i2) & (j2 // 16 == i2 // 16)) * 1.0)
    put("mask_dt", ((i2 < j2) & (j2 // 16 == i2 // 16)) * 1.0)
    put("mask_et", (i2 // 16 < j2 // 16) * 1.0)
    put("eye2", (i2 == j2) * 1.0)
    put("pick", (np.arange(30)[None, :] - 14 == p // HEAD) * 1.0)
    t = np.zeros((P, ROPE))
    for k in range(ROPE // 2):
        t[NOPE + ROPE // 2 + k, k] = -1.0
        t[NOPE + k, ROPE // 2 + k] = 1.0
    cols = np.zeros((P, 8))
    cols[:, 0] = NORM_EPS
    cols[:, 1] = GN_EPS
    freq = np.float32(10000.0) ** (-np.arange(0, ROPE, 2, dtype=np.float32) / np.float32(ROPE))
    cols[NOPE:NOPE + ROPE, 2] = np.tile(freq, 2)
    cols[:, 3] = np.pi / 2
    put("cols", cols)
    reset = np.ones((P, SEQ), np.float32)
    reset[:, ::CH] = 0.0
    spread = np.zeros((P, DM))
    spread[0:HEADS] = np.arange(DM)[None, :] // HEAD == np.arange(HEADS)[:, None]
    return c, np.concatenate([np.where(f <= p, 0.0, -1e30), t, reset, spread], axis=1).astype(np.float32)


class Steps:

    def __init__(self, sem, known):
        self.sem, self.known, self.new = sem, known, {}
        self.count, self.loop_base, self.reg, self.per, self.stage = 0, None, None, 0, ""

    def mark(self, name):
        self.count += 1
        key = (self.stage, name)
        assert key not in self.new, key
        self.new[key] = (self.count, self.loop_base)
        return self.sem, 1

    def start_loop(self, reg):
        self.loop_base, self.reg = self.count, reg

    def end_loop(self, n):
        per = self.count - self.loop_base
        self.new[("per", self.loop_base)] = (per, None)
        self.count += per * (n - 1)
        self.loop_base = self.reg = None

    def at(self, name, i=None, stage=None):
        value, base = self.known.get((stage or self.stage, name), (None, None))
        if value is None:
            assert not self.known, (stage or self.stage, name)
            return 1
        if base is None or i is None:
            return value
        return i * self.known[("per", base)][0] + value

    def __call__(self, name, i=None, stage=None):
        return self.sem, self.at(name, i, stage)


class Ring:

    def __init__(self, buf, landed):
        self.buf, self.landed = buf, landed
        self.loads = self.uses = 0

    def slot(self, s):
        return self.buf[:, s % SLOTS, :]

    def load(self, sp, view, src, last_use):
        if last_use:
            sp.wait_ge(*last_use)
        sp.dma_start(view, src).then_inc(self.landed[self.loads % SLOTS], 16)
        self.loads += 1


class Split:

    def __init__(self, hi, lo, hi_made, lo_made, ring):
        self.bufs, self.hi_made, self.lo_made, self.ring = (hi, lo), hi_made, lo_made, ring
        self.done = 0

    def make_hi(self, act, g, i=0, per=0):
        r = self.ring
        act.wait_ge(r.landed[(r.uses + g) % SLOTS], 16 * (i * (per // SLOTS) + (r.uses + g) // SLOTS + 1))
        act.activation(self.bufs[0][:, g % 2, :], r.slot(r.uses + g), ACT.Copy).then_inc(self.hi_made, 1)

    def make_lo(self, dve, g, i=0, per=0):
        dve.wait_ge(self.hi_made, i * per + (self.done + g + 1))
        hi, lo = (b[:, g % 2, :] for b in self.bufs)
        dve.tensor_tensor(lo, self.ring.slot(self.ring.uses + g), hi.bitcast(F32),
                          ALU.subtract).then_inc(self.lo_made, 1)

    def made(self, g, i=0, per=0):
        return self.lo_made, i * per + (self.done + g + 1)

    def three(self, pe, out, g, view, cols, x, start, stop):
        (wh, wl), (xh, xl) = (view(b[:, g % 2, :])[cols] for b in self.bufs), x
        pe.matmul(out, wh, xh, start=start, stop=False, skip_group_check=True)
        pe.matmul(out, wh, xl, start=False, stop=False, skip_group_check=True)
        return pe.matmul(out, wl, xh, start=False, stop=stop, skip_group_check=True)


def build(nc, a, known):
    ctx = ExitStack()
    new = {}
    with ctx:
        def sb(name, shape, dt=F32):
            return ctx.enter_context(nc.sbuf_tensor(name, shape, dt))

        def sem(name):
            return ctx.enter_context(nc.semaphore(name))

        arena_at = -(-nc.sbuf_base // 32) * 32
        arena = sb("arena", [P, 10, NT * SEQ])
        ring_buf = sb("ring", [P, SLOTS, SLOT])
        lora_at = -(-nc.sbuf_base // 32) * 32
        lora = sb("lora", [P, 5120])
        small = sb("small", [P, 1536])
        vec = sb("vec", [P, 3 * P])
        cst = sb("cst", [P, CONST_W])
        one_less_mu = sb("one_less_mu", [P, 6 * NT])
        one_less_ka = vec[:, 3 * P - NT:3 * P]
        psum = ctx.enter_context(nc.psum_tensor("psum", [P, 8, 512], F32))

        def region(k):
            return arena[:, k, :].rearrange("p (t s) -> p t s", s=SEQ)

        def const(name, rows=P):
            at, w = CONSTS[name]
            return cst[0:rows, at:at + w]

        def col(name, j):
            g, r, _ = VEC_ROW[name]
            return vec[:, g * P + r + j:g * P + r + j + 1]

        eps = cst[:, CONSTS["cols"][0]:CONSTS["cols"][0] + 1]
        gn_eps = cst[:, CONSTS["cols"][0] + 1:CONSTS["cols"][0] + 2]
        def placed(name, k, shape):
            return nc.alloc_sbuf_tensor_at(name, shape, F32R, offset=arena_at + k * NT * SEQ * 4)

        x_parts = tuple(placed(f"x_{e}", k, [P, NT, SEQ])[:] for e, k in (("hi", 3), ("lo", 4)))
        hid_parts = tuple(placed(f"hid_{e}", k, [P, NT, SEQ])[:] for e, k in (("hi", 1), ("lo", 2)))
        xk_parts = (placed("xk_hi", 7, [P, NT, SEQ])[:],
                    nc.alloc_sbuf_tensor_at("xk_lo", [P, NT, SEQ], F32R, offset=lora_at)[:])

        def tiles_at_slots(name, k):
            return placed(name, k, [P, 2, SLOT])[:]

        rstd = small[:, 0:512]
        low = [small[:, 512:1024], small[:, 1024:1536]]

        pe_s = Steps(sem("pe_steps"), known.get("pe", {}))
        act_s = Steps(sem("act_steps"), known.get("act", {}))
        dve_s = Steps(sem("dve_steps"), known.get("dve", {}))
        pool_s = Steps(sem("pool_steps"), known.get("pool", {}))
        everyone = {"pe": pe_s, "act": act_s, "dve": dve_s, "pool": pool_s}

        landed = [sem(f"weights_landed{s}") for s in range(SLOTS)]
        ring = Ring(ring_buf, landed)
        in_landed = sem("inputs_landed")
        out_landed = sem("outputs_landed")
        ins = {"n": 0}

        h, u = region(0), region(1)
        split = Split(tiles_at_slots("w_hi", 8), tiles_at_slots("w_lo", 9), sem("weights_hi"), sem("weights_lo"), ring)

        def stage(name):
            for s in everyone.values():
                s.stage = name

        passed_pe, passed_pool = sem("passed_pe"), sem("passed_pool")

        class Banks:

            def __init__(self, jobs):
                self.names = [n for n, _ in jobs]
                self.who = dict(jobs)

            def bank(self, name):
                return psum[:, self.names.index(name) % 8, :]

            def free(self, name):
                k = self.names.index(name) - 8
                if k < 0:
                    return None
                before = self.names[k]
                return (act_s if self.who[before] == "act" else dve_s)("ev " + before)

        def bring(eng, dst, src):
            eng.dma_start(dst, src).then_inc(in_landed, 16)
            ins["n"] += 16

        groups = {}

        def bring_group(eng, group, dst, src):
            if group not in groups:
                groups[group] = [sem(f"{group}_landed"), 0]
            groups[group][1] += 16
            eng.dma_start(dst, src).then_inc(groups[group][0], 16)

        def landed_group(group):
            return tuple(groups[group])

        def norm_act(act, tag, src, sq, scale=1.0 / DM, tiles=NT, meanwhile=None):
            for t in range(tiles):
                act.activation(sq[:, t, :], src[:, t, :], ACT.Square).then_inc(*act_s.mark(f"{tag} sq{t}"))
            if meanwhile:
                meanwhile()
            act.wait_ge(*pe_s(f"{tag} sum"))
            act.activation(rstd, psum[:, 7, :], ACT.Sqrt, bias=eps, scale=scale).then_inc(*act_s.mark(f"{tag} root"))

        def norm_pe(pe, tag, sq, tiles=NT):
            for t in range(tiles):
                pe.wait_ge(*act_s(f"{tag} sq{t}"))
                mm = pe.matmul(psum[:, 7, :], const("ones"), sq[:, t, :], start=(t == 0), stop=(t == tiles - 1))
            mm.then_inc(*pe_s.mark(f"{tag} sum"))

        def norm_dve(dve, tag, src, dst, gain, tiles=NT):
            dve.wait_ge(*act_s(f"{tag} root"))
            dve.reciprocal(rstd, rstd).then_inc(*dve_s.mark(f"{tag} rstd"))
            dve.wait_ge(*dve_s(f"{tag} rstd"))
            for t in range(tiles):
                dve.scalar_tensor_tensor(dst[:, t, :], src[:, t, :], gain(t), rstd, ALU.mult,
                                         ALU.mult).then_inc(*dve_s.mark(f"{tag} out{t}"))

        def fold_act(act, gain, sq):
            for t in range(NT):
                act.activation(x_parts[0][:, t, :], h[:, t, :], ACT.Copy, scale=gain(t)).then_inc(*act_s.mark(f"x{t}"))
                act.activation(sq[:, t, :], h[:, t, :], ACT.Square).then_inc(*act_s.mark(f"sq{t}"))

        def fold_root(act):
            act.wait_ge(*pe_s("sum"))
            act.activation(rstd, psum[:, 7, :], ACT.Sqrt, bias=eps, scale=1.0 / DM).then_inc(*act_s.mark("root"))

        def fold_dve(dve, gain):
            for t in range(NT):
                dve.wait_ge(*act_s(f"x{t}"))
                dve.scalar_tensor_tensor(x_parts[1][:, t, :], h[:, t, :], gain(t), x_parts[0][:, t, :].bitcast(F32),
                                         ALU.mult, ALU.subtract).then_inc(*dve_s.mark(f"x{t}"))
                if t == 0:
                    split.make_lo(dve, 0)

        def fold_rstd(dve):
            dve.wait_ge(*act_s("root"))
            dve.reciprocal(rstd, rstd).then_inc(*dve_s.mark("rstd"))
            dve.wait_ge(*dve_s("rstd"))

        def fold_pool(pool, sq, total):
            for t in range(1, NT):
                pool.wait_ge(*act_s(f"sq{t}"))
                if t > 1:
                    pool.wait_ge(*pool_s(f"total{t - 1}"))
                pool.tensor_tensor(total, sq[:, 0, :] if t == 1 else total, sq[:, t, :],
                                   ALU.add).then_inc(*pool_s.mark(f"total{t}"))

        def fold_pe(pe, total):
            pe.wait_ge(*pool_s(f"total{NT - 1}"))
            pe.matmul(psum[:, 7, :], const("ones"), total, start=True, stop=True).then_inc(*pe_s.mark("sum"))

        def cols_slot(s):
            return ring.slot(s).rearrange("p (k n) -> p k n", n=256)

        def by_cols(x):
            return x.rearrange("p (k n) -> p k n", n=256)

        def by_rows(x):
            return x.rearrange("p (k n) -> p k n", n=DM)

        def rows_slot(s):
            return ring.slot(s).rearrange("p (k n) -> p k n", n=DM)

        def load_proj(sp, w, last_use):
            wv = w.rearrange("(k p) n -> p k n", p=P)
            for s in range(SLOTS):
                ring.load(sp, cols_slot(s), wv[:, :, s * 256:(s + 1) * 256], last_use(s))

        def ffn_head(sp, layer, last_use):
            load_proj(sp, a["ff_w1"][layer][:, 0:SLOTS * 256], last_use)

        def ffn_body(sp, layer):
            w1 = a["ff_w1"][layer].rearrange("(k p) n -> p k n", p=P)
            w2 = a["ff_w2"][layer].rearrange("(c k p) n -> p c k n", p=P, k=2)
            with sp.Fori(0, TURNS - 1) as i:
                for s in range(SLOTS):
                    ring.load(sp, rows_slot(s), w2[:, i * SLOTS + s, :, :], split.made(s, i, 2 * SLOTS))
                for s in range(SLOTS):
                    ring.load(sp, cols_slot(s), w1[:, :, bass.ds((i * SLOTS + (SLOTS + s)) * 256, 256)],
                              split.made(SLOTS + s, i, 2 * SLOTS))
            for s in range(SLOTS):
                ring.load(sp, rows_slot(s), w2[:, (TURNS - 1) * SLOTS + s, :, :],
                          split.made(2 * SLOTS * (TURNS - 1) + s))
            ring.loads += 2 * SLOTS * (TURNS - 2)

        def ffn_last_use(layer):
            return lambda s: split.made(2 * SLOTS * (TURNS - 1) + SLOTS + s)

        def slot_landed(pe, s, i=0):
            pe.wait_ge(landed[(ring.uses + s) % SLOTS], 16 * (i + (ring.uses + s) // SLOTS + 1))


        def begin():
            stage("begin")
            x_in = arena[:, 2, :].rearrange("p (t d) -> p t d", d=DM)
            rows = arena[:, 3, 0:3 * P].rearrange("p (g c) -> p g c", c=P)
            with nc.Block() as block:
                @block.sync
                def _(sp):
                    bring(sp, cst[:], a["consts"])
                    bring(sp, x_in, a["x"][0].rearrange("(t p) d -> p t d", p=P))
                    for name, (g, r, k) in VEC_ROW.items():
                        src = a[name]
                        pat = {1: "(r c) -> r c", 2: "l (r c) -> (l r) c", 3: "l m (r c) -> (l m r) c"}[len(src.shape)]
                        if name == "rw_rk":
                            src, pat = src.rearrange("l h n -> l (h n)"), "l (r c) -> (l r) c"
                        bring(sp, rows[r:r + k, g, :], src.rearrange(pat, c=P))
                    first_loads(sp)

                @block.gpsimd
                def _(pool):
                    pool.memset(lora[:], 0.0).then_inc(*pool_s.mark("clear"))

                @block.tensor
                def _(pe):
                    pe.wait_ge(in_landed, ins["n"])
                    for g, names in enumerate(VECTORS):
                        r = sum(k for _, k in names)
                        mm = pe.transpose(psum[:, 7, g * P:g * P + r], rows[0:r, g, :], cst[0:r, 0:r])
                    mm.then_inc(*pe_s.mark("vectors"))
                    for t in range(NT):
                        if t == 7:
                            pe.wait_ge(*act_s("vectors"))
                        for q in range(SEQ // P):
                            mm = pe.transpose(psum[:, t, q * P:(q + 1) * P], x_in[:, q, t * P:(t + 1) * P], const("ident"))
                        mm.then_inc(*pe_s.mark(f"x{t}"))

                @block.scalar
                def _(act):
                    act.wait_ge(*pe_s("vectors"))
                    for g, names in enumerate(VECTORS):
                        r = sum(k for _, k in names)
                        op = act.activation(vec[:, g * P:g * P + r], psum[:, 7, g * P:g * P + r], ACT.Copy)
                    op.then_inc(*act_s.mark("vectors"))
                    for t in range(0, NT, 2):
                        act.wait_ge(*pe_s(f"x{t}"))
                        act.activation(h[:, t, :], psum[:, t, :], ACT.Copy).then_inc(*act_s.mark(f"ev x{t}"))

                @block.vector
                def _(dve):
                    for t in range(1, NT, 2):
                        dve.wait_ge(*pe_s(f"x{t}"))
                        dve.tensor_copy(h[:, t, :], psum[:, t, :]).then_inc(*dve_s.mark(f"ev x{t}"))

        def ffn(layer, next_loads):
            stage(f"ffn{layer}")
            sq, total, scaled, square = region(5), region(6)[:, 0, :], region(6)[:, 2:4, :], region(7)
            per = 2 * SLOTS
            hh, hl = hid_parts
            gain = lambda t: col("norm_ffn", layer * NT + t)
            part = lambda x, k: (x[0][:, k, :], x[1][:, k, :])

            with nc.Block() as block:
                @block.sync
                def _(sp):
                    ffn_body(sp, layer)
                    next_loads(sp)

                @block.gpsimd
                def _(pool):
                    fold_pool(pool, sq, total)

                @block.tensor
                def _(pe):
                    def up(pre, g0, i, now):
                        for s in range(SLOTS):
                            pe.wait_ge(*split.made(g0 + s, i, per))
                            order = [(n, k) for n in range(2) for k in range(NT)]
                            if pre and s == 0:
                                order = [(n, k) for k in range(NT) for n in range(2)]
                            for n, k in order:
                                b = 2 * s + n
                                if pre and s == 0 and n == 0:
                                    pe.wait_ge(*dve_s(f"x{k}"))
                                if pre and b == 7 and k == 0:
                                    pe.wait_ge(*act_s("root"))
                                if not pre and k == 0:
                                    pe.wait_ge(*dve_s(f"add{b}", now))
                                mm = split.three(pe, psum[:, b, :], g0 + s, by_cols,
                                                 np.s_[:, k, n * P:(n + 1) * P], part(x_parts, k), k == 0, k == NT - 1)
                                if k == NT - 1:
                                    mm.then_inc(*pe_s.mark(f"{pre}up{b}"))
                            if pre and s == 0:
                                fold_pe(pe, total)

                    def down(pre, g0, i, before):
                        for s in range(SLOTS):
                            pe.wait_ge(*split.made(g0 + s, i, per))
                            for k in range(2):
                                pe.wait_ge(*dve_s(f"hid{2 * s + k}", before))
                                for n in range(NT):
                                    if s == 0 and k == 0:
                                        pe.wait_ge(*dve_s(f"scaled{n}", before))
                                    last = s == SLOTS - 1 and k == 1
                                    mm = split.three(pe, psum[:, n, :], g0 + s, by_rows,
                                                     np.s_[:, k, n * P:(n + 1) * P], part(hid_parts, 2 * s + k),
                                                     s == 0 and k == 0, last)
                                    if last:
                                        mm.then_inc(*pe_s.mark(f"{pre}out{n}"))
                            if s < SLOTS - 1:
                                mm.then_inc(*pe_s.mark(f"{pre}down{s}"))

                    up("first ", 0, 0, None)
                    with pe.Fori(0, TURNS - 1) as i:
                        pe_s.start_loop(i)
                        down("", SLOTS, i, i - 1)
                        up("", per, i, i)
                        pe_s.end_loop(TURNS - 1)
                    down("last ", SLOTS + per * (TURNS - 1), 0, TURNS - 2)

                @block.scalar
                def _(act):
                    def up(pre, g0, i, now):
                        for s in range(SLOTS):
                            if not (pre and s == 1):
                                if s == 0 and not pre:
                                    act.wait_ge(*pe_s("out7", now))
                                elif s:
                                    act.wait_ge(*pe_s(f"{pre}up{2 * s - 1}", now))
                                split.make_hi(act, g0 + s + 1, i, per)
                            if pre and s == 0:
                                act.wait_ge(*pe_s(f"{pre}up1"))
                                split.make_hi(act, g0 + 2)
                                fold_root(act)
                            for b in (2 * s, 2 * s + 1):
                                act.wait_ge(*dve_s(f"{pre}square{b}", now))
                                act.activation(hh[:, b, :], square[:, b, :],
                                               ACT.Copy).then_inc(*act_s.mark(f"{pre}hid{b}"))

                    def down(pre, g0, i, before):
                        for s in range(SLOTS - (pre == "last ")):
                            act.wait_ge(*(pe_s(f"{pre}down{s - 1}", None if pre else i) if s else pe_s("up7", before)))
                            split.make_hi(act, g0 + s + 1, i, per)

                    split.make_hi(act, 0)
                    fold_act(act, gain, sq)
                    up("first ", 0, 0, None)
                    with act.Fori(0, TURNS - 1) as i:
                        act_s.start_loop(i)
                        down("", SLOTS, i, i - 1)
                        up("", per, i, i)
                        act_s.end_loop(TURNS - 1)
                    down("last ", SLOTS + per * (TURNS - 1), 0, TURNS - 2)

                @block.vector
                def _(dve):
                    def rest(pre, b, now):
                        dve.wait_ge(*act_s(f"{pre}hid{b}", now))
                        dve.tensor_tensor(hl[:, b, :], square[:, b, :], hh[:, b, :].bitcast(F32),
                                          ALU.subtract).then_inc(*dve_s.mark(f"{pre}hid{b}"))

                    def up(pre, g0, i, now):
                        for s in range(SLOTS):
                            if not (pre and s == 1):
                                split.make_lo(dve, g0 + s + 1, i, per)
                            if pre and s == 0:
                                split.make_lo(dve, g0 + 2)
                                fold_rstd(dve)
                            for b in (2 * s, 2 * s + 1):
                                dve.wait_ge(*pe_s(f"{pre}up{b}", now))
                                dve.tensor_tensor(scaled[:, b % 2, :], psum[:, b, :], rstd,
                                                  ALU.mult).then_inc(*dve_s.mark(f"{pre}scaled{b}"))
                                dve.wait_ge(*dve_s(f"{pre}scaled{b}", now))
                                dve.scalar_tensor_tensor(square[:, b, :], scaled[:, b % 2, :], 0.0, scaled[:, b % 2, :],
                                                         ALU.max, ALU.mult).then_inc(*dve_s.mark(f"{pre}square{b}"))
                                if b:
                                    rest(pre, b - 1, now)
                        rest(pre, 7, now)

                    def down(pre, g0, i, now):
                        for s in range(SLOTS - (pre == "last ")):
                            split.make_lo(dve, g0 + s + 1, i, per)
                        for n in range(NT):
                            dve.wait_ge(*pe_s(f"{pre}out{n}", now))
                            dve.tensor_tensor(h[:, n, :], h[:, n, :], psum[:, n, :],
                                              ALU.add).then_inc(*dve_s.mark(f"{pre}add{n}"))

                    fold_dve(dve, gain)
                    up("first ", 0, 0, None)
                    with dve.Fori(0, TURNS - 1) as i:
                        dve_s.start_loop(i)
                        down("", SLOTS, i, i)
                        up("", per, i, i)
                        dve_s.end_loop(TURNS - 1)
                    down("last ", SLOTS + per * (TURNS - 1), 0, None)
            ring.uses += per * TURNS
            split.done += per * TURNS

        def end():
            stage("end")
            sq = region(6)
            out_sb = arena[:, 2, :].rearrange("p (t d) -> p t d", d=DM)
            with nc.Block() as block:
                @block.tensor
                def _(pe):
                    norm_pe(pe, "n", sq)
                    for q in range(SEQ // P):
                        for half in range(2):
                            j = 2 * q + half
                            if j == 7:
                                pe.wait_ge(*act_s("n root"))
                            for t in range(4):
                                pe.wait_ge(*dve_s(f"n out{4 * half + t}"))
                                mm = pe.transpose(psum[:, j, t * P:(t + 1) * P],
                                                  u[:, 4 * half + t, q * P:(q + 1) * P], const("ident"))
                            mm.then_inc(*pe_s.mark(f"y{j}"))

                @block.scalar
                def _(act):
                    norm_act(act, "n", h, sq)
                    for j in range(0, 8, 2):
                        act.wait_ge(*pe_s(f"y{j}"))
                        act.activation(out_sb[:, j // 2, 0:512], psum[:, j, :], ACT.Copy).then_inc(*act_s.mark(f"y{j}"))

                @block.vector
                def _(dve):
                    norm_dve(dve, "n", h, u, lambda t: col("norm_final", t))
                    for j in range(1, 8, 2):
                        dve.wait_ge(*pe_s(f"y{j}"))
                        dve.tensor_copy(out_sb[:, j // 2, 512:1024], psum[:, j, :]).then_inc(*dve_s.mark(f"y{j}"))

                @block.sync
                def _(sp):
                    for q in range(SEQ // P):
                        sp.wait_ge(*act_s(f"y{2 * q}"))
                        sp.wait_ge(*dve_s(f"y{2 * q + 1}"))
                        sp.dma_start(a["out"][0, q * P:(q + 1) * P, :], out_sb[:, q, :]).then_inc(out_landed, 16)
                    sp.wait_ge(out_landed, 16 * (SEQ // P))

        def gemm(pe, tag, banks, x, ready, g0, first=True, after=None):
            for s in range(SLOTS):
                pe.wait_ge(*split.made(g0 + s))
                order = [(n, k) for n in range(2) for k in range(NT)]
                if s == 0 and first:
                    order = [(n, k) for k in range(NT) for n in range(2)]
                for n, k in order:
                    job = f"{tag}{2 * s + n}"
                    if k == 0 and banks.free(job):
                        pe.wait_ge(*banks.free(job))
                    if s == 0 and n == 0:
                        pe.wait_ge(*ready(k))
                    mm = split.three(pe, banks.bank(job), g0 + s, by_cols, np.s_[:, k, n * P:(n + 1) * P],
                                     (x[0][:, k, :], x[1][:, k, :]), k == 0, k == NT - 1)
                    if k == NT - 1:
                        mm.then_inc(*pe_s.mark(job))
                if after:
                    after(s)

        def rwkv_jobs(second):
            eight = lambda tag, who="act": [(f"{tag}{n}", who) for n in range(NT)]
            jobs = eight("r") + eight("k") + eight("v")
            jobs[18:18] = [("kk sum", "dve")]
            jobs += [("w low", "act")] + eight("w")
            if second:
                jobs += [("v low", "act")] + eight("vmix")
            jobs += [("a low", "act")] + eight("a") + eight("kk inv", "dve") + [("g low", "act")] + eight("g")
            return jobs

        MIX = {"r": 0, "w": 1, "k": 2, "v": 3, "a": 4, "g": 5}

        def pick(t):
            at = CONSTS["pick"][0] + 14 - 2 * t
            return cst[:, at:at + HEADS]

        def rwkv_project(layer, m):
            stage(f"project{m}")
            second = m > 0
            r, k, v, lw, av = (region(j) for j in range(5, 10))
            gate, kkn, sq = region(2), u, region(6)
            parts = {"r": x_parts, "k": xk_parts, "v": x_parts}
            mixed = {"w": region(2), "a": region(3), "g": region(4)}
            tmp = low
            kk_sq = [lora[:, 4096:4608], lora[:, 4608:5120]]
            kk_inv = rstd[0:HEADS, :]
            k_factor = region(3)
            low_v = gate[:, 0:2, :]
            flat = arena[:, 2, :]
            v1 = flat[:, 1024:1280].rearrange("p (k n) -> p k n", n=LORA_V)
            resets = flat[:, 1280:1792]
            v2 = flat[0:LORA_V, 1792:2816]
            spread = flat[0:HEADS, 2816:3840]
            w1 = lora[:, 0:512].rearrange("p (k n) -> p k n", n=LORA_W)
            a1 = lora[:, 512:1024].rearrange("p (k n) -> p k n", n=LORA_A)
            g1 = lora[:, 1024:2048].rearrange("p (k n) -> p k n", n=LORA_G)
            w2, a2 = lora[0:LORA_W, 2048:3072], lora[0:LORA_A, 3072:4096]
            g2 = lora[:, 4096:5120]
            banks = Banks(rwkv_jobs(second))
            order = "rkvw"
            mu0 = VEC_ROW["rw_mu"][1] + m * 6 * NT
            ka0 = VEC_ROW["rw_ka"][0] * P + VEC_ROW["rw_ka"][1] + m * NT

            def before_tmp(p, t):
                return f"lo {p}{t - 2}" if t >= 2 else f"lo {order[order.index(p) - 1]}{t + 6}"

            with nc.Block() as block:
                @block.sync
                def _(sp):
                    km = lambda w: w.rearrange("(k p) n -> p k n", p=P)
                    load_proj(sp, a["rw_wk"][m], lambda s: split.made(s))
                    load_proj(sp, a["rw_wv"][m], lambda s: split.made(SLOTS + s))
                    sp.wait_ge(*pe_s("k7"))
                    for dst, name in ((w1, "rw_w1"), (a1, "rw_a1"), (g1, "rw_g1")):
                        bring_group(sp, "narrow", dst, km(a[name][m]))
                    bring_group(sp, "narrow", w2, a["rw_w2"][m])
                    bring_group(sp, "narrow", a2, a["rw_a2"][m])
                    load_proj(sp, a["rw_wo"][m], lambda s: split.made(2 * SLOTS + s))
                    sp.wait_ge(*pe_s("kk part7"))
                    bring_group(sp, "g2", g2, a["rw_g2"][m])
                    if second:
                        bring_group(sp, "v_first", av, a["v_first"].rearrange("p (t s) -> p t s", s=SEQ))
                    sp.wait_ge(*pe_s("w low"))
                    if second:
                        bring_group(sp, "extra", v1, km(a["rw_v1"][0]))
                        bring_group(sp, "extra", v2, a["rw_v2"][0])
                    bring_group(sp, "extra", resets, a["extras"][:, P + ROPE:P + ROPE + SEQ])
                    bring_group(sp, "extra", spread, a["extras"][0:HEADS, P + ROPE + SEQ:])
                    if not second:
                        sp.wait_ge(*act_s(f"ev v{NT - 1}"))
                        sp.dma_start(a["v_first"].rearrange("p (t s) -> p t s", s=SEQ), v).then_inc(v_stored, 16)
                        sp.wait_ge(v_stored, 16)

                @block.tensor
                def _(pe):
                    norm_pe(pe, "n", sq)

                    def low_rank(job, w, x, rows, ready):
                        pe.wait_ge(*banks.free(job))
                        for kt in range(NT):
                            if ready:
                                pe.wait_ge(*ready(kt))
                            for j, xj in enumerate(x):
                                mm = pe.matmul(banks.bank(job)[0:rows], w[:, kt, :], xj[:, kt, :],
                                               start=(kt == 0 and j == 0), stop=(kt == NT - 1 and j == len(x) - 1))
                        mm.then_inc(*pe_s.mark(job))

                    def widen(tag, low_job, w, x):
                        pe.wait_ge(*act_s(f"ev {low_job}"))
                        for n in range(NT):
                            job = f"{tag}{n}"
                            pe.wait_ge(*banks.free(job))
                            pe.matmul(banks.bank(job), w[:, n * P:(n + 1) * P], x,
                                      start=True, stop=True).then_inc(*pe_s.mark(job))

                    def kk_sums(s):
                        if s == 0:
                            pe.wait_ge(*banks.free("kk sum"))
                        for t in (2 * s, 2 * s + 1):
                            pe.wait_ge(*act_s(f"kk sq{t}"))
                            pe.matmul(banks.bank("kk sum")[0:HEADS], pick(t), kk_sq[t % 2], start=(t == 0),
                                      stop=(t == NT - 1), skip_group_check=True).then_inc(*pe_s.mark(f"kk part{t}"))

                    for q, p in enumerate("rkv"):
                        gemm(pe, p, banks, parts[p], lambda kt: dve_s(f"lo {p}{kt}"), SLOTS * q, q == 0,
                             kk_sums if p == "v" else None)
                    pe.wait_ge(*landed_group("narrow"))
                    low_rank("w low", w1, [mixed["w"]], LORA_W, lambda kt: dve_s(f"mix w{kt}"))
                    widen("w", "w low", w2, low[1][0:LORA_W, :])
                    pe.wait_ge(*landed_group("extra"))
                    if second:
                        low_rank("v low", v1, [x.bitcast(F32) for x in parts["v"]], LORA_V, None)
                        widen("vmix", "v low", v2, low[0][0:LORA_V, :])
                    low_rank("a low", a1, [mixed["a"]], LORA_A, lambda kt: dve_s(f"mix a{kt}"))
                    widen("a", "a low", a2, low[0][0:LORA_A, :])
                    pe.wait_ge(*dve_s("kk inv"))
                    for t in range(NT):
                        pe.wait_ge(*banks.free(f"kk inv{t}"))
                        pe.matmul(banks.bank(f"kk inv{t}"), spread[:, t * P:(t + 1) * P], kk_inv,
                                  start=True, stop=True).then_inc(*pe_s.mark(f"kk inv{t}"))
                    low_rank("g low", g1, [mixed["g"]], LORA_G, lambda kt: dve_s(f"mix g{kt}"))
                    pe.wait_ge(*landed_group("g2"))
                    widen("g", "g low", g2, low[1])

                @block.scalar
                def _(act):
                    def splits_ahead():
                        split.make_hi(act, 0)
                        split.make_hi(act, 1)

                    def pre(p, t, dst):
                        j = MIX[p] * NT + t
                        act.activation(dst, u[:, t, :], ACT.Copy, scale=one_less_mu[:, j:j + 1]).then_inc(*act_s.mark(f"pre {p}{t}"))

                    def pre_tmp(p, t):
                        if p != "r" or t >= 2:
                            act.wait_ge(*dve_s(before_tmp(p, t)))
                        pre(p, t, tmp[t % 2])

                    def hi(p, t):
                        act.wait_ge(*dve_s(f"mix {p}{t}"))
                        act.activation(parts[p][0][:, t, :], tmp[t % 2], ACT.Copy).then_inc(*act_s.mark(f"hi {p}{t}"))

                    def out(job, dst, func=ACT.Copy, **kw):
                        act.wait_ge(*pe_s(job))
                        act.activation(dst, banks.bank(job)[0:dst.shape[0]], func, **kw).then_inc(*act_s.mark(f"ev {job}"))

                    norm_act(act, "n", h, sq, meanwhile=splits_ahead)
                    act.wait_ge(*dve_s("1 - mu"))
                    for t in range(NT + 1):
                        if t < NT:
                            act.wait_ge(*dve_s(f"n out{t}"))
                            pre_tmp("r", t)
                        if t:
                            hi("r", t - 1)
                    for g in range(3 * SLOTS):
                        p, nxt, s = order[g // SLOTS], order[g // SLOTS + 1], g % SLOTS
                        if g and g + 1 < 3 * SLOTS:
                            act.wait_ge(*pe_s(f"{order[(g - 1) // SLOTS]}{2 * ((g - 1) % SLOTS) + 1}"))
                            split.make_hi(act, g + 1)
                        for t in (2 * s, 2 * s + 1):
                            if nxt == "w":
                                pre("w", t, mixed["w"][:, t, :])
                            else:
                                pre_tmp(nxt, t)
                        if nxt != "w":
                            hi(nxt, 2 * s)
                            hi(nxt, 2 * s + 1)
                        if p == "v":
                            for t in (2 * s, 2 * s + 1):
                                if t >= 2:
                                    act.wait_ge(*pe_s(f"kk part{t - 2}"))
                                act.activation(kk_sq[t % 2], k[:, t, :], ACT.Square,
                                               scale=col("rw_kk", m * NT + t)).then_inc(*act_s.mark(f"kk sq{t}"))
                        for n in (2 * s, 2 * s + 1):
                            out(f"{p}{n}", {"r": r, "k": k, "v": v}[p][:, n, :])

                    def pres(p, used):
                        act.wait_ge(*pe_s(used))
                        for t in range(NT):
                            pre(p, t, mixed[p][:, t, :])

                    act.wait_ge(*dve_s("ev kk sum"))
                    act.activation(kk_inv, kk_inv, ACT.Sqrt).then_inc(*act_s.mark("kk root"))
                    out("w low", low[1][0:LORA_W, :], ACT.Tanh)
                    if not second:
                        pres("a", "v7")
                    for n in range(NT):
                        out(f"w{n}", lw[:, n, :], ACT.Sigmoid, bias=col("rw_w0", m * NT + n))
                    if second:
                        out("v low", low[0][0:LORA_V, :])
                        pres("a", "v low")
                        for n in range(NT):
                            if n >= 2:
                                act.wait_ge(*dve_s(f"vmix{n - 2}"))
                            out(f"vmix{n}", low_v[:, n % 2, :], ACT.Sigmoid, bias=col("rw_v0", n))
                    pres("g", "v low" if second else "v7")
                    if second:
                        act.wait_ge(*dve_s(f"vmix{NT - 1}"))
                        act.wait_ge(*dve_s(f"v mixed{NT - 1}"))
                        act.wait_ge(*pe_s(f"vmix{NT - 1}"))
                    out("a low", low[0][0:LORA_A, :])
                    for n in range(NT):
                        out(f"a{n}", av[:, n, :], ACT.Sigmoid, bias=col("rw_a0", m * NT + n))
                    act.wait_ge(*dve_s("1 - k_a"))
                    for t in range(NT):
                        act.wait_ge(*act_s(f"ev a{t}"))
                        act.activation(k_factor[:, t, :], av[:, t, :], ACT.Identity, scale=col("rw_ka", m * NT + t),
                                       bias=one_less_ka[:, t:t + 1]).then_inc(*act_s.mark(f"k factor{t}"))
                    act.wait_ge(*pe_s(f"w{NT - 1}"))
                    out("g low", low[1], ACT.Sigmoid)
                    act.wait_ge(*dve_s(f"decay{NT - 1}"))
                    for n in range(NT):
                        out(f"g{n}", gate[:, n, :])

                @block.vector
                def _(dve):
                    dve.tensor_scalar(one_less_mu[:], vec[:, mu0:mu0 + 6 * NT], -1.0, 1.0, ALU.mult,
                                      ALU.add).then_inc(*dve_s.mark("1 - mu"))
                    dve.tensor_scalar(one_less_ka, vec[:, ka0:ka0 + NT], -1.0, 1.0, ALU.mult,
                                      ALU.add).then_inc(*dve_s.mark("1 - k_a"))
                    split.make_lo(dve, 0)
                    split.make_lo(dve, 1)

                    def mix(p, t, dst):
                        dve.wait_ge(*act_s(f"pre {p}{t}"))
                        dve.scalar_tensor_tensor(dst[:, 1:SEQ], u[:, t, 0:SEQ - 1],
                                                 col("rw_mu", (m * 6 + MIX[p]) * NT + t), dst[:, 1:SEQ],
                                                 ALU.mult, ALU.add).then_inc(*dve_s.mark(f"mix {p}{t}"))

                    def lo(p, t):
                        dve.wait_ge(*act_s(f"hi {p}{t}"))
                        dve.tensor_tensor(parts[p][1][:, t, :], tmp[t % 2], parts[p][0][:, t, :].bitcast(F32),
                                          ALU.subtract).then_inc(*dve_s.mark(f"lo {p}{t}"))

                    def norm_out(t):
                        dve.scalar_tensor_tensor(u[:, t, :], h[:, t, :], col("norm_mix", layer * NT + t), rstd,
                                                 ALU.mult, ALU.mult).then_inc(*dve_s.mark(f"n out{t}"))

                    dve.wait_ge(*act_s("n root"))
                    dve.reciprocal(rstd, rstd).then_inc(*dve_s.mark("n rstd"))
                    dve.wait_ge(*dve_s("n rstd"))
                    norm_out(0)
                    for t in range(NT):
                        if t + 1 < NT:
                            norm_out(t + 1)
                        mix("r", t, tmp[t % 2])
                        if t:
                            lo("r", t - 1)
                    lo("r", NT - 1)
                    for g in range(3 * SLOTS):
                        nxt, s = order[g // SLOTS + 1], g % SLOTS
                        if g and g + 1 < 3 * SLOTS:
                            split.make_lo(dve, g + 1)
                        for t in (2 * s, 2 * s + 1):
                            mix(nxt, t, mixed["w"][:, t, :] if nxt == "w" else tmp[t % 2])
                        if nxt != "w":
                            lo(nxt, 2 * s)
                            lo(nxt, 2 * s + 1)
                    dve.wait_ge(*pe_s(f"kk part{NT - 1}"))
                    dve.tensor_scalar(kk_inv, banks.bank("kk sum")[0:HEADS], 1e-24, None,
                                      ALU.max).then_inc(*dve_s.mark("ev kk sum"))
                    dve.wait_ge(*act_s("kk root"))
                    dve.reciprocal(kk_inv, kk_inv).then_inc(*dve_s.mark("kk reciprocal"))
                    dve.wait_ge(*dve_s("kk reciprocal"))
                    dve.tensor_scalar(kk_inv, kk_inv, -1.0, None, ALU.mult).then_inc(*dve_s.mark("kk inv"))
                    for t in range(NT):
                        mix("a", t, mixed["a"][:, t, :])
                    if second:
                        dve.wait_ge(*landed_group("v_first"))
                        for t in range(NT):
                            dve.wait_ge(*act_s(f"ev v{t}"))
                            dve.tensor_tensor(av[:, t, :], av[:, t, :], v[:, t, :],
                                              ALU.subtract).then_inc(*dve_s.mark(f"v gap{t}"))
                        for t in range(NT):
                            dve.wait_ge(*dve_s(f"v gap{t}"))
                            dve.wait_ge(*act_s(f"ev vmix{t}"))
                            dve.tensor_tensor(av[:, t, :], av[:, t, :], low_v[:, t % 2, :],
                                              ALU.mult).then_inc(*dve_s.mark(f"vmix{t}"))
                        for t in range(NT):
                            dve.wait_ge(*dve_s(f"vmix{t}"))
                            dve.tensor_tensor(v[:, t, :], v[:, t, :], av[:, t, :],
                                              ALU.add).then_inc(*dve_s.mark(f"v mixed{t}"))
                    for t in range(NT):
                        mix("g", t, mixed["g"][:, t, :])
                    dve.wait_ge(*landed_group("extra"))
                    for t in range(NT):
                        dve.wait_ge(*act_s(f"ev w{t}"))
                        dve.tensor_tensor_scan(lw[:, t, :], resets, lw[:, t, :], 0.0, ALU.mult,
                                               ALU.add).then_inc(*dve_s.mark(f"decay{t}"))
                    dve.wait_ge(*dve_s(f"mix g{NT - 1}"))
                    for t in range(NT):
                        dve.wait_ge(*pe_s(f"kk inv{t}"))
                        dve.scalar_tensor_tensor(kkn[:, t, :], k[:, t, :], col("rw_kk", m * NT + t),
                                                 banks.bank(f"kk inv{t}"), ALU.mult,
                                                 ALU.mult).then_inc(*dve_s.mark(f"ev kk inv{t}"))
                    for t in range(NT):
                        dve.wait_ge(*dve_s(f"ev kk inv{t}"))
                        dve.wait_ge(*act_s(f"k factor{t}"))
                        dve.scalar_tensor_tensor(av[:, t, :], av[:, t, :], -1.0, kkn[:, t, :],
                                                 ALU.mult, ALU.mult).then_inc(*dve_s.mark(f"b{t}"))
                        dve.tensor_tensor(k[:, t, :], k[:, t, :], k_factor[:, t, :],
                                          ALU.mult).then_inc(*dve_s.mark(f"k eff{t}"))
            ring.uses += 3 * SLOTS
            split.done += 3 * SLOTS

        def rwkv_scan(m):
            r, k, v, lw, b, kkn = region(5), region(6), region(7), region(8), region(9), region(1)
            flat = arena[:, 3:5, :].rearrange("p a n -> p (a n)")
            at = {"n": 0}

            def take(n):
                at["n"] += n
                return flat[:, at["n"] - n:at["n"]]

            def tile3(x, w):
                return x.rearrange("p (t n) -> p t n", n=w)

            ar = take(1536).rearrange("p (t three n) -> p t three n", three=3, n=CH)
            bk = take(1024).rearrange("p (t two n) -> p t two n", two=2, n=CH)
            gm = take(2048).rearrange("p (h n) -> p h n", n=P)
            bkt = tile3(take(1024), P)
            state = tile3(take(1024), P)
            vst = tile3(take(1024), P)
            grow = prod = tile3(take(512), CH)
            uv = tile3(lora[:, 0:1024], P)
            decay = lora[:, 1024:1024 + NT * (CH + 1)].rearrange("p (t n) -> p t n", n=CH + 1)
            w_last = lora[:, 1544:1552].unsqueeze(2)
            Tt = tile3(lora[:, 1552:2064], CH)
            tb = [tile3(lora[:, 2064 + 512 * j:2576 + 512 * j], CH) for j in range(5)]
            tb += [tile3(small[:, 512 * j:512 * (j + 1)], CH) for j in range(3)]
            xs = vst[:, :, 0:CH]
            b64 = lambda j: psum[:, j, :].rearrange("p (t n) -> p t n", n=CH)
            b128 = lambda j: psum[:, j, :].rearrange("p (t n) -> p t n", n=P)

            def wide(name):
                return const(name).unsqueeze(1).broadcast_to([P, NT, CH])

            mask_g = const("mask_g").unsqueeze(1).broadcast_to([P, 4, P])
            halves = [slice(0, CH), slice(CH, P)]
            D, Dt, Et, IpD, D2, D2t, ID2t, X2 = tb
            D4, D4t, ID4t, ID8, ID8t, X4 = tb[0], tb[1], tb[6], tb[4], tb[5], tb[3]
            X8, X8t, F, Ft, IpF, IF2, Z = tb[0], tb[1], tb[6], tb[7], tb[4], tb[5], tb[3]

            def gpsimd_pass(pool, i, new, prep, use):
                if prep:
                    if i is not None:
                        pool.wait_ge(*pe_s("U1", i))
                        pool.sem_inc(passed_pool, 1)
                    pool.tensor_copy(vst[:, :, CH:P], v[:, :, new]).then_inc(*pool_s.mark("stage v"))
                    pool.wait_ge(*dve_s("K", i))
                    pool.sem_inc(passed_pool, 1)
                    pool.tensor_tensor(prod, r[:, :, new], k[:, :, new], ALU.mult).then_inc(*pool_s.mark("rk"))
                    pool.wait_ge(*pool_s("rk", i))
                    pool.sem_inc(passed_pool, 1)
                    rk0 = VEC_ROW["rw_rk"][0] * P + VEC_ROW["rw_rk"][1] + m * NT
                    pool.tensor_tensor(prod, prod, vec[:, rk0:rk0 + NT].unsqueeze(2).broadcast_to([P, NT, CH]),
                                       ALU.mult).then_inc(*pool_s.mark("rk r_k"))
                if use:
                    pool.wait_ge(*pe_s("Y", i))
                    pool.sem_inc(passed_pool, 1)
                if prep:
                    pool.wait_ge(*act_s("decay", i))
                    pool.sem_inc(passed_pool, 1)
                    pool.tensor_tensor(ar[:, :, 2, :], r[:, :, new], decay[:, :, 1:CH + 1],
                                       ALU.mult).then_inc(*pool_s.mark("R"))
                    pool.tensor_copy(ar[:, :, 1, :], ar[:, :, 0, :]).then_inc(*pool_s.mark("A"))

            def scalar_pass(act, i, new, old, prep, use):
                def out(name, dst, src):
                    act.wait_ge(*pe_s(name, i))
                    act.activation(dst, src, ACT.Copy).then_inc(*act_s.mark(f"ev {name}"))

                if prep:
                    if i is not None:
                        act.wait_ge(*dve_s("w last", i - 1))
                        act.wait_ge(*pool_s("R", i - 1))
                        act.wait_ge(*pe_s("bonus", i - 1))
                    act.activation(decay[:, :, 1:CH + 1], lw[:, :, new], ACT.Exp,
                                   scale=-DECAY).then_inc(*act_s.mark("decay"))
                    act.activation(grow, lw[:, :, new], ACT.Exp, scale=DECAY).then_inc(*act_s.mark("grow"))
                    out("D2", D2, b64(3))
                if use:
                    out("U0", uv[halves[0], :, halves[0]], b64(4)[halves[0]])
                    out("U1", uv[halves[0], :, halves[1]], b64(5)[halves[0]])
                if prep:
                    act.wait_ge(*dve_s("I+D", i))
                    out("D4", D4, b64(0))
                if use:
                    out("Y", r[:, :, old], b64(6))
                if prep:
                    out("X2", X2, b64(1))
                    out("X4", X4, b64(2))
                    out("BK0", bkt[:, 0:4, :], b128(4))
                    out("BK1", bkt[:, 4:8, :], b128(5))
                    out("V0", uv[halves[1], 0:4, :], b128(6)[halves[1]])
                    out("V", uv[halves[1], 4:8, :], b128(0)[halves[1]])
                    out("X8", X8, b64(1))
                    out("F", F, b64(5))
                    out("Ft", Ft, b64(6))
                    out("Z", Z, b64(3))

            def vector_pass(dve, i, new, prep, use):
                def evacuate(mark, job, dst, src, mask, op=ALU.mult):
                    dve.wait_ge(*pe_s(job, i))
                    dve.tensor_tensor(dst, src, mask, op).then_inc(*dve_s.mark(mark))

                def turn(mark, dst, src):
                    dve.transpose(dst.rearrange("p t n -> p (t n)"),
                                  src.rearrange("p t n -> p (t n)")).then_inc(*dve_s.mark(mark))

                def plus_one(mark, dst, src):
                    dve.tensor_tensor(dst, src, wide("eye2"), ALU.add).then_inc(*dve_s.mark(mark))

                if prep:
                    if i is not None:
                        dve.wait_ge(*pool_s("A", i - 1))
                    dve.wait_ge(*act_s("decay", i))
                    dve.tensor_tensor(ar[:, :, 0, :], kkn[:, :, new], decay[:, :, 0:CH],
                                      ALU.mult).then_inc(*dve_s.mark("A"))
                    dve.wait_ge(*act_s("grow", i))
                    dve.tensor_tensor(bk[:, :, 0, :], b[:, :, new], grow, ALU.mult).then_inc(*dve_s.mark("B"))
                    dve.tensor_tensor(bk[:, :, 1, :], k[:, :, new], grow, ALU.mult).then_inc(*dve_s.mark("K"))
                    evacuate("D", "M", D, b64(0), wide("mask_d"))
                    evacuate("Dt", "Mt", Dt, b64(1), wide("mask_dt"))
                    evacuate("Et", "Mt", Et, b64(1), wide("mask_et"))
                if use:
                    dve.wait_ge(*pe_s("X", i))
                    dve.tensor_copy(xs, b64(2)).then_inc(*dve_s.mark("X"))
                if prep:
                    dve.wait_ge(*dve_s("D", i))
                    plus_one("I+D", IpD, D)
                    dve.wait_ge(*act_s("ev D2", i))
                    turn("D2t", D2t, D2)
                    dve.wait_ge(*dve_s("D2t", i))
                    plus_one("I+D2t", ID2t, D2t)
                    dve.wait_ge(*act_s("ev D4", i))
                    turn("D4t", D4t, D4)
                    dve.wait_ge(*dve_s("D4t", i))
                    dve.wait_ge(*pe_s("X2", i))
                    plus_one("I+D4t", ID4t, D4t)
                if use:
                    dve.wait_ge(*pe_s("S", i))
                    for q, part in enumerate(halves):
                        dve.tensor_tensor(state[part, :, part], state[part, :, part], b64(7)[part],
                                          ALU.add).then_inc(*dve_s.mark(f"sum{q}"))
                    for q, part in enumerate(halves):
                        dve.wait_ge(*dve_s(f"sum{q}", i))
                        dve.tensor_tensor(state[part, :, part], state[part, :, part],
                                          w_last[part].broadcast_to([CH, NT, CH]),
                                          ALU.mult).then_inc(*dve_s.mark(f"state{q}"))
                if prep:
                    if use:
                        dve.wait_ge(*dve_s("state1", i))
                    dve.tensor_copy(w_last, decay[:, :, CH:CH + 1]).then_inc(*dve_s.mark("w last"))
                    evacuate("I+D8", "D8", ID8, b64(3), wide("eye2"), op=ALU.add)
                    dve.wait_ge(*dve_s("I+D8", i))
                    turn("I+D8t", ID8t, ID8)
                    evacuate("G0", "G0", gm[:, 0:8:2, :], b128(3), mask_g)
                    evacuate("G1", "G1", gm[:, 1:8:2, :], b128(7), mask_g)
                    dve.wait_ge(*act_s("ev X8", i))
                    turn("X8t", X8t, X8)
                    dve.wait_ge(*pe_s("bonus", i))
                    dve.tensor_tensor(k[:, :, new], v[:, :, new], b64(4), ALU.mult).then_inc(*dve_s.mark("ev bonus"))
                    dve.wait_ge(*act_s("ev F", i))
                    plus_one("I+F", IpF, F)
                    evacuate("G2", "G2", gm[:, 8:16:2, :], b128(0), mask_g)
                    evacuate("G3", "G3", gm[:, 9:16:2, :], b128(2), mask_g)
                    evacuate("I+F2", "F2", IF2, b64(1), wide("eye2"), op=ALU.add)
                    dve.wait_ge(*pe_s("Tt", i))
                    dve.tensor_copy(Tt, b64(4)).then_inc(*dve_s.mark("Tt"))

            def tensor_pass(pe, i, prep, use):
                def heads(job, j, lhsT, rhs):
                    pe.sem_inc(passed_pe, 1)
                    for t in range(NT):
                        for part in halves:
                            mm = pe.matmul(b64(j)[part, t, :], lhsT(part, t), rhs(part, t), start=True, stop=True)
                    mm.then_inc(*pe_s.mark(job))

                def products(job, j, t0, part):
                    for t in range(4):
                        mm = pe.matmul(b128(j)[:, t, :], bk[part, t0 + t, :, :], ar[part, t0 + t, 0:3:2, :],
                                       start=True, stop=True)
                    mm.then_inc(*pe_s.mark(job))

                A = lambda part, t: ar[part, t, 0, :]
                B = lambda part, t: bk[part, t, 0, :]
                of = lambda x: (lambda part, t: x[part, t, :])
                if prep:
                    pe.wait_ge(*dve_s("B", i))
                    heads("M", 0, A, B)
                    heads("Mt", 1, B, A)
                if use:
                    if i is not None:
                        pe.wait_ge(*dve_s("Tt", i - 1))
                        pe.wait_ge(*pool_s("A", i - 1))
                        pe.sem_inc(passed_pe, 1)
                    for t in range(NT):
                        for q, part in enumerate(halves):
                            pe.matmul(b64(2)[part, t, :], ar[:, t, 1, :], state[:, t, part], start=True, stop=False)
                            mm = pe.matmul(b64(2)[part, t, :], gm[:, 2 * t + q, 0:CH], uv[:, t, part],
                                           start=False, stop=True)
                    mm.then_inc(*pe_s.mark("X"))
                if prep:
                    pe.wait_ge(*dve_s("Dt", i))
                    heads("D2", 3, of(Dt), of(D))
                if use:
                    pe.wait_ge(*dve_s("X", i))
                    pe.sem_inc(passed_pe, 1)
                    for q, part in enumerate(halves):
                        for t in range(NT):
                            mm = pe.matmul(b64(4 + q)[halves[0], t, :], Tt[part, t, :], xs[part, t, :],
                                           start=True, stop=True)
                        mm.then_inc(*pe_s.mark(f"U{q}"))
                if prep:
                    pe.wait_ge(*dve_s("D2t", i))
                    heads("D4", 0, of(D2t), of(D2))
                if use:
                    pe.wait_ge(*act_s("ev U1", i))
                    pe.sem_inc(passed_pe, 1)
                    for t in range(NT):
                        pe.matmul(b64(6)[:, t, :], state[:, t, :], ar[:, t, 2, :], start=True, stop=False,
                                  skip_group_check=True)
                        for q, part in enumerate(halves):
                            mm = pe.matmul(b64(6)[part, t, :], uv[:, t, part], gm[:, 2 * t + q, CH:P],
                                           start=False, stop=True, skip_group_check=True)
                    mm.then_inc(*pe_s.mark("Y"))
                    for t in range(NT):
                        for part in halves:
                            mm = pe.matmul(b64(7)[part, t, :], bkt[:, t, part], uv[:, t, part], start=True, stop=True)
                    mm.then_inc(*pe_s.mark("S"))
                if prep:
                    pe.wait_ge(*dve_s("I+D2t", i))
                    heads("X2", 1, of(ID2t), of(IpD))
                    pe.wait_ge(*dve_s("D4t", i))
                    heads("D8", 3, of(D4t), of(D4))
                    pe.wait_ge(*dve_s("I+D4t", i))
                    pe.wait_ge(*act_s("ev X2", i))
                    heads("X4", 2, of(ID4t), of(X2))
                    pe.wait_ge(*dve_s("K", i))
                    for half in range(2):
                        for t in range(4):
                            mm = pe.transpose(b128(4 + half)[:, t, :],
                                              bk[:, 4 * half + t, :, :].rearrange("p a n -> p (a n)"), const("ident"))
                        mm.then_inc(*pe_s.mark(f"BK{half}"))
                    pe.wait_ge(*pool_s("stage v", i))
                    if use:
                        pe.wait_ge(*act_s("ev Y", i))
                    for half, j in enumerate((6, 0)):
                        for t in range(4):
                            mm = pe.transpose(b128(j)[:, t, :], vst[:, 4 * half + t, :], const("ident"))
                        mm.then_inc(*pe_s.mark("V" if half else "V0"))
                    pe.wait_ge(*act_s("ev X4", i))
                    pe.wait_ge(*dve_s("I+D8t", i))
                    heads("X8", 1, of(ID8t), of(X4))
                    pe.wait_ge(*pool_s("A", i))
                    products("G0", 3, 0, halves[0])
                    products("G1", 7, 0, halves[1])
                    pe.wait_ge(*act_s("ev V", i))
                    pe.matmul(psum[:, 4, :], const("pair"), prod.rearrange("p t n -> p (t n)"),
                              start=True, stop=True).then_inc(*pe_s.mark("bonus"))
                    products("G2", 0, 4, halves[0])
                    products("G3", 2, 4, halves[1])
                    pe.wait_ge(*act_s("ev X8", i))
                    heads("F", 5, of(Et), of(X8))
                    heads("Ft", 6, of(X8), of(Et))
                    pe.wait_ge(*act_s("ev Ft", i))
                    heads("F2", 1, of(Ft), of(F))
                    pe.wait_ge(*dve_s("I+F", i))
                    heads("Z", 3, of(IpF), of(X8t))
                    pe.wait_ge(*act_s("ev Z", i))
                    pe.wait_ge(*dve_s("I+F2", i))
                    heads("Tt", 4, of(IF2), of(Z))

            first, last = slice(0, CH), slice((NCH - 1) * CH, NCH * CH)
            stage(f"scan{m} first")
            with nc.Block() as block:
                @block.gpsimd
                def _(pool):
                    for x, name in ((state, "state"), (uv, "uv"), (vst, "v")):
                        pool.memset(x[:], 0.0).then_inc(*pool_s.mark(f"zero {name}"))
                    pool.memset(decay[:, :, 0:1], 1.0).then_inc(*pool_s.mark("ones"))
                    pool.wait_ge(*pool_s("ones"))
                    gpsimd_pass(pool, None, first, True, False)

                @block.scalar
                def _(act):
                    act.wait_ge(*pool_s("ones"))
                    scalar_pass(act, None, first, None, True, False)

                @block.vector
                def _(dve):
                    vector_pass(dve, None, first, True, False)

                @block.tensor
                def _(pe):
                    tensor_pass(pe, None, True, False)

            stage(f"scan{m}")
            with nc.Block() as block:
                @block.gpsimd
                def _(pool):
                    with pool.Fori(0, NCH - 1) as i:
                        pool_s.start_loop(i)
                        gpsimd_pass(pool, i, bass.ds(i * CH + CH, CH), True, True)
                        pool_s.end_loop(NCH - 1)

                @block.scalar
                def _(act):
                    with act.Fori(0, NCH - 1) as i:
                        act_s.start_loop(i)
                        scalar_pass(act, i, bass.ds(i * CH + CH, CH), bass.ds(i * CH, CH), True, True)
                        act_s.end_loop(NCH - 1)

                @block.vector
                def _(dve):
                    with dve.Fori(0, NCH - 1) as i:
                        dve_s.start_loop(i)
                        vector_pass(dve, i, bass.ds(i * CH + CH, CH), True, True)
                        dve_s.end_loop(NCH - 1)

                @block.tensor
                def _(pe):
                    with pe.Fori(0, NCH - 1) as i:
                        pe_s.start_loop(i)
                        tensor_pass(pe, i, True, True)
                        pe_s.end_loop(NCH - 1)

            stage(f"scan{m} last")
            with nc.Block() as block:
                @block.scalar
                def _(act):
                    scalar_pass(act, None, None, last, False, True)

                @block.vector
                def _(dve):
                    vector_pass(dve, None, None, False, True)

                @block.tensor
                def _(pe):
                    tensor_pass(pe, None, False, True)

        def rwkv_finish(layer, m):
            stage(f"finish{m}")
            y, bonus, gate, yc, sq = region(5), region(6), region(2), region(7), region(1)
            inv = rstd[0:HEADS, :]
            spread = lora[0:HEADS, 0:DM]
            banks = Banks([(f"mean{t}", "dve") for t in range(NT)] + [("var sum", "act")]
                          + [(f"inv{t}", "dve") for t in range(NT)] + [(f"o{t}", "dve") for t in range(NT)])
            with nc.Block() as block:
                @block.sync
                def _(sp):
                    bring_group(sp, "spread", spread, a["extras"][0:HEADS, P + ROPE + SEQ:])
                    ffn_head(sp, layer, lambda s: split.made(s))

                @block.tensor
                def _(pe):
                    for t in range(NT):
                        pe.matmul(banks.bank(f"mean{t}"), const("pair"), y[:, t, :],
                                  start=True, stop=True).then_inc(*pe_s.mark(f"mean{t}"))
                    pe.wait_ge(*banks.free("var sum"))
                    for t in range(NT):
                        pe.wait_ge(*act_s(f"sq{t}"))
                        mm = pe.matmul(banks.bank("var sum")[0:HEADS], pick(t), sq[:, t, :],
                                       start=(t == 0), stop=(t == NT - 1))
                    mm.then_inc(*pe_s.mark("var sum"))
                    pe.wait_ge(*landed_group("spread"))
                    pe.wait_ge(*dve_s("inv"))
                    for t in range(NT):
                        pe.wait_ge(*banks.free(f"inv{t}"))
                        pe.matmul(banks.bank(f"inv{t}"), spread[:, t * P:(t + 1) * P], inv,
                                  start=True, stop=True).then_inc(*pe_s.mark(f"inv{t}"))
                    gemm(pe, "o", banks, x_parts, lambda k: dve_s(f"lo{k}"), 0)

                @block.scalar
                def _(act):
                    split.make_hi(act, 0)
                    for t in range(NT):
                        act.wait_ge(*dve_s(f"ev mean{t}"))
                        act.activation(sq[:, t, :], yc[:, t, :], ACT.Square).then_inc(*act_s.mark(f"sq{t}"))
                    split.make_hi(act, 1)
                    act.wait_ge(*pe_s("var sum"))
                    act.activation(inv, banks.bank("var sum")[0:HEADS], ACT.Sqrt, bias=gn_eps[0:HEADS],
                                   scale=1.0 / HEAD).then_inc(*act_s.mark("ev var sum"))
                    for t in range(NT):
                        act.wait_ge(*pool_s(f"gated{t}"))
                        act.activation(x_parts[0][:, t, :], y[:, t, :], ACT.Copy).then_inc(*act_s.mark(f"hi{t}"))
                    for g in (2, 3):
                        act.wait_ge(*pe_s(f"o{2 * (g - 2) + 1}"))
                        split.make_hi(act, g)

                @block.vector
                def _(dve):
                    for t in range(NT):
                        dve.wait_ge(*pe_s(f"mean{t}"))
                        dve.scalar_tensor_tensor(yc[:, t, :], banks.bank(f"mean{t}"), -1.0 / HEAD, y[:, t, :],
                                                 ALU.mult, ALU.add).then_inc(*dve_s.mark(f"ev mean{t}"))
                    split.make_lo(dve, 0)
                    split.make_lo(dve, 1)
                    dve.wait_ge(*act_s("ev var sum"))
                    dve.reciprocal(inv, inv).then_inc(*dve_s.mark("inv"))

                    def lo(t):
                        dve.wait_ge(*act_s(f"hi{t}"))
                        dve.tensor_tensor(x_parts[1][:, t, :], y[:, t, :], x_parts[0][:, t, :].bitcast(F32),
                                          ALU.subtract).then_inc(*dve_s.mark(f"lo{t}"))

                    for t in range(NT):
                        dve.wait_ge(*pe_s(f"inv{t}"))
                        dve.scalar_tensor_tensor(yc[:, t, :], yc[:, t, :], col("rw_lnx_w", m * NT + t),
                                                 banks.bank(f"inv{t}"), ALU.mult,
                                                 ALU.mult).then_inc(*dve_s.mark(f"ev inv{t}"))
                        dve.wait_ge(*dve_s(f"ev inv{t}"))
                        dve.scalar_tensor_tensor(yc[:, t, :], yc[:, t, :], col("rw_lnx_b", m * NT + t), bonus[:, t, :],
                                                 ALU.add, ALU.add).then_inc(*dve_s.mark(f"with bonus{t}"))
                        if t >= 2:
                            lo(t - 2)
                    lo(NT - 2)
                    lo(NT - 1)
                    for s in range(SLOTS):
                        if s < 2:
                            split.make_lo(dve, s + 2)
                        for t in (2 * s, 2 * s + 1):
                            dve.wait_ge(*pe_s(f"o{t}"))
                            dve.tensor_tensor(h[:, t, :], h[:, t, :], banks.bank(f"o{t}"),
                                              ALU.add).then_inc(*dve_s.mark(f"ev o{t}"))

                @block.gpsimd
                def _(pool):
                    for t in range(NT):
                        pool.wait_ge(*dve_s(f"with bonus{t}"))
                        pool.tensor_tensor(y[:, t, :], yc[:, t, :], gate[:, t, :],
                                           ALU.mult).then_inc(*pool_s.mark(f"gated{t}"))
            ring.uses += SLOTS
            split.done += SLOTS

        def conv_glu(layer):
            stage("glu")
            sq, total, tmp = region(6), region(7)[:, 0, :], region(7)[:, 2:6, :]
            gain = lambda t: col("norm_mix", layer * NT + t)
            jobs = [[f"{'ab'[s % 2]}{4 * turn + 2 * (s // 2) + n}" for n in range(2)]
                    for turn in range(2) for s in range(SLOTS)]
            banks = Banks([(j, "dve") for pair in jobs for j in pair])
            with nc.Block() as block:
                @block.sync
                def _(sp):
                    bring(sp, taps_rows, a["cv_dw"][0])
                    w1 = a["cv_w1"][0].rearrange("(k p) n -> p k n", p=P)
                    for s in range(SLOTS):
                        c = (2 + s // 2) * 256 + (s % 2) * DM
                        ring.load(sp, cols_slot(s), w1[:, :, c:c + 256], split.made(s))
                    load_proj(sp, a["cv_w2"][0], lambda s: split.made(SLOTS + s))
                taps_in = ins["n"]

                @block.gpsimd
                def _(pool):
                    pool.memset(glu[:, :, 0:PAD], 0.0).then_inc(*pool_s.mark("pad"))
                    fold_pool(pool, sq, total)

                @block.tensor
                def _(pe):
                    pe.wait_ge(in_landed, taps_in)
                    for t in range(NT):
                        mm = pe.transpose(psum[:, 6, t * TAPS:(t + 1) * TAPS], taps_rows[:, t * P:(t + 1) * P],
                                          cst[0:TAPS, 0:TAPS])
                    mm.then_inc(*pe_s.mark("taps"))
                    for g, pair in enumerate(jobs):
                        pe.wait_ge(*split.made(g))
                        order = [(n, k) for k in range(NT) for n in range(2)]
                        if g:
                            order = [(n, k) for n in range(2) for k in range(NT)]
                        for n, k in order:
                            if k == 0 and banks.free(pair[n]):
                                pe.wait_ge(*banks.free(pair[n]))
                            if g == 3 and k == 0:
                                pe.wait_ge(*act_s("root" if n else "taps"))
                            if g == 0 and n == 0:
                                pe.wait_ge(*dve_s(f"x{k}"))
                            mm = split.three(pe, banks.bank(pair[n]), g, by_cols, np.s_[:, k, n * P:(n + 1) * P],
                                             (x_parts[0][:, k, :], x_parts[1][:, k, :]), k == 0, k == NT - 1)
                            if k == NT - 1:
                                mm.then_inc(*pe_s.mark(pair[n]))
                        if g == 0:
                            fold_pe(pe, total)

                @block.scalar
                def _(act):
                    split.make_hi(act, 0)
                    fold_act(act, gain, sq)
                    act.wait_ge(*pe_s("taps"))
                    act.activation(taps.rearrange("p t j -> p (t j)"), psum[:, 6, 0:NT * TAPS],
                                   ACT.Copy).then_inc(*act_s.mark("taps"))
                    split.make_hi(act, 1)
                    for g, pair in enumerate(jobs):
                        if g + 2 < len(jobs):
                            act.wait_ge(*pe_s(pair[1]))
                            split.make_hi(act, g + 2)
                        if g == 0:
                            fold_root(act)
                        if g % 2:
                            for n, job in enumerate(pair):
                                act.wait_ge(*dve_s(f"ev {job}"))
                                t = int(job[1:])
                                act.activation(sig[:, t, :], tmp[:, n, :], ACT.Sigmoid,
                                               bias=col("cv_b1", NT + t)).then_inc(*act_s.mark(f"sig{t}"))

                @block.vector
                def _(dve):
                    fold_dve(dve, gain)
                    split.make_lo(dve, 1)
                    for g, pair in enumerate(jobs):
                        if g + 2 < len(jobs):
                            split.make_lo(dve, g + 2)
                        if g == 0:
                            fold_rstd(dve)
                        if g % 2:
                            for j, job in enumerate(pair + jobs[g - 1]):
                                dve.wait_ge(*pe_s(job))
                                if j >= 2 and g > 1:
                                    dve.wait_ge(*dve_s(f"glu{int(job[1:]) - 2}"))
                                dve.tensor_tensor(tmp[:, j, :], banks.bank(job), rstd,
                                                  ALU.mult).then_inc(*dve_s.mark(f"ev {job}"))
                            for n, job in enumerate(jobs[g - 1]):
                                t = int(job[1:])
                                dve.wait_ge(*dve_s(f"ev {job}"))
                                dve.wait_ge(*act_s(f"sig{t}"))
                                dve.scalar_tensor_tensor(glu[:, t, PAD:PAD + SEQ], tmp[:, 2 + n, :], col("cv_b1", t),
                                                         sig[:, t, :], ALU.add, ALU.mult).then_inc(*dve_s.mark(f"glu{t}"))
            ring.uses += len(jobs)
            split.done += len(jobs)

        def conv_taps():
            stage("taps")
            z, acc, acc2 = region(5), region(6), region(7)
            diag = arena[:, 3, :].rearrange("p (b j c) -> p b j c", b=2, c=P)
            term = arena[:, 4, :].rearrange("p (b s) -> p b s", s=SEQ)
            eye = const("ident").unsqueeze(1).broadcast_to([P, PE_TAPS, P])
            with nc.Block() as block:
                @block.vector
                def _(dve):
                    for t in range(NT):
                        b = t % 2
                        if t >= 2:
                            dve.wait_ge(*pe_s(f"conv{t - 2}"))
                        dve.tensor_tensor(diag[:, b, 0:PE_TAPS, :], eye,
                                          taps[:, t, 0:PE_TAPS].unsqueeze(2).broadcast_to([P, PE_TAPS, P]),
                                          ALU.mult).then_inc(*dve_s.mark(f"diag{t}"))
                        for j in range(PE_TAPS + ACT_TAPS, TAPS):
                            first = j == PE_TAPS + ACT_TAPS
                            if first:
                                op = dve.tensor_scalar(acc[:, t, :], glu[:, t, j:j + SEQ], taps[:, t, j:j + 1], None, ALU.mult)
                            else:
                                dve.wait_ge(*dve_s(f"tap{t} {j - 1}"))
                                op = dve.scalar_tensor_tensor(acc[:, t, :], glu[:, t, j:j + SEQ], taps[:, t, j:j + 1],
                                                              acc[:, t, :], ALU.mult, ALU.add)
                            op.then_inc(*dve_s.mark(f"tap{t} {j}"))
                        dve.wait_ge(*pe_s(f"conv{t}"))
                        dve.wait_ge(*dve_s(f"tap{t} {TAPS - 1}"))
                        dve.scalar_tensor_tensor(acc[:, t, :], psum[:, t % 4, :], col("cv_bdw", t), acc[:, t, :],
                                                 ALU.add, ALU.add).then_inc(*dve_s.mark(f"taps{t}"))
                        dve.wait_ge(*dve_s(f"taps{t}"))
                        dve.wait_ge(*pool_s(f"term{t} {ACT_TAPS - 1}"))
                        dve.tensor_tensor(z[:, t, :], acc[:, t, :], acc2[:, t, :],
                                          ALU.add).then_inc(*dve_s.mark(f"z{t}"))

                @block.scalar
                def _(act):
                    for t in range(NT):
                        for j in range(ACT_TAPS):
                            n = t * ACT_TAPS + j
                            if n >= 8:
                                before = n - 8
                                act.wait_ge(*pool_s(f"term{before // ACT_TAPS} {before % ACT_TAPS}"))
                            tap = PE_TAPS + j
                            act.activation(term[:, n % 8, :], glu[:, t, tap:tap + SEQ], ACT.Copy,
                                           scale=taps[:, t, tap:tap + 1]).then_inc(*act_s.mark(f"term{t} {j}"))

                @block.gpsimd
                def _(pool):
                    for t in range(NT):
                        for j in range(ACT_TAPS):
                            n = t * ACT_TAPS + j
                            pool.wait_ge(*act_s(f"term{t} {j}"))
                            if j == 0:
                                op = pool.tensor_copy(acc2[:, t, :], term[:, n % 8, :])
                            else:
                                pool.wait_ge(*pool_s(f"term{t} {j - 1}"))
                                op = pool.tensor_tensor(acc2[:, t, :], acc2[:, t, :], term[:, n % 8, :], ALU.add)
                            op.then_inc(*pool_s.mark(f"term{t} {j}"))

                @block.tensor
                def _(pe):
                    def mean(t):
                        pe.wait_ge(*dve_s(f"z{t}"))
                        pe.matmul(psum[:, 6, :], const("ones"), z[:, t, :], start=(t == 0), stop=(t == NT - 1),
                                  skip_group_check=True).then_inc(*pe_s.mark(f"mean{t}"))

                    for t in range(NT):
                        pe.wait_ge(*dve_s(f"diag{t}"))
                        if t >= 4:
                            pe.wait_ge(*dve_s(f"taps{t - 4}"))
                        for j in range(PE_TAPS):
                            mm = pe.matmul(psum[:, t % 4, :], diag[:, t % 2, j, :], glu[:, t, j:j + SEQ],
                                           start=(j == 0), stop=(j == PE_TAPS - 1), skip_group_check=True)
                        mm.then_inc(*pe_s.mark(f"conv{t}"))
                        if t >= 2:
                            mean(t - 2)
                    mean(NT - 2)
                    mean(NT - 1)

        def conv_finish(layer):
            stage("convout")
            z, zc, sq = region(5), region(6), region(7)
            banks = Banks([(f"o{t}", "dve") for t in range(NT)])
            with nc.Block() as block:
                @block.sync
                def _(sp):
                    ffn_head(sp, layer, lambda s: split.made(s))

                @block.tensor
                def _(pe):
                    norm_pe(pe, "n", sq)
                    gemm(pe, "o", banks, x_parts, lambda k: dve_s(f"lo{k}"), 0)

                @block.scalar
                def _(act):
                    split.make_hi(act, 0)
                    for t in range(NT):
                        act.wait_ge(*dve_s(f"centred{t}"))
                        act.activation(sq[:, t, :], zc[:, t, :], ACT.Square).then_inc(*act_s.mark(f"n sq{t}"))
                    split.make_hi(act, 1)
                    act.wait_ge(*pe_s("n sum"))
                    act.activation(rstd, psum[:, 7, :], ACT.Sqrt, bias=eps, scale=1.0 / DM).then_inc(*act_s.mark("n root"))
                    for t in range(NT + 1):
                        if t < NT:
                            act.wait_ge(*dve_s(f"n out{t}"))
                            act.activation(z[:, t, :], zc[:, t, :], ACT.Silu,
                                           bias=col("cv_ln_b", t)).then_inc(*act_s.mark(f"silu{t}"))
                        if t:
                            act.wait_ge(*act_s(f"silu{t - 1}"))
                            act.activation(x_parts[0][:, t - 1, :], z[:, t - 1, :],
                                           ACT.Copy).then_inc(*act_s.mark(f"hi{t - 1}"))
                    for g in (2, 3):
                        act.wait_ge(*pe_s(f"o{2 * (g - 2) + 1}"))
                        split.make_hi(act, g)

                @block.vector
                def _(dve):
                    for t in range(NT):
                        dve.scalar_tensor_tensor(zc[:, t, :], psum[:, 6, :], -1.0 / DM, z[:, t, :],
                                                 ALU.mult, ALU.add).then_inc(*dve_s.mark(f"centred{t}"))
                    split.make_lo(dve, 0)
                    split.make_lo(dve, 1)
                    norm_dve(dve, "n", zc, zc, lambda t: col("cv_ln_w", t))
                    for t in range(NT):
                        dve.wait_ge(*act_s(f"hi{t}"))
                        dve.tensor_tensor(x_parts[1][:, t, :], z[:, t, :], x_parts[0][:, t, :].bitcast(F32),
                                          ALU.subtract).then_inc(*dve_s.mark(f"lo{t}"))
                    for t in range(NT):
                        if t in (0, 2):
                            split.make_lo(dve, 2 + t // 2)
                        dve.wait_ge(*pe_s(f"o{t}"))
                        dve.scalar_tensor_tensor(h[:, t, :], banks.bank(f"o{t}"), col("cv_b2", t), h[:, t, :],
                                                 ALU.add, ALU.add).then_inc(*dve_s.mark(f"ev o{t}"))
            ring.uses += SLOTS
            split.done += SLOTS

        glu = arena[:, 1:3, :].rearrange("p a n -> p (a n)")[:, 0:NT * (PAD + SEQ)].rearrange(
            "p (t s) -> p t s", s=PAD + SEQ)
        sig = region(5)
        taps_rows = lora[0:TAPS, 0:DM]
        taps = lora[:, DM:DM + NT * TAPS].rearrange("p (t j) -> p t j", j=TAPS)

        cbuf = region(2)
        kr, sin_t, cos_t = (cbuf[NOPE:QK, t, :] for t in (5, 6, 7))
        q_t = arena[:, 3:5, :].rearrange("p a (t s) -> p (a t) s", s=SEQ)
        k_t = arena[:, 5:7, :].rearrange("p a (t s) -> p (a t) s", s=SEQ)
        v_tok = arena[:, 7, :].rearrange("p (t d) -> p t d", d=HEADS * VDIM)
        probs = region(8)
        o_t = region(1)
        causal, turn_m = lora[:, 0:P], lora[NOPE:QK, P:P + ROPE]
        CQ, CKV = Q_LORA // P, KV_LORA // P
        Q_HEADS = [6, 6, 4]
        wd_slot = lambda s, w: ring.slot(s)[:, 0:NT * w].rearrange("p (k n) -> p k n", n=w)
        uq_slot = lambda s, w: ring.slot(s)[:, 0:CQ * w].rearrange("p (k n) -> p k n", n=w)

        def mla_down(layer):
            stage("down")
            sq, total = region(5), region(6)[:, 0, :]
            gain = lambda t: col("norm_mix", layer * NT + t)
            wd_cols = [256, 256, P + ROPE]
            steps = [[0, 1], [2, 3], [4, 5]]
            pos_i = small[NOPE:QK, 1024:1536].bitcast(I32)
            pos = lora[NOPE:QK, 512:1024]
            turns_f, turns_i, gap = lora[NOPE:QK, 1024:1536], lora[NOPE:QK, 1536:2048].bitcast(I32), lora[NOPE:QK, 2048:2560]
            angle = lora[NOPE:QK, 2560:3072]
            freq = cst[NOPE:QK, CONSTS["cols"][0] + 2:CONSTS["cols"][0] + 3]
            rstd_kv = low[0]
            with nc.Block() as block:
                @block.sync
                def _(sp):
                    bring(sp, pos_i, a["positions"][0].partition_broadcast(ROPE))
                    bring(sp, lora[:, 0:P + ROPE], a["extras"][:, 0:P + ROPE])
                    wuq = a["ml_wuq"][0].rearrange("(k p) n -> p k n", p=P)
                    wukv = a["ml_wukv"][0].rearrange("(k p) n -> p k n", p=P)
                    c = 0
                    for j, nh in enumerate(Q_HEADS):
                        ring.load(sp, uq_slot(3 + j, nh * QK), wuq[:, :, c:c + nh * QK],
                                  split.made(j - 1) if j else None)
                        c += nh * QK
                    ring.load(sp, rows_slot(2), wukv[:, :, 0:DM], split.made(2))
                loads_all = ins["n"]

                @block.gpsimd
                def _(pool):
                    fold_pool(pool, sq, total)

                @block.tensor
                def _(pe):
                    for g, tiles in enumerate(steps):
                        pe.wait_ge(*split.made(g))
                        order = [(n, k) for k in range(NT) for n in range(2)]
                        if g:
                            order = [(n, k) for n in range(2) for k in range(NT)]
                        for n, k in order:
                            if g == 0 and n == 0:
                                pe.wait_ge(*dve_s(f"x{k}"))
                            c = k * wd_cols[g] + (NOPE if tiles[n] == 5 else n * P)
                            mm = split.three(pe, psum[:, tiles[n], :], g, lambda w: w, np.s_[:, c:c + P],
                                             (x_parts[0][:, k, :], x_parts[1][:, k, :]), k == 0, k == NT - 1)
                            if k == NT - 1:
                                mm.then_inc(*pe_s.mark(f"c{tiles[n]}"))
                        if g == 0:
                            fold_pe(pe, total)
                    pe.wait_ge(*act_s("root"))
                    for t in range(CQ + CKV):
                        pe.wait_ge(*act_s(f"csq{t}"))
                        mm = pe.matmul(psum[:, 6 if t < CQ else 7, :], const("ones"), sq[:, t, :],
                                       start=t in (0, CQ), stop=t in (CQ - 1, CQ + CKV - 1))
                        if t == CQ - 1:
                            mm.then_inc(*pe_s.mark("cq sum"))
                    mm.then_inc(*pe_s.mark("ckv sum"))

                @block.scalar
                def _(act):
                    split.make_hi(act, 0)
                    fold_act(act, gain, sq)
                    split.make_hi(act, 1)
                    act.wait_ge(*pe_s("c1"))
                    split.make_hi(act, 2)
                    fold_root(act)
                    for t in range(CQ + CKV):
                        act.wait_ge(*dve_s(f"ev c{t}"))
                        act.activation(sq[:, t, :], cbuf[:, t, :], ACT.Square).then_inc(*act_s.mark(f"csq{t}"))
                    act.wait_ge(*pe_s("cq sum"))
                    act.wait_ge(*dve_s("ev c5"))
                    act.activation(rstd, psum[:, 6, :], ACT.Sqrt, bias=eps, scale=1.0 / Q_LORA).then_inc(*act_s.mark("cq root"))
                    act.wait_ge(*pe_s("ckv sum"))
                    act.activation(rstd_kv, psum[:, 7, :], ACT.Sqrt, bias=eps,
                                   scale=1.0 / KV_LORA).then_inc(*act_s.mark("ckv root"))
                    act.wait_ge(*dve_s("sin angle"))
                    act.activation(sin_t, angle, ACT.Sin).then_inc(*act_s.mark("sin"))
                    act.wait_ge(*dve_s("cos angle"))
                    act.activation(cos_t, gap, ACT.Sin).then_inc(*act_s.mark("cos"))

                @block.vector
                def _(dve):
                    fold_dve(dve, gain)
                    split.make_lo(dve, 1)
                    split.make_lo(dve, 2)
                    counter = [0]

                    def then(op):
                        counter[0] += 1
                        name = f"angle {counter[0]}"
                        op.then_inc(*dve_s.mark(name))
                        dve.wait_ge(*dve_s(name))

                    def wrap(x):
                        then(dve.tensor_scalar(turns_f, x, float(np.pi), -TWO_PI, ALU.is_gt, ALU.mult))
                        then(dve.tensor_tensor(x, x, turns_f, ALU.add))
                        then(dve.tensor_scalar(turns_f, x, -float(np.pi), TWO_PI, ALU.is_lt, ALU.mult))
                        then(dve.tensor_tensor(x, x, turns_f, ALU.add))

                    dve.wait_ge(in_landed, loads_all)
                    then(dve.tensor_copy(pos, pos_i))
                    then(dve.tensor_scalar(angle, pos, freq, None, ALU.mult))
                    then(dve.tensor_scalar(turns_i, angle, 1.0 / TWO_PI, None, ALU.mult))
                    then(dve.tensor_copy(turns_f, turns_i))
                    then(dve.scalar_tensor_tensor(angle, turns_f, -6.28125, angle, ALU.mult, ALU.add))
                    then(dve.scalar_tensor_tensor(angle, turns_f, -(TWO_PI - 6.28125), angle, ALU.mult, ALU.add))
                    wrap(angle)
                    then(dve.tensor_scalar(gap, angle, float(np.pi / 2), None, ALU.add))
                    dve.tensor_scalar(angle, angle, PI_BELOW, -PI_BELOW, ALU.min,
                                      ALU.max).then_inc(*dve_s.mark("sin angle"))
                    wrap(gap)
                    dve.tensor_scalar(gap, gap, PI_BELOW, -PI_BELOW, ALU.min, ALU.max).then_inc(*dve_s.mark("cos angle"))
                    fold_rstd(dve)
                    for t in range(6):
                        rows = slice(NOPE, QK) if t == 5 else slice(0, P)
                        dve.wait_ge(*pe_s(f"c{t}"))
                        dve.tensor_tensor(cbuf[rows, t, :], psum[rows, t, :], rstd[rows, :],
                                          ALU.mult).then_inc(*dve_s.mark(f"ev c{t}"))
                    for name, buf, ts, vector in (("cq", rstd, range(CQ), "ml_gq"), ("ckv", rstd_kv, range(CQ, CQ + CKV), "ml_gkv")):
                        dve.wait_ge(*act_s(f"{name} root"))
                        dve.reciprocal(buf, buf).then_inc(*dve_s.mark(f"{name} rstd"))
                        dve.wait_ge(*dve_s(f"{name} rstd"))
                        for t in ts:
                            dve.scalar_tensor_tensor(cbuf[:, t, :], cbuf[:, t, :], col(vector, t - ts[0]), buf,
                                                     ALU.mult, ALU.mult).then_inc(*dve_s.mark(f"latent{t}"))
            ring.uses += len(steps)
            split.done += len(steps)

        def mla_up(layer):
            stage("up")
            jobs = ["rot k"]
            for hd in range(HEADS):
                jobs += [f"q{hd}"] + ([f"rot q{hd - 1}"] if hd else [])
            jobs += [f"rot q{HEADS - 1}"] + [f"k{hd}" for hd in range(HEADS)] + [f"v{j}" for j in range(8)]
            banks = Banks([(j, "dve" if j.startswith("rot") or j[0] == "v" else "act") for j in jobs])
            rot_sin = [lora[NOPE:QK, 512:1024], lora[NOPE:QK, 1024:1536]]
            raw_cos = [lora[NOPE:QK, 1536:2048], lora[NOPE:QK, 2048:2560]]
            with nc.Block() as block:
                @block.sync
                def _(sp):
                    wukv = a["ml_wukv"][0].rearrange("(k p) n -> p k n", p=P)
                    ring.load(sp, rows_slot(3), wukv[:, :, DM:2 * DM], pe_s(f"q{Q_HEADS[0] - 1}"))
                    wv = a["ml_wo"][0].rearrange("(k p) n -> p k n", p=P)
                    last = [f"q{Q_HEADS[0] + Q_HEADS[1] - 1}", f"q{HEADS - 1}", "v6", "v7"]
                    for s in range(SLOTS):
                        ring.load(sp, cols_slot(s), wv[:, :, s * 256:(s + 1) * 256], pe_s(last[s]))

                def rotated(pe, name, rows):
                    if banks.free(f"rot {name}"):
                        pe.wait_ge(*banks.free(f"rot {name}"))
                    pe.matmul(banks.bank(f"rot {name}")[NOPE:QK], turn_m, rows,
                              start=True, stop=True).then_inc(*pe_s.mark(f"rot {name}"))

                @block.tensor
                def _(pe):
                    rotated(pe, "k", kr)
                    hd = 0
                    for j, nh in enumerate(Q_HEADS):
                        slot_landed(pe, j)
                        w = uq_slot(3 + j, nh * QK)
                        for n in range(nh):
                            if banks.free(f"q{hd}"):
                                pe.wait_ge(*banks.free(f"q{hd}"))
                            for k in range(CQ):
                                mm = pe.matmul(banks.bank(f"q{hd}")[0:QK], w[:, k, n * QK:(n + 1) * QK], cbuf[:, k, :],
                                               start=(k == 0), stop=(k == CQ - 1))
                            mm.then_inc(*pe_s.mark(f"q{hd}"))
                            if hd:
                                pe.wait_ge(*act_s(f"ev q{hd - 1}"))
                                rotated(pe, f"q{hd - 1}", q_t[NOPE:QK, hd - 1, :])
                            hd += 1
                    pe.wait_ge(*act_s(f"ev q{HEADS - 1}"))
                    rotated(pe, f"q{HEADS - 1}", q_t[NOPE:QK, HEADS - 1, :])
                    for hd in range(HEADS):
                        if hd % 8 == 0:
                            slot_landed(pe, 3 + hd // 8)
                        w = rows_slot(2 + hd // 8)
                        pe.wait_ge(*banks.free(f"k{hd}"))
                        for k in range(CKV):
                            c = (hd % 8) * (NOPE + VDIM)
                            mm = pe.matmul(banks.bank(f"k{hd}")[0:NOPE], w[:, k, c:c + NOPE], cbuf[:, CQ + k, :],
                                           start=(k == 0), stop=(k == CKV - 1))
                        mm.then_inc(*pe_s.mark(f"k{hd}"))
                    for j in range(8):
                        tok, half = j // 2, j % 2
                        pe.wait_ge(*banks.free(f"v{j}"))
                        for k in range(CKV):
                            w = rows_slot(2 + half)[:, k, :].rearrange("p (h d) -> p h d", d=NOPE + VDIM)[:, :, NOPE:]
                            mm = pe.matmul(banks.bank(f"v{j}"), cbuf[:, CQ + k, tok * P:(tok + 1) * P], w,
                                           start=(k == 0), stop=(k == CKV - 1))
                        mm.then_inc(*pe_s.mark(f"v{j}"))
                ring.uses += 5

                @block.scalar
                def _(act):
                    for hd in range(HEADS):
                        act.wait_ge(*pe_s(f"q{hd}"))
                        act.activation(q_t[0:QK, hd, :], banks.bank(f"q{hd}")[0:QK], ACT.Copy).then_inc(*act_s.mark(f"ev q{hd}"))
                    for hd in range(HEADS):
                        act.wait_ge(*pe_s(f"k{hd}"))
                        act.activation(k_t[0:NOPE, hd, :], banks.bank(f"k{hd}")[0:NOPE],
                                       ACT.Copy).then_inc(*act_s.mark(f"ev k{hd}"))

                @block.gpsimd
                def _(pool):
                    pool.tensor_tensor(raw_cos[1], kr, cos_t, ALU.mult).then_inc(*pool_s.mark("cos k"))
                    for hd in range(HEADS):
                        if hd:
                            pool.wait_ge(*dve_s("roped k" if hd == 1 else f"roped q{hd - 2}"))
                        pool.wait_ge(*act_s(f"ev q{hd}"))
                        pool.tensor_tensor(raw_cos[hd % 2], q_t[NOPE:QK, hd, :], cos_t,
                                           ALU.mult).then_inc(*pool_s.mark(f"cos q{hd}"))
                    pool.wait_ge(*dve_s("roped k"))
                    pool.tensor_copy(k_t[NOPE:QK, :, :], kr.unsqueeze(1).broadcast_to([ROPE, HEADS, SEQ])
                                     ).then_inc(*pool_s.mark("rotary key"))

                @block.vector
                def _(dve):
                    def rope(name, dst, b):
                        dve.wait_ge(*pe_s(f"rot {name}"))
                        dve.tensor_tensor(rot_sin[b], banks.bank(f"rot {name}")[NOPE:QK], sin_t,
                                          ALU.mult).then_inc(*dve_s.mark(f"ev rot {name}"))
                        dve.wait_ge(*dve_s(f"ev rot {name}"))
                        dve.wait_ge(*pool_s(f"cos {name}"))
                        dve.tensor_tensor(dst, raw_cos[b], rot_sin[b], ALU.add).then_inc(*dve_s.mark(f"roped {name}"))

                    rope("k", kr, 1)
                    for hd in range(HEADS):
                        rope(f"q{hd}", q_t[NOPE:QK, hd, :], hd % 2)
                    for j in range(8):
                        dve.wait_ge(*pe_s(f"v{j}"))
                        dve.tensor_copy(v_tok[:, j // 2, (j % 2) * 512:(j % 2 + 1) * 512],
                                        banks.bank(f"v{j}")).then_inc(*dve_s.mark(f"ev v{j}"))

        def mla_attend(layer):
            stage("attend")
            scale = 1.0 / float(np.sqrt(QK))
            NQ = SEQ // P
            blocks = [(kt, qi) for kt in (0, 1, 3, 2) for qi in range(kt, NQ)]
            turned = [lora[:, 256 + 1280 * j:1536 + 1280 * j].rearrange("p (b q) -> p b q", q=P) for j in range(2)]
            q_now = [lora[0:QK, 2816 + 512 * j:3328 + 512 * j] for j in range(2)]
            v_now = [lora[:, 3840 + 256 * j:4096 + 256 * j].rearrange("p (t d) -> p t d", d=VDIM) for j in range(2)]
            top, ntop, total, inv = (small[:, 8 * j:8 * j + 8] for j in range(4))
            with nc.Block() as block:
                @block.gpsimd
                def _(pool):
                    with pool.Fori(0, HEADS // 2) as i:
                        pool_s.start_loop(i)
                        for b in range(2):
                            pool.wait_ge(*pe_s(f"S{b}{NQ - 1}", i - 1))
                            pool.sem_inc(passed_pool, 1)
                            pool.tensor_copy(q_now[b], q_t[0:QK, i * 2 + b, :]).then_inc(*pool_s.mark(f"q{b}"))
                            pool.wait_ge(*pe_s(f"O{b}", i - 1))
                            pool.sem_inc(passed_pool, 1)
                            pool.tensor_copy(v_now[b], v_tok[:, :, bass.ds((i * 2 + b) * VDIM, VDIM)]
                                             ).then_inc(*pool_s.mark(f"v{b}"))
                        pool_s.end_loop(HEADS // 2)

                @block.tensor
                def _(pe):
                    with pe.Fori(0, HEADS // 2) as i:
                        pe_s.start_loop(i)
                        for b in range(2):
                            pe.wait_ge(*pool_s(f"q{b}", i))
                            for qi in range(NQ):
                                pe.wait_ge(*(act_s(f"exp0{qi}", i) if b else act_s(f"exp1{qi}", i - 1)))
                                n = (qi + 1) * P
                                pe.matmul(psum[:, qi, 0:n], q_now[b][:, qi * P:n], k_t[0:QK, i * 2 + b, 0:n],
                                          start=True, stop=True).then_inc(*pe_s.mark(f"S{b}{qi}"))
                        for b in range(2):
                            pe.wait_ge(*dve_s(f"p{b}{NQ - 1}", i))
                            if b:
                                pe.wait_ge(*act_s("turned02", i))
                            else:
                                pe.wait_ge(*act_s("turned12", i - 1))
                            pe.wait_ge(*dve_s("turned01", i) if b else dve_s("turned11", i - 1))
                            for j, (kt, qi) in enumerate(blocks):
                                mm = pe.transpose(psum[:, 4 + j // 4, (j % 4) * P:(j % 4 + 1) * P],
                                                  probs[:, 4 * b + qi, kt * P:(kt + 1) * P], const("ident"))
                                if j in (3, 7, 9):
                                    mm.then_inc(*pe_s.mark(f"T{b}{j // 4}"))
                            if b == 0:
                                pe.wait_ge(*act_s("O", i - 1))
                            pe.wait_ge(*pool_s(f"v{b}", i))
                            pe.wait_ge(*act_s(f"turned{b}2", i))
                            pe.wait_ge(*dve_s(f"turned{b}1", i))
                            for kt in range(NQ):
                                at = blocks.index((kt, kt))
                                mm = pe.matmul(psum[b * VDIM:(b + 1) * VDIM, 7, kt * P:SEQ], v_now[b][:, kt, :],
                                               turned[b][:, at:at + NQ - kt, :], start=(kt == 0), stop=(kt == NQ - 1))
                            mm.then_inc(*pe_s.mark(f"O{b}"))
                        pe_s.end_loop(HEADS // 2)

                @block.vector
                def _(dve):
                    with dve.Fori(0, HEADS // 2) as i:
                        dve_s.start_loop(i)
                        for b in range(2):
                            for qi in range(NQ):
                                j = 4 * b + qi
                                dve.wait_ge(*pe_s(f"S{b}{qi}", i))
                                dve.tensor_tensor(psum[:, qi, qi * P:(qi + 1) * P], psum[:, qi, qi * P:(qi + 1) * P],
                                                  causal, ALU.add).then_inc(*dve_s.mark(f"mask{j}"))
                                dve.wait_ge(*dve_s(f"mask{j}", i))
                                dve.reduce_max(top[:, j:j + 1], psum[:, qi, 0:(qi + 1) * P], AX_X
                                               ).then_inc(*dve_s.mark(f"max{j}"))
                                dve.wait_ge(*dve_s(f"max{j}", i))
                                dve.tensor_scalar(ntop[:, j:j + 1], top[:, j:j + 1], -scale, None,
                                                  ALU.mult).then_inc(*dve_s.mark(f"top{b}{qi}"))
                        for b in range(2):
                            for qi in range(NQ):
                                j = 4 * b + qi
                                dve.wait_ge(*act_s(f"exp{b}{qi}", i))
                                dve.reciprocal(inv[:, j:j + 1], total[:, j:j + 1]).then_inc(*dve_s.mark(f"inv{j}"))
                                dve.wait_ge(*dve_s(f"inv{j}", i))
                                dve.tensor_scalar(probs[:, j, 0:(qi + 1) * P], probs[:, j, 0:(qi + 1) * P],
                                                  inv[:, j:j + 1], None, ALU.mult).then_inc(*dve_s.mark(f"p{b}{qi}"))
                        for b in range(2):
                            dve.wait_ge(*pe_s(f"T{b}1", i))
                            dve.wait_ge(*pe_s(f"O{b}", i - 1))
                            dve.tensor_copy(turned[b][:, 4:8, :], psum[:, 5, :].rearrange("p (b q) -> p b q", q=P)
                                            ).then_inc(*dve_s.mark(f"turned{b}1"))
                        dve_s.end_loop(HEADS // 2)

                @block.scalar
                def _(act):
                    with act.Fori(0, HEADS // 2) as i:
                        act_s.start_loop(i)
                        for b in range(2):
                            for qi in range(NQ):
                                j = 4 * b + qi
                                act.wait_ge(*dve_s(f"top{b}{qi}", i))
                                act.wait_ge(*pe_s(f"T{b}2", i - 1))
                                act.activation(probs[:, j, 0:(qi + 1) * P], psum[:, qi, 0:(qi + 1) * P], ACT.Exp,
                                               bias=ntop[:, j:j + 1], scale=scale,
                                               accum_out=total[:, j:j + 1]).then_inc(*act_s.mark(f"exp{b}{qi}"))
                        for b in range(2):
                            for part, lo, hi in ((0, 0, 4), (2, 8, 10)):
                                act.wait_ge(*pe_s(f"T{b}{part}", i))
                                act.activation(turned[b][:, lo:hi, :],
                                               psum[:, 4 + part, 0:(hi - lo) * P].rearrange("p (b q) -> p b q", q=P),
                                               ACT.Copy).then_inc(*act_s.mark(f"turned{b}{part}"))
                        act.wait_ge(*pe_s("O1", i))
                        act.activation(o_t[:, i, :], psum[:, 7, :], ACT.Copy).then_inc(*act_s.mark("O"))
                        act_s.end_loop(HEADS // 2)

        def mla_finish(layer):
            stage("mlaout")
            banks = Banks([(f"o{t}", "dve") for t in range(NT)])
            with nc.Block() as block:
                @block.sync
                def _(sp):
                    ffn_head(sp, layer, lambda s: split.made(s))

                @block.tensor
                def _(pe):
                    gemm(pe, "o", banks, x_parts, lambda k: dve_s(f"lo{k}"), 0)

                @block.scalar
                def _(act):
                    split.make_hi(act, 0)
                    for t in range(NT):
                        act.activation(x_parts[0][:, t, :], o_t[:, t, :], ACT.Copy).then_inc(*act_s.mark(f"hi{t}"))
                    split.make_hi(act, 1)
                    for g in (2, 3):
                        act.wait_ge(*pe_s(f"o{2 * (g - 2) + 1}"))
                        split.make_hi(act, g)

                @block.vector
                def _(dve):
                    split.make_lo(dve, 0)
                    for t in range(NT):
                        dve.wait_ge(*act_s(f"hi{t}"))
                        dve.tensor_tensor(x_parts[1][:, t, :], o_t[:, t, :], x_parts[0][:, t, :].bitcast(F32),
                                          ALU.subtract).then_inc(*dve_s.mark(f"lo{t}"))
                    split.make_lo(dve, 1)
                    for t in range(NT):
                        if t in (0, 2):
                            split.make_lo(dve, 2 + t // 2)
                        dve.wait_ge(*pe_s(f"o{t}"))
                        dve.tensor_tensor(h[:, t, :], h[:, t, :], banks.bank(f"o{t}"),
                                          ALU.add).then_inc(*dve_s.mark(f"ev o{t}"))
            ring.uses += SLOTS
            split.done += SLOTS

        v_stored = sem("v_first_stored")

        def first_loads(sp):
            load_proj(sp, a["rw_wr"][0], lambda s: None)

        def conv_head(sp, last_use):
            w1 = a["cv_w1"][0].rearrange("(k p) n -> p k n", p=P)
            for s in range(SLOTS):
                c = (s // 2) * 256 + (s % 2) * DM
                ring.load(sp, cols_slot(s), w1[:, :, c:c + 256], last_use(s))

        def mla_head(sp, last_use):
            wd = a["ml_wd"][0].rearrange("(k p) n -> p k n", p=P)
            for s, w in enumerate((256, 256, P + ROPE)):
                ring.load(sp, wd_slot(s, w), wd[:, :, s * 256:s * 256 + w], last_use(s))

        last = lambda layer: ffn_last_use(layer)
        begin()
        rwkv_project(0, 0)
        rwkv_scan(0)
        rwkv_finish(0, 0)
        ffn(0, lambda sp: conv_head(sp, last(0)))
        conv_glu(1)
        conv_taps()
        conv_finish(1)
        ffn(1, lambda sp: mla_head(sp, last(1)))
        mla_down(2)
        mla_up(2)
        mla_attend(2)
        mla_finish(2)
        ffn(2, lambda sp: load_proj(sp, a["rw_wr"][1], last(2)))
        rwkv_project(3, 1)
        rwkv_scan(1)
        rwkv_finish(3, 1)
        ffn(3, lambda sp: None)
        end()
        for n, s in everyone.items():
            new[n] = s.new
    return new


IN_NAMES = ["x", "consts", "extras"] + [n for g in VECTORS for n, _ in g] + [
    "positions", "cv_dw", "cv_w1", "cv_w2", "ml_wd", "ml_wuq", "ml_wukv", "ml_wo",
    "rw_wr", "rw_wk", "rw_wv", "rw_wo", "rw_w1", "rw_w2", "rw_a1", "rw_a2", "rw_g1", "rw_g2", "rw_v1", "rw_v2", "ff_w1", "ff_w2"]

def kernel(**inputs):
    import numpy as _np
    import concourse.bacc as _bacc
    from concourse.bass_utils import run_bass_kernel_spmd as _run

    known = {}
    for _pass in range(2):
        nc = _bacc.Bacc("TRN2", target_bir_lowering=False, num_devices=1, dynamic_dma_scratch_size=1024)
        arrays, args = {}, {}
        consts, extras = constants()
        given = dict(inputs, consts=consts, extras=extras)
        for name in IN_NAMES:
            arr = _np.ascontiguousarray(given[name])
            arrays[f"in_{name}"] = arr
            args[name] = nc.dram_tensor(f"in_{name}", arr.shape, mybir.dt.from_np(arr.dtype), kind="ExternalInput").ap()
        args["out"] = nc.dram_tensor("out_0", (1, SEQ, DM), F32, kind="ExternalOutput").ap()
        args["v_first"] = nc.dram_tensor("v_first", (P, NT * SEQ), F32, kind="Internal").ap()
        known = build(nc, args, known)
    r = _run(nc, [arrays], core_ids=[0])
    return r.results[0]["out_0"]
```

```python
from contextlib import ExitStack

import numpy as np

import concourse.bass as bass
from concourse import mybir

F32 = mybir.dt.float32
F32R = mybir.dt.float32r
I32 = mybir.dt.int32
ALU = mybir.AluOpType
ACT = mybir.ActivationFunctionType
AX_X = mybir.AxisListType.X

P = 128
SEQ, DM, DEPTH = 512, 1024, 4
NT = DM // P
HEAD = 64
CH = 64
NCH = SEQ // CH
LORA_W, LORA_A, LORA_V, LORA_G = 64, 64, 32, 128
TAPS = 31
PAD = TAPS - 1
D_FF = 4 * DM
FT = D_FF // P
HEADS, NOPE, ROPE, VDIM = 16, 64, 32, 64
QK = NOPE + ROPE
Q_LORA, KV_LORA = 384, 256
NORM_EPS, GN_EPS = 1e-5, 64e-5
DECAY = float(np.exp(-0.5))
TWO_PI = 2.0 * np.pi
PI_BELOW = float(np.nextafter(np.float32(np.pi), np.float32(0)))
TURNS = D_FF // DM
PE_TAPS, ACT_TAPS = 12, 8

SLOTS = 4
SLOT = 2048

VECTORS = [
    [("rw_mu", 96), ("norm_mix", 32)],
    [("norm_ffn", 32), ("norm_final", 8), ("rw_w0", 16), ("rw_a0", 16), ("rw_kk", 16), ("rw_ka", 16),
     ("rw_rk", 16), ("rw_v0", 8)],
    [("rw_lnx_w", 16), ("rw_lnx_b", 16), ("cv_b1", 16), ("cv_bdw", 8), ("cv_ln_w", 8), ("cv_ln_b", 8),
     ("cv_b2", 8), ("ml_gq", 3), ("ml_gkv", 2)],
]
VEC_ROW = {}
for _g, _names in enumerate(VECTORS):
    _r = 0
    for _n, _k in _names:
        VEC_ROW[_n] = (_g, _r, _k)
        _r += _k

CONSTS = {}
_at = 0
for _n, _w in [("ident", P), ("ones", P), ("pair", P), ("mask_g", P), ("mask_dt", CH),
               ("mask_et", CH), ("eye2", CH), ("cols", 8), ("pick", 30)]:
    CONSTS[_n] = (_at, _w)
    _at += _w
CONST_W = _at


def constants():
    c = np.zeros((P, CONST_W), np.float32)

    def put(name, a):
        at, w = CONSTS[name]
        c[: a.shape[0], at:at + w] = a

    p, f = np.arange(P)[:, None], np.arange(P)[None, :]
    put("ident", np.eye(P))
    put("ones", np.ones((P, P)))
    put("pair", (p // HEAD == f // HEAD) * 1.0)
    j, i = p % CH, f % CH
    put("mask_g", np.where(f < CH, (p >= CH) & (j < i), j <= i) * 1.0)
    i2, j2 = np.arange(P)[:, None] % CH, np.arange(CH)[None, :]
    put("mask_dt", ((i2 < j2) & (j2 // 16 == i2 // 16)) * 1.0)
    put("mask_et", (i2 // 16 < j2 // 16) * 1.0)
    put("eye2", (i2 == j2) * 1.0)
    put("pick", (np.arange(30)[None, :] - 14 == p // HEAD) * 1.0)
    t = np.zeros((P, ROPE))
    for k in range(ROPE // 2):
        t[NOPE + ROPE // 2 + k, k] = -1.0
        t[NOPE + k, ROPE // 2 + k] = 1.0
    cols = np.zeros((P, 8))
    cols[:, 0] = NORM_EPS
    cols[:, 1] = GN_EPS
    freq = np.float32(10000.0) ** (-np.arange(0, ROPE, 2, dtype=np.float32) / np.float32(ROPE))
    cols[NOPE:NOPE + ROPE, 2] = np.tile(freq, 2)
    cols[:, 3] = np.pi / 2
    put("cols", cols)
    reset = np.ones((P, SEQ), np.float32)
    reset[:, ::CH] = 0.0
    spread = np.zeros((P, DM))
    spread[0:HEADS] = np.arange(DM)[None, :] // HEAD == np.arange(HEADS)[:, None]
    return c, np.concatenate([np.where(f <= p, 0.0, -1e30), t, reset, spread], axis=1).astype(np.float32)


class Steps:

    def __init__(self, sem, known):
        self.sem, self.known, self.new = sem, known, {}
        self.count, self.loop_base, self.reg, self.per, self.stage = 0, None, None, 0, ""

    def mark(self, name):
        self.count += 1
        key = (self.stage, name)
        assert key not in self.new, key
        self.new[key] = (self.count, self.loop_base)
        return self.sem, 1

    def start_loop(self, reg):
        self.loop_base, self.reg = self.count, reg

    def end_loop(self, n):
        per = self.count - self.loop_base
        self.new[("per", self.loop_base)] = (per, None)
        self.count += per * (n - 1)
        self.loop_base = self.reg = None

    def at(self, name, i=None, stage=None):
        value, base = self.known.get((stage or self.stage, name), (None, None))
        if value is None:
            assert not self.known, (stage or self.stage, name)
            return 1
        if base is None or i is None:
            return value
        return i * self.known[("per", base)][0] + value

    def __call__(self, name, i=None, stage=None):
        return self.sem, self.at(name, i, stage)


class Ring:

    def __init__(self, buf, landed):
        self.buf, self.landed = buf, landed
        self.loads = self.uses = 0

    def slot(self, s):
        return self.buf[:, s % SLOTS, :]

    def load(self, sp, view, src, last_use):
        if last_use:
            sp.wait_ge(*last_use)
        sp.dma_start(view, src).then_inc(self.landed[self.loads % SLOTS], 16)
        self.loads += 1


class Split:

    def __init__(self, hi, lo, hi_made, lo_made, ring):
        self.bufs, self.hi_made, self.lo_made, self.ring = (hi, lo), hi_made, lo_made, ring
        self.done = 0

    def make_hi(self, act, g, i=0, per=0):
        r = self.ring
        act.wait_ge(r.landed[(r.uses + g) % SLOTS], 16 * (i * (per // SLOTS) + (r.uses + g) // SLOTS + 1))
        act.activation(self.bufs[0][:, g % 2, :], r.slot(r.uses + g), ACT.Copy).then_inc(self.hi_made, 1)

    def make_lo(self, dve, g, i=0, per=0):
        dve.wait_ge(self.hi_made, i * per + (self.done + g + 1))
        hi, lo = (b[:, g % 2, :] for b in self.bufs)
        dve.tensor_tensor(lo, self.ring.slot(self.ring.uses + g), hi.bitcast(F32),
                          ALU.subtract).then_inc(self.lo_made, 1)

    def made(self, g, i=0, per=0):
        return self.lo_made, i * per + (self.done + g + 1)

    def three(self, pe, out, g, view, cols, x, start, stop):
        (wh, wl), (xh, xl) = (view(b[:, g % 2, :])[cols] for b in self.bufs), x
        pe.matmul(out, wh, xh, start=start, stop=False, skip_group_check=True)
        pe.matmul(out, wh, xl, start=False, stop=False, skip_group_check=True)
        return pe.matmul(out, wl, xh, start=False, stop=stop, skip_group_check=True)


def build(nc, a, known):
    ctx = ExitStack()
    new = {}
    with ctx:
        def sb(name, shape, dt=F32):
            return ctx.enter_context(nc.sbuf_tensor(name, shape, dt))

        def sem(name):
            return ctx.enter_context(nc.semaphore(name))

        arena_at = -(-nc.sbuf_base // 32) * 32
        arena = sb("arena", [P, 10, NT * SEQ])
        ring_buf = sb("ring", [P, SLOTS, SLOT])
        lora_at = -(-nc.sbuf_base // 32) * 32
        lora = sb("lora", [P, 5120])
        small = sb("small", [P, 1536])
        vec = sb("vec", [P, 3 * P])
        cst = sb("cst", [P, CONST_W])
        one_less_mu = sb("one_less_mu", [P, 6 * NT])
        one_less_ka = vec[:, 3 * P - NT:3 * P]
        psum = ctx.enter_context(nc.psum_tensor("psum", [P, 8, 512], F32))

        def region(k):
            return arena[:, k, :].rearrange("p (t s) -> p t s", s=SEQ)

        def const(name, rows=P):
            at, w = CONSTS[name]
            return cst[0:rows, at:at + w]

        def col(name, j):
            g, r, _ = VEC_ROW[name]
            return vec[:, g * P + r + j:g * P + r + j + 1]

        eps = cst[:, CONSTS["cols"][0]:CONSTS["cols"][0] + 1]
        gn_eps = cst[:, CONSTS["cols"][0] + 1:CONSTS["cols"][0] + 2]
        def placed(name, k, shape):
            return nc.alloc_sbuf_tensor_at(name, shape, F32R, offset=arena_at + k * NT * SEQ * 4)

        x_parts = tuple(placed(f"x_{e}", k, [P, NT, SEQ])[:] for e, k in (("hi", 3), ("lo", 4)))
        hid_parts = tuple(placed(f"hid_{e}", k, [P, NT, SEQ])[:] for e, k in (("hi", 1), ("lo", 2)))
        xk_parts = (placed("xk_hi", 7, [P, NT, SEQ])[:],
                    nc.alloc_sbuf_tensor_at("xk_lo", [P, NT, SEQ], F32R, offset=lora_at)[:])

        def tiles_at_slots(name, k):
            return placed(name, k, [P, 2, SLOT])[:]

        rstd = small[:, 0:512]
        low = [small[:, 512:1024], small[:, 1024:1536]]

        pe_s = Steps(sem("pe_steps"), known.get("pe", {}))
        act_s = Steps(sem("act_steps"), known.get("act", {}))
        dve_s = Steps(sem("dve_steps"), known.get("dve", {}))
        pool_s = Steps(sem("pool_steps"), known.get("pool", {}))
        everyone = {"pe": pe_s, "act": act_s, "dve": dve_s, "pool": pool_s}

        landed = [sem(f"weights_landed{s}") for s in range(SLOTS)]
        ring = Ring(ring_buf, landed)
        in_landed = sem("inputs_landed")
        out_landed = sem("outputs_landed")
        ins = {"n": 0}

        h, u = region(0), region(1)
        split = Split(tiles_at_slots("w_hi", 8), tiles_at_slots("w_lo", 9), sem("weights_hi"), sem("weights_lo"), ring)

        def stage(name):
            for s in everyone.values():
                s.stage = name

        passed_pe, passed_pool = sem("passed_pe"), sem("passed_pool")

        class Banks:

            def __init__(self, jobs):
                self.names = [n for n, _ in jobs]
                self.who = dict(jobs)

            def bank(self, name):
                return psum[:, self.names.index(name) % 8, :]

            def free(self, name):
                k = self.names.index(name) - 8
                if k < 0:
                    return None
                before = self.names[k]
                return (act_s if self.who[before] == "act" else dve_s)("ev " + before)

        def bring(eng, dst, src):
            eng.dma_start(dst, src).then_inc(in_landed, 16)
            ins["n"] += 16

        groups = {}

        def bring_group(eng, group, dst, src):
            if group not in groups:
                groups[group] = [sem(f"{group}_landed"), 0]
            groups[group][1] += 16
            eng.dma_start(dst, src).then_inc(groups[group][0], 16)

        def landed_group(group):
            return tuple(groups[group])

        def norm_act(act, tag, src, sq, scale=1.0 / DM, tiles=NT, meanwhile=None):
            for t in range(tiles):
                act.activation(sq[:, t, :], src[:, t, :], ACT.Square).then_inc(*act_s.mark(f"{tag} sq{t}"))
            if meanwhile:
                meanwhile()
            act.wait_ge(*pe_s(f"{tag} sum"))
            act.activation(rstd, psum[:, 7, :], ACT.Sqrt, bias=eps, scale=scale).then_inc(*act_s.mark(f"{tag} root"))

        def norm_pe(pe, tag, sq, tiles=NT):
            for t in range(tiles):
                pe.wait_ge(*act_s(f"{tag} sq{t}"))
                mm = pe.matmul(psum[:, 7, :], const("ones"), sq[:, t, :], start=(t == 0), stop=(t == tiles - 1))
            mm.then_inc(*pe_s.mark(f"{tag} sum"))

        def norm_dve(dve, tag, src, dst, gain, tiles=NT):
            dve.wait_ge(*act_s(f"{tag} root"))
            dve.reciprocal(rstd, rstd).then_inc(*dve_s.mark(f"{tag} rstd"))
            dve.wait_ge(*dve_s(f"{tag} rstd"))
            for t in range(tiles):
                dve.scalar_tensor_tensor(dst[:, t, :], src[:, t, :], gain(t), rstd, ALU.mult,
                                         ALU.mult).then_inc(*dve_s.mark(f"{tag} out{t}"))

        def fold_act(act, gain, sq):
            for t in range(NT):
                act.activation(x_parts[0][:, t, :], h[:, t, :], ACT.Copy, scale=gain(t)).then_inc(*act_s.mark(f"x{t}"))
                act.activation(sq[:, t, :], h[:, t, :], ACT.Square).then_inc(*act_s.mark(f"sq{t}"))

        def fold_root(act):
            act.wait_ge(*pe_s("sum"))
            act.activation(rstd, psum[:, 7, :], ACT.Sqrt, bias=eps, scale=1.0 / DM).then_inc(*act_s.mark("root"))

        def fold_dve(dve, gain):
            for t in range(NT):
                dve.wait_ge(*act_s(f"x{t}"))
                dve.scalar_tensor_tensor(x_parts[1][:, t, :], h[:, t, :], gain(t), x_parts[0][:, t, :].bitcast(F32),
                                         ALU.mult, ALU.subtract).then_inc(*dve_s.mark(f"x{t}"))

        def fold_rstd(dve):
            dve.wait_ge(*act_s("root"))
            dve.reciprocal(rstd, rstd).then_inc(*dve_s.mark("rstd"))
            dve.wait_ge(*dve_s("rstd"))

        def fold_pool(pool, sq, total):
            for t in range(1, NT):
                pool.wait_ge(*act_s(f"sq{t}"))
                if t > 1:
                    pool.wait_ge(*pool_s(f"total{t - 1}"))
                pool.tensor_tensor(total, sq[:, 0, :] if t == 1 else total, sq[:, t, :],
                                   ALU.add).then_inc(*pool_s.mark(f"total{t}"))

        def fold_pe(pe, total):
            pe.wait_ge(*pool_s(f"total{NT - 1}"))
            pe.matmul(psum[:, 7, :], const("ones"), total, start=True, stop=True).then_inc(*pe_s.mark("sum"))

        def cols_slot(s):
            return ring.slot(s).rearrange("p (k n) -> p k n", n=256)

        def by_cols(x):
            return x.rearrange("p (k n) -> p k n", n=256)

        def by_rows(x):
            return x.rearrange("p (k n) -> p k n", n=DM)

        def rows_slot(s):
            return ring.slot(s).rearrange("p (k n) -> p k n", n=DM)

        def load_proj(sp, w, last_use, slots=range(SLOTS)):
            wv = w.rearrange("(k p) n -> p k n", p=P)
            for s in slots:
                ring.load(sp, cols_slot(s), wv[:, :, s * 256:(s + 1) * 256], last_use(s))

        def ffn_head(sp, layer, last_use):
            load_proj(sp, a["ff_w1"][layer][:, 0:SLOTS * 256], last_use)

        def ffn_body(sp, layer):
            w1 = a["ff_w1"][layer].rearrange("(k p) n -> p k n", p=P)
            w2 = a["ff_w2"][layer].rearrange("(c k p) n -> p c k n", p=P, k=2)
            with sp.Fori(0, TURNS - 1) as i:
                for s in range(SLOTS):
                    ring.load(sp, rows_slot(s), w2[:, i * SLOTS + s, :, :], split.made(s, i, 2 * SLOTS))
                for s in range(SLOTS):
                    ring.load(sp, cols_slot(s), w1[:, :, bass.ds((i * SLOTS + (SLOTS + s)) * 256, 256)],
                              split.made(SLOTS + s, i, 2 * SLOTS))
            for s in range(SLOTS):
                ring.load(sp, rows_slot(s), w2[:, (TURNS - 1) * SLOTS + s, :, :],
                          split.made(2 * SLOTS * (TURNS - 1) + s))
            ring.loads += 2 * SLOTS * (TURNS - 2)

        def ffn_last_use(layer):
            return lambda s: split.made(2 * SLOTS * (TURNS - 1) + SLOTS + s)

        def slot_landed(pe, s, i=0):
            pe.wait_ge(landed[(ring.uses + s) % SLOTS], 16 * (i + (ring.uses + s) // SLOTS + 1))


        def begin():
            stage("begin")
            x_in = arena[:, 2, :].rearrange("p (t d) -> p t d", d=DM)
            rows = arena[:, 3, 0:3 * P].rearrange("p (g c) -> p g c", c=P)
            with nc.Block() as block:
                @block.sync
                def _(sp):
                    bring(sp, cst[:], a["consts"])
                    bring(sp, x_in, a["x"][0].rearrange("(t p) d -> p t d", p=P))
                    for name, (g, r, k) in VEC_ROW.items():
                        src = a[name]
                        pat = {1: "(r c) -> r c", 2: "l (r c) -> (l r) c", 3: "l m (r c) -> (l m r) c"}[len(src.shape)]
                        if name == "rw_rk":
                            src, pat = src.rearrange("l h n -> l (h n)"), "l (r c) -> (l r) c"
                        bring(sp, rows[r:r + k, g, :], src.rearrange(pat, c=P))
                    first_loads(sp)

                @block.gpsimd
                def _(pool):
                    pool.memset(lora[:], 0.0).then_inc(*pool_s.mark("clear"))

                @block.tensor
                def _(pe):
                    pe.wait_ge(in_landed, ins["n"])
                    for g, names in enumerate(VECTORS):
                        r = sum(k for _, k in names)
                        mm = pe.transpose(psum[:, 7, g * P:g * P + r], rows[0:r, g, :], cst[0:r, 0:r])
                    mm.then_inc(*pe_s.mark("vectors"))
                    for t in range(NT):
                        if t == 7:
                            pe.wait_ge(*act_s("vectors"))
                        for q in range(SEQ // P):
                            mm = pe.transpose(psum[:, t, q * P:(q + 1) * P], x_in[:, q, t * P:(t + 1) * P], const("ident"))
                        mm.then_inc(*pe_s.mark(f"x{t}"))

                @block.scalar
                def _(act):
                    act.wait_ge(*pe_s("vectors"))
                    for g, names in enumerate(VECTORS):
                        r = sum(k for _, k in names)
                        op = act.activation(vec[:, g * P:g * P + r], psum[:, 7, g * P:g * P + r], ACT.Copy)
                    op.then_inc(*act_s.mark("vectors"))
                    for t in range(0, NT, 2):
                        act.wait_ge(*pe_s(f"x{t}"))
                        act.activation(h[:, t, :], psum[:, t, :], ACT.Copy).then_inc(*act_s.mark(f"ev x{t}"))

                @block.vector
                def _(dve):
                    for t in range(1, NT, 2):
                        dve.wait_ge(*pe_s(f"x{t}"))
                        dve.tensor_copy(h[:, t, :], psum[:, t, :]).then_inc(*dve_s.mark(f"ev x{t}"))

        def ffn(layer, next_loads):
            stage(f"ffn{layer}")
            sq, total, scaled, square = region(5), region(6)[:, 0, :], region(6)[:, 2:4, :], region(7)
            per = 2 * SLOTS
            hh, hl = hid_parts
            gain = lambda t: col("norm_ffn", layer * NT + t)
            part = lambda x, k: (x[0][:, k, :], x[1][:, k, :])

            with nc.Block() as block:
                @block.sync
                def _(sp):
                    ffn_body(sp, layer)
                    next_loads(sp)

                @block.gpsimd
                def _(pool):
                    fold_pool(pool, sq, total)

                @block.tensor
                def _(pe):
                    def up(pre, g0, i, now):
                        for s in range(SLOTS):
                            pe.wait_ge(*split.made(g0 + s, i, per))
                            order = [(n, k) for n in range(2) for k in range(NT)]
                            if pre and s == 0:
                                order = [(n, k) for k in range(NT) for n in range(2)]
                            for n, k in order:
                                b = 2 * s + n
                                if pre and s == 0 and n == 0:
                                    pe.wait_ge(*dve_s(f"x{k}"))
                                if pre and b == 7 and k == 0:
                                    pe.wait_ge(*act_s("root"))
                                if not pre and k == 0:
                                    pe.wait_ge(*dve_s(f"add{b}", now))
                                mm = split.three(pe, psum[:, b, :], g0 + s, by_cols,
                                                 np.s_[:, k, n * P:(n + 1) * P], part(x_parts, k), k == 0, k == NT - 1)
                                if k == NT - 1:
                                    mm.then_inc(*pe_s.mark(f"{pre}up{b}"))
                            if pre and s == 0:
                                fold_pe(pe, total)

                    def down(pre, g0, i, before):
                        for s in range(SLOTS):
                            pe.wait_ge(*split.made(g0 + s, i, per))
                            for k in range(2):
                                pe.wait_ge(*dve_s(f"hid{2 * s + k}", before))
                                for n in range(NT):
                                    if s == 0 and k == 0:
                                        pe.wait_ge(*dve_s(f"scaled{n}", before))
                                    last = s == SLOTS - 1 and k == 1
                                    mm = split.three(pe, psum[:, n, :], g0 + s, by_rows,
                                                     np.s_[:, k, n * P:(n + 1) * P], part(hid_parts, 2 * s + k),
                                                     s == 0 and k == 0, last)
                                    if last:
                                        mm.then_inc(*pe_s.mark(f"{pre}out{n}"))
                            if s < SLOTS - 1:
                                mm.then_inc(*pe_s.mark(f"{pre}down{s}"))

                    up("first ", 0, 0, None)
                    with pe.Fori(0, TURNS - 1) as i:
                        pe_s.start_loop(i)
                        down("", SLOTS, i, i - 1)
                        up("", per, i, i)
                        pe_s.end_loop(TURNS - 1)
                    down("last ", SLOTS + per * (TURNS - 1), 0, TURNS - 2)

                @block.scalar
                def _(act):
                    def up(pre, g0, i, now):
                        for s in range(SLOTS):
                            if not (pre and s == 1):
                                if s == 0 and not pre:
                                    act.wait_ge(*pe_s("out7", now))
                                elif s:
                                    act.wait_ge(*pe_s(f"{pre}up{2 * s - 1}", now))
                                split.make_hi(act, g0 + s + 1, i, per)
                            if pre and s == 0:
                                act.wait_ge(*pe_s(f"{pre}up1"))
                                split.make_hi(act, g0 + 2)
                                fold_root(act)
                            for b in (2 * s, 2 * s + 1):
                                act.wait_ge(*dve_s(f"{pre}square{b}", now))
                                act.activation(hh[:, b, :], square[:, b, :],
                                               ACT.Copy).then_inc(*act_s.mark(f"{pre}hid{b}"))

                    def down(pre, g0, i, before):
                        for s in range(SLOTS - (pre == "last " and layer == DEPTH - 1)):
                            act.wait_ge(*(pe_s(f"{pre}down{s - 1}", None if pre else i) if s else pe_s("up7", before)))
                            split.make_hi(act, g0 + s + 1, i, per)

                    fold_act(act, gain, sq)
                    up("first ", 0, 0, None)
                    with act.Fori(0, TURNS - 1) as i:
                        act_s.start_loop(i)
                        down("", SLOTS, i, i - 1)
                        up("", per, i, i)
                        act_s.end_loop(TURNS - 1)
                    down("last ", SLOTS + per * (TURNS - 1), 0, TURNS - 2)

                @block.vector
                def _(dve):
                    def rest(pre, b, now):
                        dve.wait_ge(*act_s(f"{pre}hid{b}", now))
                        dve.tensor_tensor(hl[:, b, :], square[:, b, :], hh[:, b, :].bitcast(F32),
                                          ALU.subtract).then_inc(*dve_s.mark(f"{pre}hid{b}"))

                    def up(pre, g0, i, now):
                        for s in range(SLOTS):
                            if not (pre and s == 1):
                                split.make_lo(dve, g0 + s + 1, i, per)
                            if pre and s == 0:
                                split.make_lo(dve, g0 + 2)
                                fold_rstd(dve)
                            for b in (2 * s, 2 * s + 1):
                                dve.wait_ge(*pe_s(f"{pre}up{b}", now))
                                dve.tensor_tensor(scaled[:, b % 2, :], psum[:, b, :], rstd,
                                                  ALU.mult).then_inc(*dve_s.mark(f"{pre}scaled{b}"))
                                dve.wait_ge(*dve_s(f"{pre}scaled{b}", now))
                                dve.scalar_tensor_tensor(square[:, b, :], scaled[:, b % 2, :], 0.0, scaled[:, b % 2, :],
                                                         ALU.max, ALU.mult).then_inc(*dve_s.mark(f"{pre}square{b}"))
                                if b:
                                    rest(pre, b - 1, now)
                        rest(pre, 7, now)

                    def down(pre, g0, i, now):
                        for s in range(SLOTS - (pre == "last " and layer == DEPTH - 1)):
                            split.make_lo(dve, g0 + s + 1, i, per)
                        for n in range(NT):
                            dve.wait_ge(*pe_s(f"{pre}out{n}", now))
                            dve.tensor_tensor(h[:, n, :], h[:, n, :], psum[:, n, :],
                                              ALU.add).then_inc(*dve_s.mark(f"{pre}add{n}"))

                    fold_dve(dve, gain)
                    up("first ", 0, 0, None)
                    with dve.Fori(0, TURNS - 1) as i:
                        dve_s.start_loop(i)
                        down("", SLOTS, i, i)
                        up("", per, i, i)
                        dve_s.end_loop(TURNS - 1)
                    down("last ", SLOTS + per * (TURNS - 1), 0, None)
            ring.uses += per * TURNS
            split.done += per * TURNS

        def end():
            stage("end")
            sq = region(6)
            out_sb = arena[:, 2, :].rearrange("p (t d) -> p t d", d=DM)
            with nc.Block() as block:
                @block.tensor
                def _(pe):
                    norm_pe(pe, "n", sq)
                    for q in range(SEQ // P):
                        for half in range(2):
                            j = 2 * q + half
                            if j == 7:
                                pe.wait_ge(*act_s("n root"))
                            for t in range(4):
                                pe.wait_ge(*dve_s(f"n out{4 * half + t}"))
                                mm = pe.transpose(psum[:, j, t * P:(t + 1) * P],
                                                  u[:, 4 * half + t, q * P:(q + 1) * P], const("ident"))
                            mm.then_inc(*pe_s.mark(f"y{j}"))

                @block.scalar
                def _(act):
                    norm_act(act, "n", h, sq)
                    for j in range(0, 8, 2):
                        act.wait_ge(*pe_s(f"y{j}"))
                        act.activation(out_sb[:, j // 2, 0:512], psum[:, j, :], ACT.Copy).then_inc(*act_s.mark(f"y{j}"))

                @block.vector
                def _(dve):
                    norm_dve(dve, "n", h, u, lambda t: col("norm_final", t))
                    for j in range(1, 8, 2):
                        dve.wait_ge(*pe_s(f"y{j}"))
                        dve.tensor_copy(out_sb[:, j // 2, 512:1024], psum[:, j, :]).then_inc(*dve_s.mark(f"y{j}"))

                @block.sync
                def _(sp):
                    for q in range(SEQ // P):
                        sp.wait_ge(*act_s(f"y{2 * q}"))
                        sp.wait_ge(*dve_s(f"y{2 * q + 1}"))
                        sp.dma_start(a["out"][0, q * P:(q + 1) * P, :], out_sb[:, q, :]).then_inc(out_landed, 16)
                    sp.wait_ge(out_landed, 16 * (SEQ // P))

        def gemm(pe, tag, banks, x, ready, g0, first=True, after=None):
            for s in range(SLOTS):
                pe.wait_ge(*split.made(g0 + s))
                order = [(n, k) for n in range(2) for k in range(NT)]
                if s == 0 and first:
                    order = [(n, k) for k in range(NT) for n in range(2)]
                for n, k in order:
                    job = f"{tag}{2 * s + n}"
                    if k == 0 and banks.free(job):
                        pe.wait_ge(*banks.free(job))
                    if s == 0 and n == 0:
                        pe.wait_ge(*ready(k))
                    mm = split.three(pe, banks.bank(job), g0 + s, by_cols, np.s_[:, k, n * P:(n + 1) * P],
                                     (x[0][:, k, :], x[1][:, k, :]), k == 0, k == NT - 1)
                    if k == NT - 1:
                        mm.then_inc(*pe_s.mark(job))
                if after:
                    after(s)

        def rwkv_jobs(second):
            eight = lambda tag, who="act": [(f"{tag}{n}", who) for n in range(NT)]
            jobs = eight("r") + eight("k") + eight("v")
            jobs[18:18] = [("kk sum", "dve")]
            jobs += [("w low", "act")] + eight("w")
            if second:
                jobs += [("v low", "act")] + eight("vmix")
            jobs += [("a low", "act")] + eight("a") + eight("kk inv", "dve") + [("g low", "act")] + eight("g")
            return jobs

        MIX = {"r": 0, "w": 1, "k": 2, "v": 3, "a": 4, "g": 5}

        def pick(t):
            at = CONSTS["pick"][0] + 14 - 2 * t
            return cst[:, at:at + HEADS]

        def rwkv_project(layer, m):
            stage(f"project{m}")
            second = m > 0
            r, k, v, lw, av = (region(j) for j in range(5, 10))
            gate, kkn, sq = region(2), u, region(6)
            parts = {"r": x_parts, "k": xk_parts, "v": x_parts}
            mixed = {"w": region(2), "a": region(3), "g": region(4)}
            tmp = low
            kk_sq = [lora[:, 4096:4608], lora[:, 4608:5120]]
            kk_inv = rstd[0:HEADS, :]
            k_factor = region(3)
            low_v = gate[:, 0:2, :]
            flat = arena[:, 2, :]
            v1 = flat[:, 1024:1280].rearrange("p (k n) -> p k n", n=LORA_V)
            resets = flat[:, 1280:1792]
            v2 = flat[0:LORA_V, 1792:2816]
            spread = flat[0:HEADS, 2816:3840]
            w1 = lora[:, 0:512].rearrange("p (k n) -> p k n", n=LORA_W)
            a1 = lora[:, 512:1024].rearrange("p (k n) -> p k n", n=LORA_A)
            g1 = lora[:, 1024:2048].rearrange("p (k n) -> p k n", n=LORA_G)
            w2, a2 = lora[0:LORA_W, 2048:3072], lora[0:LORA_A, 3072:4096]
            g2 = lora[:, 4096:5120]
            banks = Banks(rwkv_jobs(second))
            order = "rkvw"
            mu0 = VEC_ROW["rw_mu"][1] + m * 6 * NT
            ka0 = VEC_ROW["rw_ka"][0] * P + VEC_ROW["rw_ka"][1] + m * NT

            def before_tmp(p, t):
                return f"lo {p}{t - 2}" if t >= 2 else f"lo {order[order.index(p) - 1]}{t + 6}"

            with nc.Block() as block:
                @block.sync
                def _(sp):
                    km = lambda w: w.rearrange("(k p) n -> p k n", p=P)
                    load_proj(sp, a["rw_wk"][m], lambda s: split.made(s))
                    load_proj(sp, a["rw_wv"][m], lambda s: split.made(SLOTS + s))
                    sp.wait_ge(*pe_s("k7"))
                    for dst, name in ((w1, "rw_w1"), (a1, "rw_a1"), (g1, "rw_g1")):
                        bring_group(sp, "narrow", dst, km(a[name][m]))
                    bring_group(sp, "narrow", w2, a["rw_w2"][m])
                    bring_group(sp, "narrow", a2, a["rw_a2"][m])
                    load_proj(sp, a["rw_wo"][m], lambda s: split.made(2 * SLOTS + s), range(SLOTS - 1))
                    sp.wait_ge(*pe_s("kk part7"))
                    bring_group(sp, "g2", g2, a["rw_g2"][m])
                    if second:
                        bring_group(sp, "v_first", av, a["v_first"].rearrange("p (t s) -> p t s", s=SEQ))
                    sp.wait_ge(*pe_s("w low"))
                    if second:
                        bring_group(sp, "extra", v1, km(a["rw_v1"][0]))
                        bring_group(sp, "extra", v2, a["rw_v2"][0])
                    bring_group(sp, "extra", resets, a["extras"][:, P + ROPE:P + ROPE + SEQ])
                    bring_group(sp, "extra", spread, a["extras"][0:HEADS, P + ROPE + SEQ:])
                    if not second:
                        sp.wait_ge(*act_s(f"ev v{NT - 1}"))
                        sp.dma_start(a["v_first"].rearrange("p (t s) -> p t s", s=SEQ), v).then_inc(v_stored, 16)
                        sp.wait_ge(v_stored, 16)

                @block.tensor
                def _(pe):
                    norm_pe(pe, "n", sq)

                    def low_rank(job, w, x, rows, ready):
                        pe.wait_ge(*banks.free(job))
                        for kt in range(NT):
                            if ready:
                                pe.wait_ge(*ready(kt))
                            for j, xj in enumerate(x):
                                mm = pe.matmul(banks.bank(job)[0:rows], w[:, kt, :], xj[:, kt, :],
                                               start=(kt == 0 and j == 0), stop=(kt == NT - 1 and j == len(x) - 1))
                        mm.then_inc(*pe_s.mark(job))

                    def widen(tag, low_job, w, x):
                        pe.wait_ge(*act_s(f"ev {low_job}"))
                        for n in range(NT):
                            job = f"{tag}{n}"
                            pe.wait_ge(*banks.free(job))
                            pe.matmul(banks.bank(job), w[:, n * P:(n + 1) * P], x,
                                      start=True, stop=True).then_inc(*pe_s.mark(job))

                    def kk_sums(s):
                        if s == 0:
                            pe.wait_ge(*banks.free("kk sum"))
                        for t in (2 * s, 2 * s + 1):
                            pe.wait_ge(*act_s(f"kk sq{t}"))
                            pe.matmul(banks.bank("kk sum")[0:HEADS], pick(t), kk_sq[t % 2], start=(t == 0),
                                      stop=(t == NT - 1), skip_group_check=True).then_inc(*pe_s.mark(f"kk part{t}"))

                    for q, p in enumerate("rkv"):
                        gemm(pe, p, banks, parts[p], lambda kt: dve_s(f"lo {p}{kt}"), SLOTS * q, q == 0,
                             kk_sums if p == "v" else None)
                    pe.wait_ge(*landed_group("narrow"))
                    low_rank("w low", w1, [mixed["w"]], LORA_W, lambda kt: dve_s(f"mix w{kt}"))
                    widen("w", "w low", w2, low[1][0:LORA_W, :])
                    pe.wait_ge(*landed_group("extra"))
                    if second:
                        low_rank("v low", v1, [x.bitcast(F32) for x in parts["v"]], LORA_V, None)
                        widen("vmix", "v low", v2, low[0][0:LORA_V, :])
                    low_rank("a low", a1, [mixed["a"]], LORA_A, lambda kt: dve_s(f"mix a{kt}"))
                    widen("a", "a low", a2, low[0][0:LORA_A, :])
                    pe.wait_ge(*dve_s("kk inv"))
                    for t in range(NT):
                        pe.wait_ge(*banks.free(f"kk inv{t}"))
                        pe.matmul(banks.bank(f"kk inv{t}"), spread[:, t * P:(t + 1) * P], kk_inv,
                                  start=True, stop=True).then_inc(*pe_s.mark(f"kk inv{t}"))
                    low_rank("g low", g1, [mixed["g"]], LORA_G, lambda kt: dve_s(f"mix g{kt}"))
                    pe.wait_ge(*landed_group("g2"))
                    widen("g", "g low", g2, low[1])

                @block.scalar
                def _(act):
                    def splits_ahead():
                        if m == 0:
                            split.make_hi(act, 0)
                        split.make_hi(act, 1)

                    def pre(p, t, dst):
                        j = MIX[p] * NT + t
                        act.activation(dst, u[:, t, :], ACT.Copy, scale=one_less_mu[:, j:j + 1]).then_inc(*act_s.mark(f"pre {p}{t}"))

                    def pre_tmp(p, t):
                        if p != "r" or t >= 2:
                            act.wait_ge(*dve_s(before_tmp(p, t)))
                        pre(p, t, tmp[t % 2])

                    def hi(p, t):
                        act.wait_ge(*dve_s(f"mix {p}{t}"))
                        act.activation(parts[p][0][:, t, :], tmp[t % 2], ACT.Copy).then_inc(*act_s.mark(f"hi {p}{t}"))

                    def out(job, dst, func=ACT.Copy, **kw):
                        act.wait_ge(*pe_s(job))
                        act.activation(dst, banks.bank(job)[0:dst.shape[0]], func, **kw).then_inc(*act_s.mark(f"ev {job}"))

                    norm_act(act, "n", h, sq, meanwhile=splits_ahead)
                    act.wait_ge(*dve_s("1 - mu"))
                    for t in range(NT + 1):
                        if t < NT:
                            act.wait_ge(*dve_s(f"n out{t}"))
                            pre_tmp("r", t)
                        if t:
                            hi("r", t - 1)
                    for g in range(3 * SLOTS):
                        p, nxt, s = order[g // SLOTS], order[g // SLOTS + 1], g % SLOTS
                        if g and g + 1 < 3 * SLOTS:
                            act.wait_ge(*pe_s(f"{order[(g - 1) // SLOTS]}{2 * ((g - 1) % SLOTS) + 1}"))
                            split.make_hi(act, g + 1)
                        for t in (2 * s, 2 * s + 1):
                            if nxt == "w":
                                pre("w", t, mixed["w"][:, t, :])
                            else:
                                pre_tmp(nxt, t)
                        if nxt != "w":
                            hi(nxt, 2 * s)
                            hi(nxt, 2 * s + 1)
                        if p == "v":
                            for t in (2 * s, 2 * s + 1):
                                if t >= 2:
                                    act.wait_ge(*pe_s(f"kk part{t - 2}"))
                                act.activation(kk_sq[t % 2], k[:, t, :], ACT.Square,
                                               scale=col("rw_kk", m * NT + t)).then_inc(*act_s.mark(f"kk sq{t}"))
                        for n in (2 * s, 2 * s + 1):
                            out(f"{p}{n}", {"r": r, "k": k, "v": v}[p][:, n, :])

                    def pres(p, used):
                        act.wait_ge(*pe_s(used))
                        for t in range(NT):
                            pre(p, t, mixed[p][:, t, :])

                    act.wait_ge(*dve_s("ev kk sum"))
                    act.activation(kk_inv, kk_inv, ACT.Sqrt).then_inc(*act_s.mark("kk root"))
                    out("w low", low[1][0:LORA_W, :], ACT.Tanh)
                    if not second:
                        pres("a", "v7")
                    for n in range(NT):
                        out(f"w{n}", lw[:, n, :], ACT.Sigmoid, bias=col("rw_w0", m * NT + n))
                    if second:
                        out("v low", low[0][0:LORA_V, :])
                        pres("a", "v low")
                        for n in range(NT):
                            if n >= 2:
                                act.wait_ge(*dve_s(f"vmix{n - 2}"))
                            out(f"vmix{n}", low_v[:, n % 2, :], ACT.Sigmoid, bias=col("rw_v0", n))
                    pres("g", "v low" if second else "v7")
                    if second:
                        act.wait_ge(*dve_s(f"vmix{NT - 1}"))
                        act.wait_ge(*dve_s(f"v mixed{NT - 1}"))
                        act.wait_ge(*pe_s(f"vmix{NT - 1}"))
                    out("a low", low[0][0:LORA_A, :])
                    for n in range(NT):
                        out(f"a{n}", av[:, n, :], ACT.Sigmoid, bias=col("rw_a0", m * NT + n))
                    act.wait_ge(*dve_s("1 - k_a"))
                    for t in range(NT):
                        act.wait_ge(*act_s(f"ev a{t}"))
                        act.activation(k_factor[:, t, :], av[:, t, :], ACT.Identity, scale=col("rw_ka", m * NT + t),
                                       bias=one_less_ka[:, t:t + 1]).then_inc(*act_s.mark(f"k factor{t}"))
                    act.wait_ge(*pe_s(f"w{NT - 1}"))
                    out("g low", low[1], ACT.Sigmoid)
                    act.wait_ge(*dve_s(f"decay{NT - 1}"))
                    for n in range(NT):
                        out(f"g{n}", gate[:, n, :])

                @block.vector
                def _(dve):
                    dve.tensor_scalar(one_less_mu[:], vec[:, mu0:mu0 + 6 * NT], -1.0, 1.0, ALU.mult,
                                      ALU.add).then_inc(*dve_s.mark("1 - mu"))
                    dve.tensor_scalar(one_less_ka, vec[:, ka0:ka0 + NT], -1.0, 1.0, ALU.mult,
                                      ALU.add).then_inc(*dve_s.mark("1 - k_a"))
                    if m == 0:
                        split.make_lo(dve, 0)
                    split.make_lo(dve, 1)

                    def mix(p, t, dst):
                        dve.wait_ge(*act_s(f"pre {p}{t}"))
                        dve.scalar_tensor_tensor(dst[:, 1:SEQ], u[:, t, 0:SEQ - 1],
                                                 col("rw_mu", (m * 6 + MIX[p]) * NT + t), dst[:, 1:SEQ],
                                                 ALU.mult, ALU.add).then_inc(*dve_s.mark(f"mix {p}{t}"))

                    def lo(p, t):
                        dve.wait_ge(*act_s(f"hi {p}{t}"))
                        dve.tensor_tensor(parts[p][1][:, t, :], tmp[t % 2], parts[p][0][:, t, :].bitcast(F32),
                                          ALU.subtract).then_inc(*dve_s.mark(f"lo {p}{t}"))

                    def norm_out(t):
                        dve.scalar_tensor_tensor(u[:, t, :], h[:, t, :], col("norm_mix", layer * NT + t), rstd,
                                                 ALU.mult, ALU.mult).then_inc(*dve_s.mark(f"n out{t}"))

                    dve.wait_ge(*act_s("n root"))
                    dve.reciprocal(rstd, rstd).then_inc(*dve_s.mark("n rstd"))
                    dve.wait_ge(*dve_s("n rstd"))
                    norm_out(0)
                    for t in range(NT):
                        if t + 1 < NT:
                            norm_out(t + 1)
                        mix("r", t, tmp[t % 2])
                        if t:
                            lo("r", t - 1)
                    lo("r", NT - 1)
                    for g in range(3 * SLOTS):
                        nxt, s = order[g // SLOTS + 1], g % SLOTS
                        if g and g + 1 < 3 * SLOTS:
                            split.make_lo(dve, g + 1)
                        for t in (2 * s, 2 * s + 1):
                            mix(nxt, t, mixed["w"][:, t, :] if nxt == "w" else tmp[t % 2])
                        if nxt != "w":
                            lo(nxt, 2 * s)
                            lo(nxt, 2 * s + 1)
                    dve.wait_ge(*pe_s(f"kk part{NT - 1}"))
                    dve.tensor_scalar(kk_inv, banks.bank("kk sum")[0:HEADS], 1e-24, None,
                                      ALU.max).then_inc(*dve_s.mark("ev kk sum"))
                    dve.wait_ge(*act_s("kk root"))
                    dve.reciprocal(kk_inv, kk_inv).then_inc(*dve_s.mark("kk reciprocal"))
                    dve.wait_ge(*dve_s("kk reciprocal"))
                    dve.tensor_scalar(kk_inv, kk_inv, -1.0, None, ALU.mult).then_inc(*dve_s.mark("kk inv"))
                    for t in range(NT):
                        mix("a", t, mixed["a"][:, t, :])
                    if second:
                        dve.wait_ge(*landed_group("v_first"))
                        for t in range(NT):
                            dve.wait_ge(*act_s(f"ev v{t}"))
                            dve.tensor_tensor(av[:, t, :], av[:, t, :], v[:, t, :],
                                              ALU.subtract).then_inc(*dve_s.mark(f"v gap{t}"))
                        for t in range(NT):
                            dve.wait_ge(*dve_s(f"v gap{t}"))
                            dve.wait_ge(*act_s(f"ev vmix{t}"))
                            dve.tensor_tensor(av[:, t, :], av[:, t, :], low_v[:, t % 2, :],
                                              ALU.mult).then_inc(*dve_s.mark(f"vmix{t}"))
                        for t in range(NT):
                            dve.wait_ge(*dve_s(f"vmix{t}"))
                            dve.tensor_tensor(v[:, t, :], v[:, t, :], av[:, t, :],
                                              ALU.add).then_inc(*dve_s.mark(f"v mixed{t}"))
                    for t in range(NT):
                        mix("g", t, mixed["g"][:, t, :])
                    dve.wait_ge(*landed_group("extra"))
                    for t in range(NT):
                        dve.wait_ge(*act_s(f"ev w{t}"))
                        dve.tensor_tensor_scan(lw[:, t, :], resets, lw[:, t, :], 0.0, ALU.mult,
                                               ALU.add).then_inc(*dve_s.mark(f"decay{t}"))
                    dve.wait_ge(*dve_s(f"mix g{NT - 1}"))
                    for t in range(NT):
                        dve.wait_ge(*pe_s(f"kk inv{t}"))
                        dve.scalar_tensor_tensor(kkn[:, t, :], k[:, t, :], col("rw_kk", m * NT + t),
                                                 banks.bank(f"kk inv{t}"), ALU.mult,
                                                 ALU.mult).then_inc(*dve_s.mark(f"ev kk inv{t}"))
                    for t in range(NT):
                        dve.wait_ge(*dve_s(f"ev kk inv{t}"))
                        dve.wait_ge(*act_s(f"k factor{t}"))
                        dve.scalar_tensor_tensor(av[:, t, :], av[:, t, :], -1.0, kkn[:, t, :],
                                                 ALU.mult, ALU.mult).then_inc(*dve_s.mark(f"b{t}"))
                        dve.tensor_tensor(k[:, t, :], k[:, t, :], k_factor[:, t, :],
                                          ALU.mult).then_inc(*dve_s.mark(f"k eff{t}"))
            ring.uses += 3 * SLOTS
            split.done += 3 * SLOTS

        def rwkv_scan(m):
            r, k, v, lw, b, kkn = region(5), region(6), region(7), region(8), region(9), region(1)
            flat = arena[:, 3:5, :].rearrange("p a n -> p (a n)")
            at = {"n": 0}

            def take(n):
                at["n"] += n
                return flat[:, at["n"] - n:at["n"]]

            def tile3(x, w):
                return x.rearrange("p (t n) -> p t n", n=w)

            ar = take(1536).rearrange("p (t three n) -> p t three n", three=3, n=CH)
            bk = take(1024).rearrange("p (t two n) -> p t two n", two=2, n=CH)
            gm = take(2048).rearrange("p (h n) -> p h n", n=P)
            bkt = tile3(take(1024), P)
            state = tile3(take(1024), P)
            vst = tile3(take(1024), P)
            grow = tile3(take(512), CH)
            uv = tile3(lora[:, 0:1024], P)
            decay = lora[:, 1024:1024 + NT * (CH + 1)].rearrange("p (t n) -> p t n", n=CH + 1)
            w_last = lora[:, 1544:1552].unsqueeze(2)
            Tt = tile3(lora[:, 1552:2064], CH)
            spare = ring_buf[:, SLOTS - 1, :]
            pair1, pair2 = tile3(lora[:, 2064:3088], P), tile3(lora[:, 3088:4112], P)
            Et = tile3(spare[:, 0:1024], P)
            prod = tile3(small[:, 1024:1536], CH)
            beside = [x.rearrange("p (t two n) -> p t two n", two=2, n=CH) for x in (small[:, 0:1024], spare[:, 1024:2048])]
            xs = vst[:, :, 0:CH]
            b64 = lambda j: psum[:, j, :].rearrange("p (t n) -> p t n", n=CH)
            b128 = lambda j: psum[:, j, :].rearrange("p (t n) -> p t n", n=P)

            def wide(name):
                return const(name).unsqueeze(1).broadcast_to([P, NT, CH])

            mask_g = const("mask_g").unsqueeze(1).broadcast_to([P, 4, P])
            halves = [slice(0, CH), slice(CH, P)]
            Bp, D2t, D8t = [pair1] * 3
            Dtp, D4t, F = [pair2] * 3
            D2, IpD = beside[0][:, :, 0, :], beside[0][:, :, 1, :]
            D4, X2 = beside[1][:, :, 0, :], beside[1][:, :, 1, :]
            Dt, D = D4, X2
            X4, X8 = D2, IpD
            X8t, Z1, Z2 = D4, X2, X4

            def b128x2(j):
                return psum[:, j:j + 2, :].rearrange("p b (t n) -> p (b t) n", n=P)

            def gpsimd_pass(pool, i, new, prep, use):
                if prep:
                    if i is not None:
                        pool.wait_ge(*pe_s("X8", i - 1))
                        pool.sem_inc(passed_pool, 1)
                    pool.wait_ge(*act_s("grow", i))
                    pool.sem_inc(passed_pool, 1)
                    if i is not None:
                        pool.wait_ge(*pool_s("A", i - 1))
                        pool.sem_inc(passed_pool, 1)
                    for q, part in enumerate(halves):
                        pool.tensor_tensor(Bp[part, :, part], b[part, :, new], grow[part],
                                           ALU.mult).then_inc(*pool_s.mark(f"B{q}"))
                    pool.wait_ge(*pool_s("B1", i))
                    pool.sem_inc(passed_pool, 1)
                    if i is not None:
                        pool.wait_ge(*pe_s("G3", i - 1))
                        pool.sem_inc(passed_pool, 1)
                    pool.tensor_tensor(bk[:, :, 1, :], k[:, :, new], grow, ALU.mult).then_inc(*pool_s.mark("K"))
                    if i is not None:
                        pool.wait_ge(*pe_s("U1", i))
                        pool.sem_inc(passed_pool, 1)
                    pool.tensor_copy(vst[:, :, CH:P], v[:, :, new]).then_inc(*pool_s.mark("stage v"))
                    if i is not None:
                        pool.wait_ge(*pe_s("bonus", i - 1))
                        pool.sem_inc(passed_pool, 1)
                    pool.tensor_tensor(prod, r[:, :, new], k[:, :, new], ALU.mult).then_inc(*pool_s.mark("rk"))
                    pool.wait_ge(*pool_s("rk", i))
                    pool.sem_inc(passed_pool, 1)
                    rk0 = VEC_ROW["rw_rk"][0] * P + VEC_ROW["rw_rk"][1] + m * NT
                    pool.tensor_tensor(prod, prod, vec[:, rk0:rk0 + NT].unsqueeze(2).broadcast_to([P, NT, CH]),
                                       ALU.mult).then_inc(*pool_s.mark("rk r_k"))
                if use:
                    pool.wait_ge(*pe_s("Y", i))
                    pool.sem_inc(passed_pool, 1)
                if prep:
                    pool.wait_ge(*act_s("decay", i))
                    pool.sem_inc(passed_pool, 1)
                    pool.tensor_tensor(ar[:, :, 2, :], r[:, :, new], decay[:, :, 1:CH + 1],
                                       ALU.mult).then_inc(*pool_s.mark("R"))
                    pool.wait_ge(*dve_s("A", i))
                    pool.sem_inc(passed_pool, 1)
                    pool.tensor_copy(ar[:, :, 1, :], ar[:, :, 0, :]).then_inc(*pool_s.mark("A"))

            def scalar_pass(act, i, new, old, prep, use):
                def out(name, dst, src):
                    act.wait_ge(*pe_s(name, i))
                    act.activation(dst, src, ACT.Copy).then_inc(*act_s.mark(f"ev {name}"))

                if prep:
                    if i is not None:
                        act.wait_ge(*dve_s("w last", i - 1))
                        act.wait_ge(*pool_s("R", i - 1))
                    act.activation(decay[:, :, 1:CH + 1], lw[:, :, new], ACT.Exp,
                                   scale=-DECAY).then_inc(*act_s.mark("decay"))
                    act.activation(grow, lw[:, :, new], ACT.Exp, scale=DECAY).then_inc(*act_s.mark("grow"))
                    act.wait_ge(*dve_s("Dt", i))
                    if i is not None:
                        act.wait_ge(*pe_s("Tt", i - 1))
                    for q, part in enumerate(halves):
                        act.activation(Dtp[part, :, part], Dt[part], ACT.Copy).then_inc(*act_s.mark(f"Dt{q}"))
                if use:
                    out("U0", uv[halves[0], :, halves[0]], b64(4)[halves[0]])
                    out("U1", uv[halves[0], :, halves[1]], b64(5)[halves[0]])
                if prep:
                    act.wait_ge(*act_s("Dt1", i))
                    act.wait_ge(*dve_s("D", i))
                    out("D2", D2, b64(3))
                if use:
                    out("Y", r[:, :, old], b64(6))
                if prep:
                    act.wait_ge(*dve_s("I+D", i))
                    out("D4 X2", D4, b128x2(0)[:, :, 0:CH])
                if prep:
                    out("BK0", bkt[:, 0:4, :], b128(4))
                    out("BK1", bkt[:, 4:8, :], b128(5))
                    out("V0", uv[halves[1], 0:4, :], b128(6)[halves[1]])
                    out("V", uv[halves[1], 4:8, :], b128(0)[halves[1]])
                    act.wait_ge(*pe_s("F", i))
                    for q, part in enumerate(halves):
                        act.activation(F[part, :, part], b64(5)[part], ACT.Copy).then_inc(*act_s.mark(f"F{q}"))

            def vector_pass(dve, i, new, prep, use):
                def evacuate(mark, job, dst, src, mask, op=ALU.mult):
                    dve.wait_ge(*pe_s(job, i))
                    dve.tensor_tensor(dst, src, mask, op).then_inc(*dve_s.mark(mark))

                def turn(mark, dst, src):
                    dve.transpose(dst, src).then_inc(*dve_s.mark(mark))

                def turn_pair(mark, dst, src):
                    for q, part in enumerate(halves):
                        dve.transpose(dst[part, :, part], src[part]).then_inc(*dve_s.mark(f"{mark}{q}"))

                if prep:
                    if i is not None:
                        dve.wait_ge(*pool_s("A", i - 1))
                        dve.wait_ge(*pe_s("G3", i - 1))
                    dve.wait_ge(*act_s("decay", i))
                    dve.tensor_tensor(ar[:, :, 0, :], kkn[:, :, new], decay[:, :, 0:CH],
                                      ALU.mult).then_inc(*dve_s.mark("A"))
                    dve.wait_ge(*act_s("grow", i))
                    dve.tensor_tensor(bk[:, :, 0, :], b[:, :, new], grow, ALU.mult).then_inc(*dve_s.mark("B"))
                if use:
                    dve.wait_ge(*pe_s("X", i))
                    dve.tensor_copy(xs, b64(2)).then_inc(*dve_s.mark("X"))
                if prep:
                    evacuate("Dt", "Mt", Dt, b64(1), wide("mask_dt"))
                    dve.wait_ge(*dve_s("Dt", i))
                    turn("D", D, Dt)
                    for q, part in enumerate(halves):
                        dve.tensor_tensor(Et[part, :, part], b64(1)[part], wide("mask_et")[part],
                                          ALU.mult).then_inc(*dve_s.mark(f"Et{q}"))
                    dve.wait_ge(*dve_s("D", i))
                    dve.tensor_tensor(IpD, D, wide("eye2"), ALU.add).then_inc(*dve_s.mark("I+D"))
                    dve.wait_ge(*act_s("ev D2", i))
                    turn_pair("D2t", D2t, D2)
                    dve.wait_ge(*act_s("ev D4 X2", i))
                    turn_pair("D4t", D4t, D4)
                    dve.tensor_tensor(X2, b128x2(0)[:, :, CH:P], IpD, ALU.add).then_inc(*dve_s.mark("X2"))
                if use:
                    dve.wait_ge(*pe_s("S", i))
                    for q, part in enumerate(halves):
                        dve.tensor_tensor(state[part, :, part], state[part, :, part], b64(7)[part],
                                          ALU.add).then_inc(*dve_s.mark(f"sum{q}"))
                if prep:
                    dve.wait_ge(*pe_s("D8 X4", i))
                    turn_pair("D8t", D8t, b128x2(2)[:, :, 0:CH])
                    dve.wait_ge(*dve_s("X2", i))
                    dve.tensor_tensor(X4, b128x2(2)[:, :, CH:P], X2, ALU.add).then_inc(*dve_s.mark("X4"))
                if use:
                    for q, part in enumerate(halves):
                        dve.wait_ge(*dve_s(f"sum{q}", i))
                        dve.tensor_tensor(state[part, :, part], state[part, :, part],
                                          w_last[part].broadcast_to([CH, NT, CH]),
                                          ALU.mult).then_inc(*dve_s.mark(f"state{q}"))
                if prep:
                    evacuate("G1", "G1", gm[:, 1:8:2, :], b128(7), mask_g)
                    dve.wait_ge(*pe_s("X8", i))
                    dve.wait_ge(*dve_s("X4", i))
                    dve.tensor_tensor(X8, b64(1), X4, ALU.add).then_inc(*dve_s.mark("X8"))
                    dve.wait_ge(*dve_s("X8", i))
                    turn("X8t", X8t, X8)
                    if use:
                        dve.wait_ge(*dve_s("state1", i))
                    dve.tensor_copy(w_last, decay[:, :, CH:CH + 1]).then_inc(*dve_s.mark("w last"))
                    evacuate("G0", "G0", gm[:, 0:8:2, :], b128(3), mask_g)

                    def horner(z, dst, j):
                        dve.wait_ge(*pe_s(z, i))
                        dve.wait_ge(*dve_s("X8t", i))
                        dve.tensor_tensor(dst, b64(j), X8t, ALU.add).then_inc(*dve_s.mark(z))

                    evacuate("G2", "G2", gm[:, 8:16:2, :], b128(0), mask_g)
                    horner("Z1", Z1, 6)
                    evacuate("G3", "G3", gm[:, 9:16:2, :], b128(2), mask_g)
                    horner("Z2", Z2, 1)
                    horner("Tt", Tt, 5)
                    dve.wait_ge(*pe_s("bonus", i))
                    dve.wait_ge(*pool_s("rk", i))
                    dve.tensor_tensor(k[:, :, new], v[:, :, new], b64(4), ALU.mult).then_inc(*dve_s.mark("ev bonus"))

            def tensor_pass(pe, i, prep, use):
                def heads(job, j, left, right):
                    pe.sem_inc(passed_pe, 1)
                    for t in range(NT):
                        mm = pe.matmul(b64(j)[:, t, :], left[:, t, :], right[:, t, :], start=True, stop=True)
                    mm.then_inc(*pe_s.mark(job))

                def both(job, j, left, right):
                    pe.sem_inc(passed_pe, 1)
                    for t in range(NT):
                        mm = pe.matmul(b128x2(j)[:, t, :], left[:, t, :], right[:, t, :, :], start=True, stop=True)
                    mm.then_inc(*pe_s.mark(job))

                def products(job, j, t0, part):
                    for t in range(4):
                        mm = pe.matmul(b128(j)[:, t, :], bk[part, t0 + t, :, :], ar[part, t0 + t, 0:3:2, :],
                                       start=True, stop=True)
                    mm.then_inc(*pe_s.mark(job))

                if use:
                    if i is not None:
                        pe.wait_ge(*dve_s("G3", i - 1))
                        pe.wait_ge(*pool_s("A", i - 1))
                        pe.sem_inc(passed_pe, 1)
                    for t in range(NT):
                        for q, part in enumerate(halves):
                            pe.matmul(b64(2)[part, t, :], ar[:, t, 1, :], state[:, t, part], start=True, stop=False)
                            mm = pe.matmul(b64(2)[part, t, :], gm[:, 2 * t + q, 0:CH], uv[:, t, part],
                                           start=False, stop=True)
                    mm.then_inc(*pe_s.mark("X"))
                if prep:
                    pe.wait_ge(*dve_s("A", i))
                    pe.wait_ge(*pool_s("B1", i))
                    heads("Mt", 1, Bp, ar[:, :, 0, :])
                if use:
                    if i is not None:
                        pe.wait_ge(*dve_s("ev bonus", i - 1))
                    pe.wait_ge(*dve_s("X", i))
                    pe.sem_inc(passed_pe, 1)
                    for q, part in enumerate(halves):
                        for t in range(NT):
                            mm = pe.matmul(b64(4 + q)[halves[0], t, :], Tt[part, t, :], xs[part, t, :],
                                           start=True, stop=True)
                        mm.then_inc(*pe_s.mark(f"U{q}"))
                if prep:
                    pe.wait_ge(*dve_s("D", i))
                    pe.wait_ge(*act_s("Dt1", i))
                    heads("D2", 3, Dtp, D)
                if use:
                    pe.wait_ge(*act_s("ev U1", i))
                    pe.sem_inc(passed_pe, 1)
                    for t in range(NT):
                        pe.matmul(b64(6)[:, t, :], state[:, t, :], ar[:, t, 2, :], start=True, stop=False,
                                  skip_group_check=True)
                        for q, part in enumerate(halves):
                            mm = pe.matmul(b64(6)[part, t, :], uv[:, t, part], gm[:, 2 * t + q, CH:P],
                                           start=False, stop=True, skip_group_check=True)
                    mm.then_inc(*pe_s.mark("Y"))
                if prep:
                    pe.wait_ge(*dve_s("D2t1", i))
                    pe.wait_ge(*act_s("ev D2", i))
                    pe.wait_ge(*dve_s("I+D", i))
                    both("D4 X2", 0, D2t, beside[0])
                if use:
                    for t in range(NT):
                        for part in halves:
                            mm = pe.matmul(b64(7)[part, t, :], bkt[:, t, part], uv[:, t, part], start=True, stop=True)
                    mm.then_inc(*pe_s.mark("S"))
                if prep:
                    pe.wait_ge(*dve_s("B", i))
                    pe.wait_ge(*pool_s("K", i))
                    for half in range(2):
                        for t in range(4):
                            mm = pe.transpose(b128(4 + half)[:, t, :],
                                              bk[:, 4 * half + t, :, :].rearrange("p a n -> p (a n)"), const("ident"))
                        mm.then_inc(*pe_s.mark(f"BK{half}"))
                    pe.wait_ge(*dve_s("X2", i))
                    both("D8 X4", 2, D4t, beside[1])
                    pe.wait_ge(*pool_s("stage v", i))
                    if use:
                        pe.wait_ge(*act_s("ev Y", i))
                    for half, j in enumerate((6, 0)):
                        for t in range(4):
                            mm = pe.transpose(b128(j)[:, t, :], vst[:, 4 * half + t, :], const("ident"))
                        mm.then_inc(*pe_s.mark("V" if half else "V0"))
                    if use:
                        pe.wait_ge(*dve_s("sum1", i))
                    pe.wait_ge(*pool_s("A", i))
                    products("G1", 7, 0, halves[1])
                    pe.wait_ge(*dve_s("D8t1", i))
                    pe.wait_ge(*dve_s("X4", i))
                    heads("X8", 1, D8t, X4)
                    products("G0", 3, 0, halves[0])
                    pe.wait_ge(*act_s("ev BK1", i))
                    pe.wait_ge(*dve_s("X8", i))
                    heads("F", 5, Et, X8)
                    pe.wait_ge(*act_s("ev V", i))
                    products("G2", 0, 4, halves[0])
                    pe.wait_ge(*dve_s("X8t", i))
                    pe.wait_ge(*act_s("F1", i))
                    heads("Z1", 6, F, X8t)
                    products("G3", 2, 4, halves[1])
                    pe.wait_ge(*dve_s("Z1", i))
                    heads("Z2", 1, F, Z1)
                    pe.wait_ge(*pool_s("rk r_k", i))
                    pe.matmul(psum[:, 4, :], const("pair"), prod.rearrange("p t n -> p (t n)"),
                              start=True, stop=True).then_inc(*pe_s.mark("bonus"))
                    pe.wait_ge(*dve_s("Z2", i))
                    heads("Tt", 5, F, Z2)

            first, last = slice(0, CH), slice((NCH - 1) * CH, NCH * CH)
            stage(f"scan{m} first")
            with nc.Block() as block:
                @block.gpsimd
                def _(pool):
                    for x, name in ((state, "state"), (uv, "uv"), (vst, "v")):
                        pool.memset(x[:], 0.0).then_inc(*pool_s.mark(f"zero {name}"))
                    pool.wait_ge(*dve_s("zero Et"))
                    pool.wait_ge(*pool_s("zero v"))
                    gpsimd_pass(pool, None, first, True, False)

                @block.scalar
                def _(act):
                    act.wait_ge(*dve_s("ones"))
                    scalar_pass(act, None, first, None, True, False)

                @block.vector
                def _(dve):
                    dve.memset(decay[:, :, 0:1], 1.0).then_inc(*dve_s.mark("ones"))
                    for x, name in ((pair1, "pair1"), (pair2, "pair2"), (Et, "Et")):
                        dve.memset(x[:], 0.0).then_inc(*dve_s.mark(f"zero {name}"))
                    dve.wait_ge(*dve_s("zero Et"))
                    vector_pass(dve, None, first, True, False)

                @block.tensor
                def _(pe):
                    tensor_pass(pe, None, True, False)

            stage(f"scan{m}")
            with nc.Block() as block:
                @block.gpsimd
                def _(pool):
                    with pool.Fori(0, NCH - 1) as i:
                        pool_s.start_loop(i)
                        gpsimd_pass(pool, i, bass.ds(i * CH + CH, CH), True, True)
                        pool_s.end_loop(NCH - 1)

                @block.scalar
                def _(act):
                    with act.Fori(0, NCH - 1) as i:
                        act_s.start_loop(i)
                        scalar_pass(act, i, bass.ds(i * CH + CH, CH), bass.ds(i * CH, CH), True, True)
                        act_s.end_loop(NCH - 1)

                @block.vector
                def _(dve):
                    with dve.Fori(0, NCH - 1) as i:
                        dve_s.start_loop(i)
                        vector_pass(dve, i, bass.ds(i * CH + CH, CH), True, True)
                        dve_s.end_loop(NCH - 1)

                @block.tensor
                def _(pe):
                    with pe.Fori(0, NCH - 1) as i:
                        pe_s.start_loop(i)
                        tensor_pass(pe, i, True, True)
                        pe_s.end_loop(NCH - 1)

            stage(f"scan{m} last")
            with nc.Block() as block:
                @block.scalar
                def _(act):
                    scalar_pass(act, None, None, last, False, True)

                @block.vector
                def _(dve):
                    vector_pass(dve, None, None, False, True)

                @block.tensor
                def _(pe):
                    tensor_pass(pe, None, False, True)

        def rwkv_finish(layer, m):
            stage(f"finish{m}")
            y, bonus, gate, yc, sq = region(5), region(6), region(2), region(7), region(1)
            inv = rstd[0:HEADS, :]
            spread = lora[0:HEADS, 0:DM]
            banks = Banks([(f"mean{t}", "dve") for t in range(NT)] + [("var sum", "act")]
                          + [(f"inv{t}", "dve") for t in range(NT)] + [(f"o{t}", "dve") for t in range(NT)])
            with nc.Block() as block:
                @block.sync
                def _(sp):
                    load_proj(sp, a["rw_wo"][m], lambda s: None, [SLOTS - 1])
                    bring_group(sp, "spread", spread, a["extras"][0:HEADS, P + ROPE + SEQ:])
                    ffn_head(sp, layer, lambda s: split.made(s))

                @block.tensor
                def _(pe):
                    for t in range(NT):
                        pe.matmul(banks.bank(f"mean{t}"), const("pair"), y[:, t, :],
                                  start=True, stop=True).then_inc(*pe_s.mark(f"mean{t}"))
                    pe.wait_ge(*banks.free("var sum"))
                    for t in range(NT):
                        pe.wait_ge(*act_s(f"sq{t}"))
                        mm = pe.matmul(banks.bank("var sum")[0:HEADS], pick(t), sq[:, t, :],
                                       start=(t == 0), stop=(t == NT - 1))
                    mm.then_inc(*pe_s.mark("var sum"))
                    pe.wait_ge(*landed_group("spread"))
                    pe.wait_ge(*dve_s("inv"))
                    for t in range(NT):
                        pe.wait_ge(*banks.free(f"inv{t}"))
                        pe.matmul(banks.bank(f"inv{t}"), spread[:, t * P:(t + 1) * P], inv,
                                  start=True, stop=True).then_inc(*pe_s.mark(f"inv{t}"))
                    gemm(pe, "o", banks, x_parts, lambda k: dve_s(f"lo{k}"), 0)

                @block.scalar
                def _(act):
                    split.make_hi(act, 0)
                    for t in range(NT):
                        act.wait_ge(*dve_s(f"ev mean{t}"))
                        act.activation(sq[:, t, :], yc[:, t, :], ACT.Square).then_inc(*act_s.mark(f"sq{t}"))
                    split.make_hi(act, 1)
                    act.wait_ge(*pe_s("var sum"))
                    act.activation(inv, banks.bank("var sum")[0:HEADS], ACT.Sqrt, bias=gn_eps[0:HEADS],
                                   scale=1.0 / HEAD).then_inc(*act_s.mark("ev var sum"))
                    for t in range(NT):
                        act.wait_ge(*pool_s(f"gated{t}"))
                        act.activation(x_parts[0][:, t, :], y[:, t, :], ACT.Copy).then_inc(*act_s.mark(f"hi{t}"))
                    for g in (2, 3, 4):
                        act.wait_ge(*pe_s(f"o{2 * (g - 2) + 1}"))
                        split.make_hi(act, g)

                @block.vector
                def _(dve):
                    for t in range(NT):
                        dve.wait_ge(*pe_s(f"mean{t}"))
                        dve.scalar_tensor_tensor(yc[:, t, :], banks.bank(f"mean{t}"), -1.0 / HEAD, y[:, t, :],
                                                 ALU.mult, ALU.add).then_inc(*dve_s.mark(f"ev mean{t}"))
                    split.make_lo(dve, 0)
                    split.make_lo(dve, 1)
                    dve.wait_ge(*act_s("ev var sum"))
                    dve.reciprocal(inv, inv).then_inc(*dve_s.mark("inv"))

                    def lo(t):
                        dve.wait_ge(*act_s(f"hi{t}"))
                        dve.tensor_tensor(x_parts[1][:, t, :], y[:, t, :], x_parts[0][:, t, :].bitcast(F32),
                                          ALU.subtract).then_inc(*dve_s.mark(f"lo{t}"))

                    for t in range(NT):
                        dve.wait_ge(*pe_s(f"inv{t}"))
                        dve.scalar_tensor_tensor(yc[:, t, :], yc[:, t, :], col("rw_lnx_w", m * NT + t),
                                                 banks.bank(f"inv{t}"), ALU.mult,
                                                 ALU.mult).then_inc(*dve_s.mark(f"ev inv{t}"))
                        dve.wait_ge(*dve_s(f"ev inv{t}"))
                        dve.scalar_tensor_tensor(yc[:, t, :], yc[:, t, :], col("rw_lnx_b", m * NT + t), bonus[:, t, :],
                                                 ALU.add, ALU.add).then_inc(*dve_s.mark(f"with bonus{t}"))
                        if t >= 2:
                            lo(t - 2)
                    lo(NT - 2)
                    lo(NT - 1)
                    for s in range(SLOTS):
                        if s < 3:
                            split.make_lo(dve, s + 2)
                        for t in (2 * s, 2 * s + 1):
                            dve.wait_ge(*pe_s(f"o{t}"))
                            dve.tensor_tensor(h[:, t, :], h[:, t, :], banks.bank(f"o{t}"),
                                              ALU.add).then_inc(*dve_s.mark(f"ev o{t}"))

                @block.gpsimd
                def _(pool):
                    for t in range(NT):
                        pool.wait_ge(*dve_s(f"with bonus{t}"))
                        pool.tensor_tensor(y[:, t, :], yc[:, t, :], gate[:, t, :],
                                           ALU.mult).then_inc(*pool_s.mark(f"gated{t}"))
            ring.uses += SLOTS
            split.done += SLOTS

        def conv_glu(layer):
            stage("glu")
            sq, total, tmp = region(6), region(7)[:, 0, :], region(7)[:, 2:6, :]
            gain = lambda t: col("norm_mix", layer * NT + t)
            jobs = [[f"{'ab'[s % 2]}{4 * turn + 2 * (s // 2) + n}" for n in range(2)]
                    for turn in range(2) for s in range(SLOTS)]
            banks = Banks([(j, "dve") for pair in jobs for j in pair])
            with nc.Block() as block:
                @block.sync
                def _(sp):
                    bring(sp, taps_rows, a["cv_dw"][0])
                    w1 = a["cv_w1"][0].rearrange("(k p) n -> p k n", p=P)
                    for s in range(SLOTS):
                        c = (2 + s // 2) * 256 + (s % 2) * DM
                        ring.load(sp, cols_slot(s), w1[:, :, c:c + 256], split.made(s))
                    load_proj(sp, a["cv_w2"][0], lambda s: split.made(SLOTS + s))
                taps_in = ins["n"]

                @block.gpsimd
                def _(pool):
                    pool.memset(glu[:, :, 0:PAD], 0.0).then_inc(*pool_s.mark("pad"))
                    fold_pool(pool, sq, total)

                @block.tensor
                def _(pe):
                    pe.wait_ge(in_landed, taps_in)
                    for t in range(NT):
                        mm = pe.transpose(psum[:, 6, t * TAPS:(t + 1) * TAPS], taps_rows[:, t * P:(t + 1) * P],
                                          cst[0:TAPS, 0:TAPS])
                    mm.then_inc(*pe_s.mark("taps"))
                    for g, pair in enumerate(jobs):
                        pe.wait_ge(*split.made(g))
                        order = [(n, k) for k in range(NT) for n in range(2)]
                        if g:
                            order = [(n, k) for n in range(2) for k in range(NT)]
                        for n, k in order:
                            if k == 0 and banks.free(pair[n]):
                                pe.wait_ge(*banks.free(pair[n]))
                            if g == 3 and k == 0:
                                pe.wait_ge(*act_s("root" if n else "taps"))
                            if g == 0 and n == 0:
                                pe.wait_ge(*dve_s(f"x{k}"))
                            mm = split.three(pe, banks.bank(pair[n]), g, by_cols, np.s_[:, k, n * P:(n + 1) * P],
                                             (x_parts[0][:, k, :], x_parts[1][:, k, :]), k == 0, k == NT - 1)
                            if k == NT - 1:
                                mm.then_inc(*pe_s.mark(pair[n]))
                        if g == 0:
                            fold_pe(pe, total)

                @block.scalar
                def _(act):
                    fold_act(act, gain, sq)
                    act.wait_ge(*pe_s("taps"))
                    act.activation(taps.rearrange("p t j -> p (t j)"), psum[:, 6, 0:NT * TAPS],
                                   ACT.Copy).then_inc(*act_s.mark("taps"))
                    split.make_hi(act, 1)
                    for g, pair in enumerate(jobs):
                        if g + 2 <= len(jobs):
                            act.wait_ge(*pe_s(pair[1]))
                            split.make_hi(act, g + 2)
                        if g == 0:
                            fold_root(act)
                        if g % 2:
                            for n, job in enumerate(pair):
                                act.wait_ge(*dve_s(f"ev {job}"))
                                t = int(job[1:])
                                act.activation(sig[:, t, :], tmp[:, n, :], ACT.Sigmoid,
                                               bias=col("cv_b1", NT + t)).then_inc(*act_s.mark(f"sig{t}"))

                @block.vector
                def _(dve):
                    fold_dve(dve, gain)
                    split.make_lo(dve, 1)
                    for g, pair in enumerate(jobs):
                        if g + 2 <= len(jobs):
                            split.make_lo(dve, g + 2)
                        if g == 0:
                            fold_rstd(dve)
                        if g % 2:
                            for j, job in enumerate(pair + jobs[g - 1]):
                                dve.wait_ge(*pe_s(job))
                                if j >= 2 and g > 1:
                                    dve.wait_ge(*dve_s(f"glu{int(job[1:]) - 2}"))
                                dve.tensor_tensor(tmp[:, j, :], banks.bank(job), rstd,
                                                  ALU.mult).then_inc(*dve_s.mark(f"ev {job}"))
                            for n, job in enumerate(jobs[g - 1]):
                                t = int(job[1:])
                                dve.wait_ge(*dve_s(f"ev {job}"))
                                dve.wait_ge(*act_s(f"sig{t}"))
                                dve.scalar_tensor_tensor(glu[:, t, PAD:PAD + SEQ], tmp[:, 2 + n, :], col("cv_b1", t),
                                                         sig[:, t, :], ALU.add, ALU.mult).then_inc(*dve_s.mark(f"glu{t}"))
            ring.uses += len(jobs)
            split.done += len(jobs)

        def conv_taps():
            stage("taps")
            z, acc, acc2 = region(5), region(6), region(7)
            diag = arena[:, 3, :].rearrange("p (b j c) -> p b j c", b=2, c=P)
            term = arena[:, 4, :].rearrange("p (b s) -> p b s", s=SEQ)
            eye = const("ident").unsqueeze(1).broadcast_to([P, PE_TAPS, P])
            with nc.Block() as block:
                @block.vector
                def _(dve):
                    def diagonals(t):
                        if t >= 2:
                            dve.wait_ge(*pe_s(f"conv{t - 2}"))
                        dve.tensor_tensor(diag[:, t % 2, 0:PE_TAPS, :], eye,
                                          taps[:, t, 0:PE_TAPS].unsqueeze(2).broadcast_to([P, PE_TAPS, P]),
                                          ALU.mult).then_inc(*dve_s.mark(f"diag{t}"))

                    diagonals(0)
                    for t in range(NT):
                        for j in range(PE_TAPS + ACT_TAPS, TAPS):
                            first = j == PE_TAPS + ACT_TAPS
                            if j == PE_TAPS + ACT_TAPS + 3 and t + 1 < NT:
                                diagonals(t + 1)
                            if first:
                                op = dve.tensor_scalar(acc[:, t, :], glu[:, t, j:j + SEQ], taps[:, t, j:j + 1], None, ALU.mult)
                            else:
                                dve.wait_ge(*dve_s(f"tap{t} {j - 1}"))
                                op = dve.scalar_tensor_tensor(acc[:, t, :], glu[:, t, j:j + SEQ], taps[:, t, j:j + 1],
                                                              acc[:, t, :], ALU.mult, ALU.add)
                            op.then_inc(*dve_s.mark(f"tap{t} {j}"))
                        dve.wait_ge(*pe_s(f"conv{t}"))
                        dve.wait_ge(*dve_s(f"tap{t} {TAPS - 1}"))
                        dve.scalar_tensor_tensor(acc[:, t, :], psum[:, t % 4, :], col("cv_bdw", t), acc[:, t, :],
                                                 ALU.add, ALU.add).then_inc(*dve_s.mark(f"taps{t}"))
                        dve.wait_ge(*dve_s(f"taps{t}"))
                        dve.wait_ge(*pool_s(f"term{t} {ACT_TAPS - 1}"))
                        dve.tensor_tensor(z[:, t, :], acc[:, t, :], acc2[:, t, :],
                                          ALU.add).then_inc(*dve_s.mark(f"z{t}"))

                @block.scalar
                def _(act):
                    for t in range(NT):
                        for j in range(ACT_TAPS):
                            n = t * ACT_TAPS + j
                            if n >= 8:
                                before = n - 8
                                act.wait_ge(*pool_s(f"term{before // ACT_TAPS} {before % ACT_TAPS}"))
                            tap = PE_TAPS + j
                            act.activation(term[:, n % 8, :], glu[:, t, tap:tap + SEQ], ACT.Copy,
                                           scale=taps[:, t, tap:tap + 1]).then_inc(*act_s.mark(f"term{t} {j}"))

                @block.gpsimd
                def _(pool):
                    for t in range(NT):
                        for j in range(ACT_TAPS):
                            n = t * ACT_TAPS + j
                            pool.wait_ge(*act_s(f"term{t} {j}"))
                            if j == 0:
                                op = pool.tensor_copy(acc2[:, t, :], term[:, n % 8, :])
                            else:
                                pool.wait_ge(*pool_s(f"term{t} {j - 1}"))
                                op = pool.tensor_tensor(acc2[:, t, :], acc2[:, t, :], term[:, n % 8, :], ALU.add)
                            op.then_inc(*pool_s.mark(f"term{t} {j}"))

                @block.tensor
                def _(pe):
                    def mean(t):
                        pe.wait_ge(*dve_s(f"z{t}"))
                        pe.matmul(psum[:, 6, :], const("ones"), z[:, t, :], start=(t == 0), stop=(t == NT - 1),
                                  skip_group_check=True).then_inc(*pe_s.mark(f"mean{t}"))

                    for t in range(NT):
                        pe.wait_ge(*dve_s(f"diag{t}"))
                        if t >= 4:
                            pe.wait_ge(*dve_s(f"taps{t - 4}"))
                        for j in range(PE_TAPS):
                            mm = pe.matmul(psum[:, t % 4, :], diag[:, t % 2, j, :], glu[:, t, j:j + SEQ],
                                           start=(j == 0), stop=(j == PE_TAPS - 1), skip_group_check=True)
                        mm.then_inc(*pe_s.mark(f"conv{t}"))
                        if t >= 2:
                            mean(t - 2)
                    mean(NT - 2)
                    mean(NT - 1)

        def conv_finish(layer):
            stage("convout")
            z, zc, sq = region(5), region(6), region(7)
            banks = Banks([(f"o{t}", "dve") for t in range(NT)])
            with nc.Block() as block:
                @block.sync
                def _(sp):
                    ffn_head(sp, layer, lambda s: split.made(s))

                @block.tensor
                def _(pe):
                    norm_pe(pe, "n", sq)
                    gemm(pe, "o", banks, x_parts, lambda k: dve_s(f"lo{k}"), 0)

                @block.scalar
                def _(act):
                    for t in range(NT):
                        act.wait_ge(*dve_s(f"centred{t}"))
                        act.activation(sq[:, t, :], zc[:, t, :], ACT.Square).then_inc(*act_s.mark(f"n sq{t}"))
                    split.make_hi(act, 1)
                    act.wait_ge(*pe_s("n sum"))
                    act.activation(rstd, psum[:, 7, :], ACT.Sqrt, bias=eps, scale=1.0 / DM).then_inc(*act_s.mark("n root"))
                    for t in range(NT + 1):
                        if t < NT:
                            act.wait_ge(*dve_s(f"n out{t}"))
                            act.activation(z[:, t, :], zc[:, t, :], ACT.Silu,
                                           bias=col("cv_ln_b", t)).then_inc(*act_s.mark(f"silu{t}"))
                        if t:
                            act.wait_ge(*act_s(f"silu{t - 1}"))
                            act.activation(x_parts[0][:, t - 1, :], z[:, t - 1, :],
                                           ACT.Copy).then_inc(*act_s.mark(f"hi{t - 1}"))
                    for g in (2, 3, 4):
                        act.wait_ge(*pe_s(f"o{2 * (g - 2) + 1}"))
                        split.make_hi(act, g)

                @block.vector
                def _(dve):
                    for t in range(NT):
                        dve.scalar_tensor_tensor(zc[:, t, :], psum[:, 6, :], -1.0 / DM, z[:, t, :],
                                                 ALU.mult, ALU.add).then_inc(*dve_s.mark(f"centred{t}"))
                    split.make_lo(dve, 1)
                    norm_dve(dve, "n", zc, zc, lambda t: col("cv_ln_w", t))
                    for t in range(NT):
                        dve.wait_ge(*act_s(f"hi{t}"))
                        dve.tensor_tensor(x_parts[1][:, t, :], z[:, t, :], x_parts[0][:, t, :].bitcast(F32),
                                          ALU.subtract).then_inc(*dve_s.mark(f"lo{t}"))
                    for t in range(NT):
                        if t in (0, 2, 4):
                            split.make_lo(dve, 2 + t // 2)
                        dve.wait_ge(*pe_s(f"o{t}"))
                        dve.scalar_tensor_tensor(h[:, t, :], banks.bank(f"o{t}"), col("cv_b2", t), h[:, t, :],
                                                 ALU.add, ALU.add).then_inc(*dve_s.mark(f"ev o{t}"))
            ring.uses += SLOTS
            split.done += SLOTS

        glu = arena[:, 1:3, :].rearrange("p a n -> p (a n)")[:, 0:NT * (PAD + SEQ)].rearrange(
            "p (t s) -> p t s", s=PAD + SEQ)
        sig = region(5)
        taps_rows = lora[0:TAPS, 0:DM]
        taps = lora[:, DM:DM + NT * TAPS].rearrange("p (t j) -> p t j", j=TAPS)

        cbuf = region(2)
        kr, sin_t, cos_t = (cbuf[NOPE:QK, t, :] for t in (5, 6, 7))
        q_t = arena[:, 3:5, :].rearrange("p a (t s) -> p (a t) s", s=SEQ)
        k_t = arena[:, 5:7, :].rearrange("p a (t s) -> p (a t) s", s=SEQ)
        v_tok = arena[:, 7, :].rearrange("p (t d) -> p t d", d=HEADS * VDIM)
        probs = region(8)
        o_t = region(1)
        causal, turn_m = lora[:, 0:P], lora[NOPE:QK, P:P + ROPE]
        CQ, CKV = Q_LORA // P, KV_LORA // P
        Q_HEADS = [6, 6, 4]
        wd_slot = lambda s, w: ring.slot(s)[:, 0:NT * w].rearrange("p (k n) -> p k n", n=w)
        uq_slot = lambda s, w: ring.slot(s)[:, 0:CQ * w].rearrange("p (k n) -> p k n", n=w)

        def mla_down(layer):
            stage("down")
            sq, total = region(5), region(6)[:, 0, :]
            gain = lambda t: col("norm_mix", layer * NT + t)
            wd_cols = [256, 256, P + ROPE]
            steps = [[0, 1], [2, 3], [4, 5]]
            pos_i = small[NOPE:QK, 1024:1536].bitcast(I32)
            pos = lora[NOPE:QK, 512:1024]
            turns_f, turns_i, gap = lora[NOPE:QK, 1024:1536], lora[NOPE:QK, 1536:2048].bitcast(I32), lora[NOPE:QK, 2048:2560]
            angle = lora[NOPE:QK, 2560:3072]
            freq = cst[NOPE:QK, CONSTS["cols"][0] + 2:CONSTS["cols"][0] + 3]
            rstd_kv = low[0]
            with nc.Block() as block:
                @block.sync
                def _(sp):
                    bring(sp, pos_i, a["positions"][0].partition_broadcast(ROPE))
                    bring(sp, lora[:, 0:P + ROPE], a["extras"][:, 0:P + ROPE])
                    wuq = a["ml_wuq"][0].rearrange("(k p) n -> p k n", p=P)
                    wukv = a["ml_wukv"][0].rearrange("(k p) n -> p k n", p=P)
                    c = 0
                    for j, nh in enumerate(Q_HEADS):
                        ring.load(sp, uq_slot(3 + j, nh * QK), wuq[:, :, c:c + nh * QK],
                                  split.made(j - 1) if j else None)
                        c += nh * QK
                    ring.load(sp, rows_slot(2), wukv[:, :, 0:DM], split.made(2))
                loads_all = ins["n"]

                @block.gpsimd
                def _(pool):
                    fold_pool(pool, sq, total)

                @block.tensor
                def _(pe):
                    for g, tiles in enumerate(steps):
                        pe.wait_ge(*split.made(g))
                        order = [(n, k) for k in range(NT) for n in range(2)]
                        if g:
                            order = [(n, k) for n in range(2) for k in range(NT)]
                        for n, k in order:
                            if g == 0 and n == 0:
                                pe.wait_ge(*dve_s(f"x{k}"))
                            c = k * wd_cols[g] + (NOPE if tiles[n] == 5 else n * P)
                            mm = split.three(pe, psum[:, tiles[n], :], g, lambda w: w, np.s_[:, c:c + P],
                                             (x_parts[0][:, k, :], x_parts[1][:, k, :]), k == 0, k == NT - 1)
                            if k == NT - 1:
                                mm.then_inc(*pe_s.mark(f"c{tiles[n]}"))
                        if g == 0:
                            fold_pe(pe, total)
                    pe.wait_ge(*act_s("root"))
                    for t in range(CQ + CKV):
                        pe.wait_ge(*act_s(f"csq{t}"))
                        mm = pe.matmul(psum[:, 6 if t < CQ else 7, :], const("ones"), sq[:, t, :],
                                       start=t in (0, CQ), stop=t in (CQ - 1, CQ + CKV - 1))
                        if t == CQ - 1:
                            mm.then_inc(*pe_s.mark("cq sum"))
                    mm.then_inc(*pe_s.mark("ckv sum"))

                @block.scalar
                def _(act):
                    fold_act(act, gain, sq)
                    split.make_hi(act, 1)
                    act.wait_ge(*pe_s("c1"))
                    split.make_hi(act, 2)
                    fold_root(act)
                    for t in range(CQ + CKV):
                        act.wait_ge(*dve_s(f"ev c{t}"))
                        act.activation(sq[:, t, :], cbuf[:, t, :], ACT.Square).then_inc(*act_s.mark(f"csq{t}"))
                    act.wait_ge(*pe_s("cq sum"))
                    act.wait_ge(*dve_s("ev c5"))
                    act.activation(rstd, psum[:, 6, :], ACT.Sqrt, bias=eps, scale=1.0 / Q_LORA).then_inc(*act_s.mark("cq root"))
                    act.wait_ge(*pe_s("ckv sum"))
                    act.activation(rstd_kv, psum[:, 7, :], ACT.Sqrt, bias=eps,
                                   scale=1.0 / KV_LORA).then_inc(*act_s.mark("ckv root"))
                    act.wait_ge(*dve_s("sin angle"))
                    act.activation(sin_t, angle, ACT.Sin).then_inc(*act_s.mark("sin"))
                    act.wait_ge(*dve_s("cos angle"))
                    act.activation(cos_t, gap, ACT.Sin).then_inc(*act_s.mark("cos"))

                @block.vector
                def _(dve):
                    fold_dve(dve, gain)
                    split.make_lo(dve, 1)
                    split.make_lo(dve, 2)
                    counter = [0]

                    def then(op):
                        counter[0] += 1
                        name = f"angle {counter[0]}"
                        op.then_inc(*dve_s.mark(name))
                        dve.wait_ge(*dve_s(name))

                    def wrap(x):
                        then(dve.tensor_scalar(turns_f, x, float(np.pi), -TWO_PI, ALU.is_gt, ALU.mult))
                        then(dve.tensor_tensor(x, x, turns_f, ALU.add))
                        then(dve.tensor_scalar(turns_f, x, -float(np.pi), TWO_PI, ALU.is_lt, ALU.mult))
                        then(dve.tensor_tensor(x, x, turns_f, ALU.add))

                    dve.wait_ge(in_landed, loads_all)
                    then(dve.tensor_copy(pos, pos_i))
                    then(dve.tensor_scalar(angle, pos, freq, None, ALU.mult))
                    then(dve.tensor_scalar(turns_i, angle, 1.0 / TWO_PI, None, ALU.mult))
                    then(dve.tensor_copy(turns_f, turns_i))
                    then(dve.scalar_tensor_tensor(angle, turns_f, -6.28125, angle, ALU.mult, ALU.add))
                    then(dve.scalar_tensor_tensor(angle, turns_f, -(TWO_PI - 6.28125), angle, ALU.mult, ALU.add))
                    wrap(angle)
                    then(dve.tensor_scalar(gap, angle, float(np.pi / 2), None, ALU.add))
                    dve.tensor_scalar(angle, angle, PI_BELOW, -PI_BELOW, ALU.min,
                                      ALU.max).then_inc(*dve_s.mark("sin angle"))
                    wrap(gap)
                    dve.tensor_scalar(gap, gap, PI_BELOW, -PI_BELOW, ALU.min, ALU.max).then_inc(*dve_s.mark("cos angle"))
                    fold_rstd(dve)
                    for t in range(6):
                        rows = slice(NOPE, QK) if t == 5 else slice(0, P)
                        dve.wait_ge(*pe_s(f"c{t}"))
                        dve.tensor_tensor(cbuf[rows, t, :], psum[rows, t, :], rstd[rows, :],
                                          ALU.mult).then_inc(*dve_s.mark(f"ev c{t}"))
                    for name, buf, ts, vector in (("cq", rstd, range(CQ), "ml_gq"), ("ckv", rstd_kv, range(CQ, CQ + CKV), "ml_gkv")):
                        dve.wait_ge(*act_s(f"{name} root"))
                        dve.reciprocal(buf, buf).then_inc(*dve_s.mark(f"{name} rstd"))
                        dve.wait_ge(*dve_s(f"{name} rstd"))
                        for t in ts:
                            dve.scalar_tensor_tensor(cbuf[:, t, :], cbuf[:, t, :], col(vector, t - ts[0]), buf,
                                                     ALU.mult, ALU.mult).then_inc(*dve_s.mark(f"latent{t}"))
            ring.uses += len(steps)
            split.done += len(steps)

        def mla_up(layer):
            stage("up")
            jobs = ["rot k"]
            for hd in range(HEADS):
                jobs += [f"q{hd}"] + ([f"rot q{hd - 1}"] if hd else [])
            jobs += [f"rot q{HEADS - 1}"] + [f"k{hd}" for hd in range(HEADS)] + [f"v{j}" for j in range(8)]
            banks = Banks([(j, "dve" if j.startswith("rot") or j[0] == "v" else "act") for j in jobs])
            rot_sin = [lora[NOPE:QK, 512:1024], lora[NOPE:QK, 1024:1536]]
            raw_cos = [lora[NOPE:QK, 1536:2048], lora[NOPE:QK, 2048:2560]]
            with nc.Block() as block:
                @block.sync
                def _(sp):
                    wukv = a["ml_wukv"][0].rearrange("(k p) n -> p k n", p=P)
                    ring.load(sp, rows_slot(3), wukv[:, :, DM:2 * DM], pe_s(f"q{Q_HEADS[0] - 1}"))
                    wv = a["ml_wo"][0].rearrange("(k p) n -> p k n", p=P)
                    last = [f"q{Q_HEADS[0] + Q_HEADS[1] - 1}", f"q{HEADS - 1}", "v6", "v7"]
                    for s in range(SLOTS):
                        ring.load(sp, cols_slot(s), wv[:, :, s * 256:(s + 1) * 256], pe_s(last[s]))

                def rotated(pe, name, rows):
                    if banks.free(f"rot {name}"):
                        pe.wait_ge(*banks.free(f"rot {name}"))
                    pe.matmul(banks.bank(f"rot {name}")[NOPE:QK], turn_m, rows,
                              start=True, stop=True).then_inc(*pe_s.mark(f"rot {name}"))

                @block.tensor
                def _(pe):
                    rotated(pe, "k", kr)
                    hd = 0
                    for j, nh in enumerate(Q_HEADS):
                        slot_landed(pe, j)
                        w = uq_slot(3 + j, nh * QK)
                        for n in range(nh):
                            if banks.free(f"q{hd}"):
                                pe.wait_ge(*banks.free(f"q{hd}"))
                            for k in range(CQ):
                                mm = pe.matmul(banks.bank(f"q{hd}")[0:QK], w[:, k, n * QK:(n + 1) * QK], cbuf[:, k, :],
                                               start=(k == 0), stop=(k == CQ - 1))
                            mm.then_inc(*pe_s.mark(f"q{hd}"))
                            if hd:
                                pe.wait_ge(*act_s(f"ev q{hd - 1}"))
                                rotated(pe, f"q{hd - 1}", q_t[NOPE:QK, hd - 1, :])
                            hd += 1
                    pe.wait_ge(*act_s(f"ev q{HEADS - 1}"))
                    rotated(pe, f"q{HEADS - 1}", q_t[NOPE:QK, HEADS - 1, :])
                    for hd in range(HEADS):
                        if hd % 8 == 0:
                            slot_landed(pe, 3 + hd // 8)
                        w = rows_slot(2 + hd // 8)
                        pe.wait_ge(*banks.free(f"k{hd}"))
                        for k in range(CKV):
                            c = (hd % 8) * (NOPE + VDIM)
                            mm = pe.matmul(banks.bank(f"k{hd}")[0:NOPE], w[:, k, c:c + NOPE], cbuf[:, CQ + k, :],
                                           start=(k == 0), stop=(k == CKV - 1))
                        mm.then_inc(*pe_s.mark(f"k{hd}"))
                    for j in range(8):
                        tok, half = j // 2, j % 2
                        pe.wait_ge(*banks.free(f"v{j}"))
                        for k in range(CKV):
                            w = rows_slot(2 + half)[:, k, :].rearrange("p (h d) -> p h d", d=NOPE + VDIM)[:, :, NOPE:]
                            mm = pe.matmul(banks.bank(f"v{j}"), cbuf[:, CQ + k, tok * P:(tok + 1) * P], w,
                                           start=(k == 0), stop=(k == CKV - 1))
                        mm.then_inc(*pe_s.mark(f"v{j}"))
                ring.uses += 5

                @block.scalar
                def _(act):
                    for hd in range(HEADS):
                        act.wait_ge(*pe_s(f"q{hd}"))
                        act.activation(q_t[0:QK, hd, :], banks.bank(f"q{hd}")[0:QK], ACT.Copy).then_inc(*act_s.mark(f"ev q{hd}"))
                    for hd in range(HEADS):
                        act.wait_ge(*pe_s(f"k{hd}"))
                        act.activation(k_t[0:NOPE, hd, :], banks.bank(f"k{hd}")[0:NOPE],
                                       ACT.Copy).then_inc(*act_s.mark(f"ev k{hd}"))

                @block.gpsimd
                def _(pool):
                    pool.tensor_tensor(raw_cos[1], kr, cos_t, ALU.mult).then_inc(*pool_s.mark("cos k"))
                    for hd in range(HEADS):
                        if hd:
                            pool.wait_ge(*dve_s("roped k" if hd == 1 else f"roped q{hd - 2}"))
                        pool.wait_ge(*act_s(f"ev q{hd}"))
                        pool.tensor_tensor(raw_cos[hd % 2], q_t[NOPE:QK, hd, :], cos_t,
                                           ALU.mult).then_inc(*pool_s.mark(f"cos q{hd}"))
                    pool.wait_ge(*dve_s("roped k"))
                    pool.tensor_copy(k_t[NOPE:QK, :, :], kr.unsqueeze(1).broadcast_to([ROPE, HEADS, SEQ])
                                     ).then_inc(*pool_s.mark("rotary key"))

                @block.vector
                def _(dve):
                    def rope(name, dst, b):
                        dve.wait_ge(*pe_s(f"rot {name}"))
                        dve.tensor_tensor(rot_sin[b], banks.bank(f"rot {name}")[NOPE:QK], sin_t,
                                          ALU.mult).then_inc(*dve_s.mark(f"ev rot {name}"))
                        dve.wait_ge(*dve_s(f"ev rot {name}"))
                        dve.wait_ge(*pool_s(f"cos {name}"))
                        dve.tensor_tensor(dst, raw_cos[b], rot_sin[b], ALU.add).then_inc(*dve_s.mark(f"roped {name}"))

                    rope("k", kr, 1)
                    for hd in range(HEADS):
                        rope(f"q{hd}", q_t[NOPE:QK, hd, :], hd % 2)
                    for j in range(8):
                        dve.wait_ge(*pe_s(f"v{j}"))
                        dve.tensor_copy(v_tok[:, j // 2, (j % 2) * 512:(j % 2 + 1) * 512],
                                        banks.bank(f"v{j}")).then_inc(*dve_s.mark(f"ev v{j}"))

        def mla_attend(layer):
            stage("attend")
            scale = 1.0 / float(np.sqrt(QK))
            NQ = SEQ // P
            groups = [[2, 0], [1], [3]]
            order = [2, 0, 1, 3]
            start_col = {2: 0, 0: 3 * P, 1: 0, 3: 0}
            G, Q = len(groups), NQ
            blocks = [(kt, qi) for kt in (0, 1, 3, 2) for qi in range(kt, NQ)]
            turned = [lora[:, 256 + 1280 * j:1536 + 1280 * j].rearrange("p (b q) -> p b q", q=P) for j in range(2)]
            q_now = [lora[0:QK, 2816 + 512 * j:3328 + 512 * j] for j in range(2)]
            v_now = [lora[:, 3840 + 256 * j:4096 + 256 * j].rearrange("p (t d) -> p t d", d=VDIM) for j in range(2)]
            top, ntop, total, inv = (small[:, 8 * j:8 * j + 8] for j in range(4))
            scores_made, parts_turned, outputs_made = sem("scores_made"), sem("parts_turned"), sem("outputs_made")
            masked, maxed, tops_made, inverted = sem("masked"), sem("maxed"), sem("tops_made"), sem("inverted")
            probs_made, exps_made = sem("probs_made"), sem("exps_made")
            middle_out, ends_out, output_out = sem("turned_middle_out"), sem("turned_ends_out"), sem("output_out")
            q_here, v_here = sem("q_here"), sem("v_here")

            class Head:

                def __init__(self, i, off):
                    self.i, self.off, self.c = i, off, off % 2

                def __add__(self, n):
                    return Head(self.i, self.off + n)

                def index(self):
                    return self.off if self.i is None else self.i * 2 + self.off

                def tile(self):
                    return self.off // 2 if self.i is None else self.i + self.off // 2

                def count(self, per, more=0):
                    return self.off * per + more if self.i is None else self.i * (2 * per) + (self.off * per + more)

                def after(self, n):
                    return self.i is not None or self.off >= n

            def block(x, qi):
                j = [qi in g for g in groups].index(True)
                return psum[:, 3 * x.c + j, start_col[qi]:start_col[qi] + (qi + 1) * P]

            def run(eng, step):
                step(None, 0, True)
                for off in (0, 1):
                    step(None, off)
                with eng.Fori(0, HEADS // 2 - 2) as i:
                    for off in (2, 3):
                        step(i, off)
                for off in (HEADS - 2, HEADS - 1, HEADS):
                    step(None, off)

            with nc.Block() as nc_block:
                @nc_block.gpsimd
                def _(pool):
                    def query(x):
                        if x.after(2):
                            pool.wait_ge(scores_made, (x + -1).count(G))
                            pool.sem_inc(passed_pool, 1)
                        pool.tensor_copy(q_now[x.c], q_t[0:QK, x.index(), :]).then_inc(q_here, 1)

                    def step(i, off, before=False):
                        x = Head(i, off)
                        if before:
                            query(x)
                            query(x + 1)
                        elif i is not None or off < HEADS:
                            if i is not None or off < HEADS - 2:
                                query(x + 2)
                            if x.after(2):
                                pool.wait_ge(outputs_made, (x + -1).count(1))
                                pool.sem_inc(passed_pool, 1)
                            at = x.index() * VDIM
                            pool.tensor_copy(v_now[x.c], v_tok[:, :, bass.ds(at, VDIM)]).then_inc(v_here, 1)

                    run(pool, step)

                @nc_block.tensor
                def _(pe):
                    def scores(x):
                        pe.wait_ge(q_here, x.count(1, 1))
                        if x.after(2):
                            pe.wait_ge(ends_out, (x + -1).count(2))
                            pe.wait_ge(middle_out, (x + -1).count(1))
                        for group in groups:
                            for qi in group:
                                mm = pe.matmul(block(x, qi), q_now[x.c][:, qi * P:(qi + 1) * P],
                                               k_t[0:QK, x.index(), 0:(qi + 1) * P], start=True, stop=True)
                            mm.then_inc(scores_made, 1)

                    def turn(x):
                        pe.wait_ge(probs_made, x.count(Q, Q))
                        for j, (kt, qi) in enumerate(blocks):
                            mm = pe.transpose(psum[:, 3 * x.c + j // 4, (j % 4) * P:(j % 4 + 1) * P],
                                              probs[:, 4 * x.c + qi, kt * P:(kt + 1) * P], const("ident"))
                            if j in (3, 7, 9):
                                mm.then_inc(parts_turned, 1)

                    def output(x):
                        pe.wait_ge(v_here, x.count(1, 1))
                        pe.wait_ge(ends_out, x.count(2, 2))
                        pe.wait_ge(middle_out, x.count(1, 1))
                        if x.after(2):
                            pe.wait_ge(output_out, (x + -1).count(1))
                        for kt in range(NQ):
                            at = blocks.index((kt, kt))
                            mm = pe.matmul(psum[x.c * VDIM:(x.c + 1) * VDIM, 6 + x.c, kt * P:SEQ], v_now[x.c][:, kt, :],
                                           turned[x.c][:, at:at + NQ - kt, :], start=(kt == 0), stop=(kt == NQ - 1))
                        mm.then_inc(outputs_made, 1)

                    def step(i, off, before=False):
                        x = Head(i, off)
                        if before:
                            scores(x)
                            return
                        if i is not None or off < HEADS - 1:
                            scores(x + 1)
                        if i is not None or off < HEADS:
                            turn(x)
                        if x.after(1):
                            output(x + -1)

                    run(pe, step)

                @nc_block.vector
                def _(dve):
                    def maxima(x):
                        pos = 0
                        for g, group in enumerate(groups):
                            dve.wait_ge(scores_made, x.count(G, g + 1))
                            for qi in group:
                                diag = block(x, qi)[:, qi * P:(qi + 1) * P]
                                dve.tensor_tensor(diag, diag, causal, ALU.add).then_inc(masked, 1)
                            for n, qi in enumerate(group):
                                j = 4 * x.c + pos + n
                                dve.wait_ge(masked, x.count(Q, pos + n + 1))
                                dve.reduce_max(top[:, j:j + 1], block(x, qi), AX_X).then_inc(maxed, 1)
                            j, pos = 4 * x.c + pos, pos + len(group)
                            dve.wait_ge(maxed, x.count(Q, pos))
                            dve.tensor_scalar(ntop[:, j:j + len(group)], top[:, j:j + len(group)], -scale, None,
                                              ALU.mult).then_inc(tops_made, 1)

                    def probabilities(x):
                        pos = 0
                        for g, group in enumerate(groups):
                            j, n = 4 * x.c + pos, len(group)
                            dve.wait_ge(exps_made, x.count(G, g + 1))
                            dve.reciprocal(inv[:, j:j + n], total[:, j:j + n]).then_inc(inverted, 1)
                            dve.wait_ge(inverted, x.count(G, g + 1))
                            for m, qi in enumerate(group):
                                row = probs[:, 4 * x.c + qi, 0:(qi + 1) * P]
                                dve.tensor_scalar(row, row, inv[:, j + m:j + m + 1], None,
                                                  ALU.mult).then_inc(probs_made, 1)
                            pos += n

                    def step(i, off, before=False):
                        x = Head(i, off)
                        if before:
                            maxima(x)
                            probabilities(x)
                            return
                        if i is not None or off < HEADS - 1:
                            maxima(x + 1)
                        if i is not None or off < HEADS:
                            dve.wait_ge(parts_turned, x.count(3, 2))
                            if x.after(2):
                                dve.wait_ge(outputs_made, (x + -1).count(1))
                            dve.tensor_copy(turned[x.c][:, 4:8, :], psum[:, 3 * x.c + 1, :].rearrange(
                                "p (b q) -> p b q", q=P)).then_inc(middle_out, 1)
                        if i is not None or off < HEADS - 1:
                            probabilities(x + 1)

                    run(dve, step)

                @nc_block.scalar
                def _(act):
                    def exps(x):
                        pos = 0
                        if x.after(2):
                            act.wait_ge(parts_turned, (x + -1).count(3))
                        for g, group in enumerate(groups):
                            act.wait_ge(tops_made, x.count(G, g + 1))
                            for m, qi in enumerate(group):
                                j = 4 * x.c + pos + m
                                op = act.activation(probs[:, 4 * x.c + qi, 0:(qi + 1) * P], block(x, qi), ACT.Exp,
                                                    bias=ntop[:, j:j + 1], scale=scale, accum_out=total[:, j:j + 1])
                            op.then_inc(exps_made, 1)
                            pos += len(group)

                    def step(i, off, before=False):
                        x = Head(i, off)
                        if before:
                            exps(x)
                            return
                        if i is not None or off < HEADS - 1:
                            exps(x + 1)
                        if i is not None or off < HEADS:
                            if x.after(2):
                                act.wait_ge(outputs_made, (x + -1).count(1))
                            for part, lo, hi in ((0, 0, 4), (2, 8, 10)):
                                act.wait_ge(parts_turned, x.count(3, part + 1))
                                act.activation(turned[x.c][:, lo:hi, :],
                                               psum[:, 3 * x.c + part, 0:(hi - lo) * P].rearrange("p (b q) -> p b q", q=P),
                                               ACT.Copy).then_inc(ends_out, 1)
                        if x.after(1):
                            y = x + -1
                            rows = slice(y.c * VDIM, (y.c + 1) * VDIM)
                            act.wait_ge(outputs_made, y.count(1, 1))
                            act.activation(o_t[rows, y.tile(), :], psum[rows, 6 + y.c, :], ACT.Copy).then_inc(output_out, 1)

                    run(act, step)

        def mla_finish(layer):
            stage("mlaout")
            banks = Banks([(f"o{t}", "dve") for t in range(NT)])
            with nc.Block() as block:
                @block.sync
                def _(sp):
                    ffn_head(sp, layer, lambda s: split.made(s))

                @block.tensor
                def _(pe):
                    gemm(pe, "o", banks, x_parts, lambda k: dve_s(f"lo{k}"), 0)

                @block.scalar
                def _(act):
                    split.make_hi(act, 0)
                    for t in range(NT):
                        act.activation(x_parts[0][:, t, :], o_t[:, t, :], ACT.Copy).then_inc(*act_s.mark(f"hi{t}"))
                    split.make_hi(act, 1)
                    for g in (2, 3, 4):
                        act.wait_ge(*pe_s(f"o{2 * (g - 2) + 1}"))
                        split.make_hi(act, g)

                @block.vector
                def _(dve):
                    split.make_lo(dve, 0)
                    for t in range(NT):
                        dve.wait_ge(*act_s(f"hi{t}"))
                        dve.tensor_tensor(x_parts[1][:, t, :], o_t[:, t, :], x_parts[0][:, t, :].bitcast(F32),
                                          ALU.subtract).then_inc(*dve_s.mark(f"lo{t}"))
                    split.make_lo(dve, 1)
                    for t in range(NT):
                        if t in (0, 2, 4):
                            split.make_lo(dve, 2 + t // 2)
                        dve.wait_ge(*pe_s(f"o{t}"))
                        dve.tensor_tensor(h[:, t, :], h[:, t, :], banks.bank(f"o{t}"),
                                          ALU.add).then_inc(*dve_s.mark(f"ev o{t}"))
            ring.uses += SLOTS
            split.done += SLOTS

        v_stored = sem("v_first_stored")

        def first_loads(sp):
            load_proj(sp, a["rw_wr"][0], lambda s: None)

        def conv_head(sp, last_use):
            w1 = a["cv_w1"][0].rearrange("(k p) n -> p k n", p=P)
            for s in range(SLOTS):
                c = (s // 2) * 256 + (s % 2) * DM
                ring.load(sp, cols_slot(s), w1[:, :, c:c + 256], last_use(s))

        def mla_head(sp, last_use):
            wd = a["ml_wd"][0].rearrange("(k p) n -> p k n", p=P)
            for s, w in enumerate((256, 256, P + ROPE)):
                ring.load(sp, wd_slot(s, w), wd[:, :, s * 256:s * 256 + w], last_use(s))

        last = lambda layer: ffn_last_use(layer)
        begin()
        rwkv_project(0, 0)
        rwkv_scan(0)
        rwkv_finish(0, 0)
        ffn(0, lambda sp: conv_head(sp, last(0)))
        conv_glu(1)
        conv_taps()
        conv_finish(1)
        ffn(1, lambda sp: mla_head(sp, last(1)))
        mla_down(2)
        mla_up(2)
        mla_attend(2)
        mla_finish(2)
        ffn(2, lambda sp: load_proj(sp, a["rw_wr"][1], last(2)))
        rwkv_project(3, 1)
        rwkv_scan(1)
        rwkv_finish(3, 1)
        ffn(3, lambda sp: None)
        end()
        for n, s in everyone.items():
            new[n] = s.new
    return new


IN_NAMES = ["x", "consts", "extras"] + [n for g in VECTORS for n, _ in g] + [
    "positions", "cv_dw", "cv_w1", "cv_w2", "ml_wd", "ml_wuq", "ml_wukv", "ml_wo",
    "rw_wr", "rw_wk", "rw_wv", "rw_wo", "rw_w1", "rw_w2", "rw_a1", "rw_a2", "rw_g1", "rw_g2", "rw_v1", "rw_v2", "ff_w1", "ff_w2"]

def kernel(**inputs):
    import numpy as _np
    import concourse.bacc as _bacc
    from concourse.bass_utils import run_bass_kernel_spmd as _run

    known = {}
    for _pass in range(2):
        nc = _bacc.Bacc("TRN2", target_bir_lowering=False, num_devices=1, dynamic_dma_scratch_size=1024)
        arrays, args = {}, {}
        consts, extras = constants()
        given = dict(inputs, consts=consts, extras=extras)
        for name in IN_NAMES:
            arr = _np.ascontiguousarray(given[name])
            arrays[f"in_{name}"] = arr
            args[name] = nc.dram_tensor(f"in_{name}", arr.shape, mybir.dt.from_np(arr.dtype), kind="ExternalInput").ap()
        args["out"] = nc.dram_tensor("out_0", (1, SEQ, DM), F32, kind="ExternalOutput").ap()
        args["v_first"] = nc.dram_tensor("v_first", (P, NT * SEQ), F32, kind="Internal").ap()
        known = build(nc, args, known)
    r = _run(nc, [arrays], core_ids=[0])
    return r.results[0]["out_0"]
```
